# Optimizing a Trainium2 kernel written in Bass

```python
import jax, jax.numpy as jnp
from jax import lax
import numpy as np

D_MODEL = 1024
BATCH = 1
SEQ = 512
DEPTH = 1
DEC_BATCH = 8
DEC_SEQ = 16
PAST_LEN = 256

CHUNK = 64
D_MIX = D_MODEL
D_CONV = D_MIX // 2
CONV_W = 3
N_HEADS = 8
HEAD_DIM = (D_MIX - D_CONV) // N_HEADS
N_KV_HEADS = 2
GROUP = N_HEADS // N_KV_HEADS
ROT_DIM = HEAD_DIM // 4
ROPE_THETA = 500000.0
N_IDX_HEADS = 8
IDX_DIM = 64
IDX_ROT_DIM = IDX_DIM // 4
TOP_K = 256
Q_BLOCK = 128
D_FF = 2816
EPS = 1e-6

SPLITS = (D_CONV, D_CONV, D_CONV,
          N_HEADS * HEAD_DIM, N_KV_HEADS * HEAD_DIM, N_KV_HEADS * HEAD_DIM,
          N_IDX_HEADS * IDX_DIM, IDX_DIM, N_IDX_HEADS)
D_IN = sum(SPLITS)
SPLIT_POINTS = tuple(int(s) for s in np.cumsum(SPLITS)[:-1])

kernel_name = 'hybrid_conv_dsa_macaron_stream_step'

def rmsnorm(x, g):
    xf = x.astype(jnp.float32)
    y = xf * lax.rsqrt(jnp.mean(xf * xf, axis=-1, keepdims=True) + EPS)
    return (y * g.astype(jnp.float32)).astype(x.dtype)

def swiglu(x, w_gate, w_up, w_down):
    return (jax.nn.silu(x @ w_gate) * (x @ w_up)) @ w_down

def rope_partial(x, pos, rot):
    half = rot // 2
    inv = ROPE_THETA ** (-jnp.arange(half, dtype=jnp.float32) * (2.0 / rot))
    ang = pos.astype(jnp.float32)[:, None] * inv[None, :]
    cos = jnp.cos(ang)[None, :, None, :]
    sin = jnp.sin(ang)[None, :, None, :]
    xr = x[..., :rot].astype(jnp.float32)
    x1, x2 = xr[..., :half], xr[..., half:]
    xr = jnp.concatenate([x1 * cos - x2 * sin, x1 * sin + x2 * cos], axis=-1).astype(x.dtype)
    return jnp.concatenate([xr, x[..., rot:]], axis=-1)

def dsa_attention(q, q_idx, w_idx, k, v, k_idx, q_pos, n_sel):
    B, T = q.shape[0], q.shape[1]
    S = k.shape[1]
    qb = Q_BLOCK if T % Q_BLOCK == 0 else T
    nb = T // qb
    key_pos = jnp.arange(S)

    def blocks(a):
        return jnp.moveaxis(a.reshape((B, nb, qb) + a.shape[2:]), 1, 0)

    def one_block(args):
        qq, qi, wi, pp = args
        limit = (pp // CHUNK + 1) * CHUNK
        adm = key_pos[None, :] < limit[:, None]
        dots = jnp.einsum('bthd,bsd->bths', qi.astype(jnp.float32), k_idx.astype(jnp.float32)) * (IDX_DIM ** -0.5)
        score = jnp.einsum('bths,bth->bts', jax.nn.relu(dots), wi.astype(jnp.float32))
        score = jnp.where(adm[None], score, -jnp.inf)
        _, sel = lax.top_k(score, n_sel)
        valid = sel < limit[None, :, None]
        k_sel = jax.vmap(lambda kb, ib: kb[ib])(k, sel)
        v_sel = jax.vmap(lambda vb, ib: vb[ib])(v, sel)
        qg = qq.reshape(B, qb, N_KV_HEADS, GROUP, HEAD_DIM)
        logits = jnp.einsum('btkgd,btnkd->btkgn', qg, k_sel).astype(jnp.float32) * (HEAD_DIM ** -0.5)
        logits = jnp.where(valid[:, :, None, None, :], logits, -jnp.inf)
        p = jax.nn.softmax(logits, axis=-1).astype(v.dtype)
        o = jnp.einsum('btkgn,btnkd->btkgd', p, v_sel)
        return o.reshape(B, qb, N_HEADS * HEAD_DIM)

    out = lax.map(one_block, (blocks(q), blocks(q_idx), blocks(w_idx), q_pos.reshape(nb, qb)))
    return jnp.moveaxis(out, 0, 1).reshape(B, T, N_HEADS * HEAD_DIM)

def trunk_layer(x, pos, k_past, v_past, idxk_past, conv_prev,
                ffn1_norm, ffn1_w_gate, ffn1_w_up, ffn1_w_down,
                mix_norm, w_in, conv_w, q_norm, k_norm, idx_k_norm, w_out,
                ffn2_norm, ffn2_w_gate, ffn2_w_up, ffn2_w_down):
    B, T, _ = x.shape
    x = x + 0.5 * swiglu(rmsnorm(x, ffn1_norm), ffn1_w_gate, ffn1_w_up, ffn1_w_down)
    h = rmsnorm(x, mix_norm)
    z = h @ w_in
    gb, gc, xv, q, k, v, qi, ki, wi = jnp.split(z, SPLIT_POINTS, axis=-1)
    u = gc * xv
    up = jnp.concatenate([conv_prev.astype(u.dtype), u], axis=1)
    conv = sum(up[:, j:j + T] * conv_w[j] for j in range(CONV_W))
    conv_out = gb * conv
    conv_state = up[:, up.shape[1] - (CONV_W - 1):]
    q = rope_partial(rmsnorm(q.reshape(B, T, N_HEADS, HEAD_DIM), q_norm), pos, ROT_DIM)
    k = rope_partial(rmsnorm(k.reshape(B, T, N_KV_HEADS, HEAD_DIM), k_norm), pos, ROT_DIM)
    v = v.reshape(B, T, N_KV_HEADS, HEAD_DIM)
    qi = rope_partial(qi.reshape(B, T, N_IDX_HEADS, IDX_DIM), pos, IDX_ROT_DIM)
    ki = rope_partial(rmsnorm(ki, idx_k_norm)[:, :, None, :], pos, IDX_ROT_DIM)[:, :, 0]
    wi = wi * (N_IDX_HEADS ** -0.5)
    k_all = jnp.concatenate([k_past.astype(k.dtype), k], axis=1)
    v_all = jnp.concatenate([v_past.astype(v.dtype), v], axis=1)
    ki_all = jnp.concatenate([idxk_past.astype(ki.dtype), ki], axis=1)
    L = k_all.shape[1]
    n_sel = max(1, min(TOP_K, L // 4))
    attn = dsa_attention(q, qi, wi, k_all, v_all, ki_all, pos, n_sel)
    x = x + jnp.concatenate([conv_out, attn], axis=-1) @ w_out
    x = x + 0.5 * swiglu(rmsnorm(x, ffn2_norm), ffn2_w_gate, ffn2_w_up, ffn2_w_down)
    return x, k, v, ki, conv_state

def setup_inputs(seed: int = 0) -> dict:
    key = jax.random.key(seed)
    ks = jax.random.split(key, 24)
    f32 = jnp.float32
    nrm = lambda k, shape, s: jax.random.normal(k, shape, f32) * s
    gain = lambda k, n: 1.0 + nrm(k, (DEPTH, n), 0.02)
    return {
        'x_prompt': nrm(ks[0], (BATCH, SEQ, D_MODEL), 1.0),
        'x_sample': nrm(ks[1], (DEC_BATCH, DEC_SEQ, D_MODEL), 1.0),
        'cache_k': nrm(ks[2], (DEPTH, DEC_BATCH, PAST_LEN, N_KV_HEADS, HEAD_DIM), 1.0),
        'cache_v': nrm(ks[3], (DEPTH, DEC_BATCH, PAST_LEN, N_KV_HEADS, HEAD_DIM), 1.0),
        'cache_idx_k': nrm(ks[4], (DEPTH, DEC_BATCH, PAST_LEN, IDX_DIM), 1.0),
        'state_conv': nrm(ks[5], (DEPTH, DEC_BATCH, CONV_W - 1, D_CONV), 0.5),
        'ffn1_norm': gain(ks[6], D_MODEL),
        'ffn1_w_gate': nrm(ks[7], (DEPTH, D_MODEL, D_FF), D_MODEL ** -0.5),
        'ffn1_w_up': nrm(ks[8], (DEPTH, D_MODEL, D_FF), D_MODEL ** -0.5),
        'ffn1_w_down': nrm(ks[9], (DEPTH, D_FF, D_MODEL), D_FF ** -0.5),
        'mix_norm': gain(ks[10], D_MODEL),
        'w_in': nrm(ks[11], (DEPTH, D_MODEL, D_IN), D_MODEL ** -0.5),
        'conv_w': nrm(ks[12], (DEPTH, CONV_W, D_CONV), CONV_W ** -0.5),
        'q_norm': gain(ks[13], HEAD_DIM),
        'k_norm': gain(ks[14], HEAD_DIM),
        'idx_k_norm': gain(ks[15], IDX_DIM),
        'w_out': nrm(ks[16], (DEPTH, D_MIX, D_MODEL), D_MIX ** -0.5),
        'ffn2_norm': gain(ks[17], D_MODEL),
        'ffn2_w_gate': nrm(ks[18], (DEPTH, D_MODEL, D_FF), D_MODEL ** -0.5),
        'ffn2_w_up': nrm(ks[19], (DEPTH, D_MODEL, D_FF), D_MODEL ** -0.5),
        'ffn2_w_down': nrm(ks[20], (DEPTH, D_FF, D_MODEL), D_FF ** -0.5),
    }

def reference(x_prompt, x_sample, cache_k, cache_v, cache_idx_k, state_conv,
              ffn1_norm, ffn1_w_gate, ffn1_w_up, ffn1_w_down,
              mix_norm, w_in, conv_w, q_norm, k_norm, idx_k_norm, w_out,
              ffn2_norm, ffn2_w_gate, ffn2_w_up, ffn2_w_down):
    Bp, Tp = x_prompt.shape[0], x_prompt.shape[1]
    Bs, Ts = x_sample.shape[0], x_sample.shape[1]
    past = cache_k.shape[2]
    pos_p = jnp.arange(Tp)
    pos_s = past + jnp.arange(Ts)
    dt = x_prompt.dtype
    empty_kv = jnp.zeros((Bp, 0, N_KV_HEADS, HEAD_DIM), dt)
    empty_ik = jnp.zeros((Bp, 0, IDX_DIM), dt)
    zero_conv = jnp.zeros((Bp, CONV_W - 1, D_CONV), dt)
    hp, hs = x_prompt, x_sample
    kp_l, vp_l, ip_l, cp_l, ks_l, vs_l, is_l, cs_l = [], [], [], [], [], [], [], []
    for l in range(DEPTH):
        w = (ffn1_norm[l], ffn1_w_gate[l], ffn1_w_up[l], ffn1_w_down[l],
             mix_norm[l], w_in[l], conv_w[l], q_norm[l], k_norm[l], idx_k_norm[l], w_out[l],
             ffn2_norm[l], ffn2_w_gate[l], ffn2_w_up[l], ffn2_w_down[l])
        hp, kp, vp, ip, cp = trunk_layer(hp, pos_p, empty_kv, empty_kv, empty_ik, zero_conv, *w)
        hs, ks_, vs, is_, cs = trunk_layer(hs, pos_s, cache_k[l], cache_v[l], cache_idx_k[l], state_conv[l], *w)
        kp_l.append(kp); vp_l.append(vp); ip_l.append(ip); cp_l.append(cp)
        ks_l.append(ks_); vs_l.append(vs); is_l.append(is_); cs_l.append(cs)
    k_prompt = jnp.stack(kp_l); v_prompt = jnp.stack(vp_l)
    idx_k_prompt = jnp.stack(ip_l); conv_prompt = jnp.stack(cp_l)
    k_sample = jnp.stack(ks_l); v_sample = jnp.stack(vs_l)
    idx_k_sample = jnp.stack(is_l); conv_sample = jnp.stack(cs_l)
    return (hp, hs, k_prompt, v_prompt, idx_k_prompt, conv_prompt, k_sample, v_sample, idx_k_sample, conv_sample)


_drawn_inputs = setup_inputs


def setup_inputs(seed=0):
    import zlib

    import numpy as np

    out = dict(_drawn_inputs(seed))
    spreads = {}
    factors = {'ffn1_norm': 3.549,
     'q_norm': 25.371,
     'k_norm': 8.607,
     'idx_k_norm': 3.037,
     'ffn2_norm': 8.0}
    for name, (base, spread) in spreads.items():
        noise = np.random.default_rng([zlib.crc32(name.encode()), seed]).standard_normal(out[name].shape)
        drawn = base * np.exp(spread * noise) if base else spread * noise
        out[name] = __import__('jax').numpy.asarray(drawn.astype(out[name].dtype))
    for name, factor in factors.items():
        out[name] = (out[name] * factor).astype(out[name].dtype)
    return out
```

```python
from contextlib import ExitStack

import numpy as np

import concourse.bass as bass
from concourse import mybir

F32 = mybir.dt.float32
F32R = mybir.dt.float32r
BF16 = mybir.dt.bfloat16
ALU = mybir.AluOpType
ACT = mybir.ActivationFunctionType
AX = mybir.AxisListType

P = 128
D = 1024
C = D // P
F = 2816
NF = F // P
SEQ, NB, NT, PAST = 512, 8, 16, 256
TOK = SEQ + NB * NT
TT = TOK // P
HALF = TOK // 2
HD = 64
NG = 4
ROT = 8
KP = 128
KD = 68
PAD = 4
EPS = 1e-6
SD = PAST + P
TAKEN = -3.4e38
NEVER = -3.0e38
OFF = -1.0e30
GU, DN = NF, NF
UF = GU + DN
U_TOK, U_CONV, U_OUT, U_FFN2 = UF, UF + 6, UF + 12, UF + 16
TOK_N = (256, 72, 256, 256, 256, 256)
NJ = 5 * 6
NPROJ, NOUT = 12, 8


def trunk(nc, xt, gu1, dn1, gu2, dn2, wtok, wkiwi, wconv, wout, small, gains, kcache, vcache, ikcache,
          conv_past, tables, bf_tables, y_out, k_out, v_out, ik_out, conv_out):
    with ExitStack() as ctx:
        def sb(name, shape, dt=F32):
            return ctx.enter_context(nc.sbuf_tensor(name, shape, dt))

        def sem(name):
            return ctx.enter_context(nc.semaphore(name))

        ps = ctx.enter_context(nc.psum_tensor("ps", [P, 8, 512], F32))
        x = sb("x", [P, C, TOK])
        xh = sb("xh", [P, C, TOK], F32R)
        xl = sb("xl", [P, C, TOK], F32R)
        raw = sb("raw", [P, 2, 2048])
        wh = sb("wh", [P, 2, 2048], F32R)
        wl = sb("wl", [P, 2, 2048], F32R)
        rbc = sb("rbc", [P, TOK])
        sqacc = sb("sqacc", [P, TOK])
        sq = sb("sq", [P, TOK])
        ones = sb("ones", [P, P])
        half_pow = sb("half_pow", [P, 40])
        var = sb("var", [P, TT])
        rstd = sb("rstd", [P, TT])
        sm = sb("sm", [P, 36])
        gn = sb("gn", [P, 3, HD])
        tab = sb("tab", [P, 128 + 40 + 40 + 16 + 240 + 8 + 128])
        bft = sb("bft", [P, 9, P], BF16)
        cpast = sb("cpast", [P, 4, NB, 2])
        cstate = sb("cstate", [P, 4, NB + 1, 2])
        ident = tab[:, 0:128]
        cos_t = tab[:, 128:168].rearrange("p (t r) -> p t r", t=TT)
        sin_t = tab[:, 168:208].rearrange("p (t r) -> p t r", t=TT)
        same_t = tab[:, 208:224]
        spread = tab[:, 224:464]
        same_b = tab[:, 464:472]
        other_b = tab[:, 472:600]
        ident_bf = bft[:, 8, :]
        gain = lambda s, c: sm[:, 8 * s + c:8 * s + c + 1]
        conv_w = lambda i, j: sm[:, 24 + 3 * i + j:25 + 3 * i + j]

        with ExitStack() as ffn_scope:
            fs = lambda name, shape, dt=F32: ffn_scope.enter_context(nc.sbuf_tensor(name, shape, dt))
            hid = fs("hid", [P, NF * TOK])
            glu_g = fs("glu_g", [P, TOK])
            glu_t = fs("glu_t", [P, TOK])
            glu_u = fs("glu_u", [P, TOK])
            hh = fs("hh", [P, 2, 2 * TOK], F32R)
            hl = fs("hl", [P, 2, 2 * TOK], F32R)
        zq = sb("zq", [P, TT, 512])
        zkv = sb("zkv", [P, TT, 256])
        zki = sb("zki", [P, TT, P])
        zwi = sb("zwi", [P, TT, 8])
        qit_k = sb("qit_k", [P, 4 * TOK])
        q_all = sb("q_all", [P, NG * TOK])
        kt = sb("kt", [P, TOK])
        kit = sb("kit", [P, TOK])
        ikc_v = sb("ikc_v", [P, 2048])
        score = sb("score", [P, 256 + 384 + 512 + SD + PAD])
        mask = sb("mask", [P, 128 + 256 + 384 + 512 + SD], BF16)
        rp = sb("rp", [P, 2, 512])
        conv_g = sb("conv_g", [P, TOK])
        conv_v = sb("conv_v", [P, TOK])
        conv_b = sb("conv_b", [P, TOK])
        conv_u = sb("conv_u", [P, 2 + SEQ + NB * (NT + 2)])
        conv_o = sb("conv_o", [P, 4, TOK])
        stat = sb("stat", [P, 3 * 40])
        head_ss = sb("head_ss", [P, 40])
        head_rs = sb("head_rs", [P, 40])
        wcols = sb("wcols", [P, NB])
        wfold = sb("wfold", [P, P])
        top8 = sb("top8", [P, 8])

        qit = qit_k[:, 0:4 * SEQ].rearrange("p (j t) -> p j t", j=4)
        qit_s = qit_k[:, 4 * SEQ:].rearrange("p (b j t) -> p j b t", b=NB, j=4)
        qt = q_all[:, 0:4 * SEQ].rearrange("p (j t) -> p j t", j=4)
        qt_s = q_all[:, 4 * SEQ:].rearrange("p (b j t) -> p j b t", b=NB, j=4)
        kct = qit_k[:, 0:2048].rearrange("p (b s) -> p b s", b=NB)
        ikct = ikc_v[:, :].rearrange("p (b s) -> p b s", b=NB)
        vc = ikc_v[:, :].rearrange("p (b k d) -> p b k d", b=NB, k=2)
        wt = zq[:, :, :].rearrange("p t n -> p (t n)")[:, 0:1024].rearrange("p (s n) -> p s n", s=2)
        rot = [(sqacc if n < 2 else sq)[:, 320 * (n % 2):320 * (n % 2) + 320] for n in range(4)]
        score_at = {1: 0, 2: 256, 3: 640, 4: 1152}
        width = {0: 128, 1: 256, 2: 384, 3: 512, 4: SD}
        scores = {t: score[:, a:a + width[t] + (PAD if t == 4 else 0)] for t, a in score_at.items()}
        mask_at = {0: 0, 1: 128, 2: 384, 3: 768, 4: 1280}
        masks = {t: mask[:, a:a + width[t]] for t, a in mask_at.items()}

        x_in = [sem(f"x_in{i}") for i in range(4)]
        consts_in = sem("consts_in")
        ones_set = sem("ones_set")
        raw_in = [sem("raw_in0"), sem("raw_in1")]
        hi_ready = sem("hi_ready")
        lo_ready = sem("lo_ready")
        unit_done = sem("unit_done")
        xh_ready = sem("xh_ready")
        xl_ready = sem("xl_ready")
        sq_ready = sem("sq_ready")
        sq_added = sem("sq_added")
        colsum_done = sem("colsum_done")
        var_ready = sem("var_ready")
        rstd_ready = sem("rstd_ready")
        diag_ready = sem("diag_ready")
        bcast_done = sem("bcast_done")
        rbc_ready = sem("rbc_ready")
        glu_g_ready = sem("glu_g_ready")
        glu_free = sem("glu_free")
        tanh_ready = sem("tanh_ready")
        glu_m_ready = sem("glu_m_ready")
        hid_ready = sem("hid_ready")
        hh_ready = sem("hh_ready")
        hl_ready = sem("hl_ready")
        res_added = sem("res_added")
        tok_job = sem("tok_job")
        tok_evac = sem("tok_evac")
        proj_job = sem("proj_job")
        proj_evac = sem("proj_evac")
        bank_full = {b: sem(f"bank{b}_full") for b in range(4, 8)}
        bank_free = {b: sem(f"bank{b}_free") for b in range(4, 8)}
        ikc_in = sem("ikc_in")
        kc_in = sem("kc_in")
        vc_in = sem("vc_in")
        dchain = sem("vector_chain")
        pchain = sem("gpsimd_chain")
        ki_ss_ready = sem("ki_ss_ready")
        k_ss_ready = sem("k_ss_ready")
        q_ss_ready = sem("q_ss_ready")
        head_rs_ready = sem("head_rs_ready")
        ki_ready = sem("ki_ready")
        qi_ready = sem("qi_ready")
        k_ready = sem("k_ready")
        q_ready = sem("q_ready")
        wfold_ready = sem("wfold_ready")
        relu_used = sem("relu_used")
        dec_relu_used = sem("dec_relu_used")
        score_fill = sem("score_fill")
        mask0_ready = sem("mask0_ready")
        mask_ready = sem("mask_ready")
        conv_done = sem("conv_done")
        cvh_ready = sem("cvh_ready")
        cvl_ready = sem("cvl_ready")
        max_ready = sem("max_ready")
        p_ready = sem("p_ready")
        pv_done = sem("pv_done")
        att_h_ready = sem("att_h_ready")
        kv_stored = sem("kv_stored")
        y_stored = sem("y_stored")

        bank_use, uses = {}, {b: 0 for b in range(4, 8)}

        def place(job, bank):
            bank_use[job] = (bank, uses[bank])
            uses[bank] += 1

        DOT_TILES = (3, 2)
        ATT_TILES = (3, 4, 2, 1, 0)
        ITEMS = [(t, n) for t in ATT_TILES for n in range(8)]
        for n, job in enumerate(["tki0", "tki1", "tqi0", "tqi1", "tqi2", "tqi3", "tqi4"]):
            place(job, 4 + n % 2)
        place("wcol", 6)
        for n, (t, h) in enumerate([(t, h) for t in DOT_TILES for h in range(8)]):
            place(("dot", t, h), 4 + n % 3)
        for b in range(NB):
            place(("dot", 4, b), 4 + b % 3)
        place("decsum", 7)
        for h in range(8):
            place(("dot", 1, h), 4 + h % 3)
        for n, job in enumerate(["tk0", "tk1", "tq0", "tq1", "tq2", "tq3", "tq4"]):
            place(job, 4 + n % 2)
        for n, item in enumerate(ITEMS):
            place(("logit", n), 4 + n % 2)
            place(("turn", n), 6)
            if item[1] == 7:
                place(("pv", item[0]), 7)

        def wait_bank_free(eng, job):
            b, k = bank_use[job]
            if k:
                eng.wait_ge(bank_free[b], k)

        def wait_bank_full(eng, job):
            b, k = bank_use[job]
            eng.wait_ge(bank_full[b], k + 1)

        def wait_bank_read(eng, job):
            b, k = bank_use[job]
            eng.wait_ge(bank_free[b], k + 1)

        def bank(job):
            return bank_use[job][0]

        def wait_unit_used(eng, U):
            if U < U_TOK:
                eng.wait_ge(unit_done, U + 1)
            elif U < U_CONV:
                eng.wait_ge(tok_job, 5 * (U - U_TOK) + 5)
            elif U < U_OUT:
                eng.wait_ge(proj_job, 2 * (U - U_CONV) + 2)
            else:
                eng.wait_ge(proj_job, NPROJ + 4 * (U - U_OUT) + 4)

        def pv_bank(t):
            if t == 4:
                return ps[:, 7, :].rearrange("p (b g t) -> p b g t", b=NB, g=NG)
            return ps[:, 7, :].rearrange("p (g t) -> p g t", g=NG)

        def attended(buf, t):
            if t == 4:
                return buf[:, 4:8, SEQ:TOK].rearrange("p g (b t) -> p b g t", b=NB)
            return buf[:, 4:8, t * P:(t + 1) * P]

        unit_n = {U_TOK + i: 8 * n for i, n in enumerate(TOK_N)}

        block = ctx.enter_context(nc.Block())

        @block.sync
        def _(sp):
            def load(U, k, slot, src, n, wait=True):
                if wait:
                    sp.wait_ge(lo_ready, U - 1)
                sp.dma_start(raw[:, slot, 0:n], src).then_inc(raw_in[slot], 16)

            def ffn(gu, dn, base):
                first = 0
                if base == 0:
                    load(0, 0, 0, gu[0], 2048, wait=False)
                    load(1, 0, 1, gu[1], 2048, wait=False)
                    first = 1
                with sp.Fori(first, GU // 2) as i:
                    for s in range(2):
                        load(base + 2 * i + s, 0, s, gu[2 * i + s], 2048)
                with sp.Fori(0, DN // 2) as i:
                    for s in range(2):
                        load(base + GU + 2 * i + s, 0, s, dn[2 * i + s], 1024)

            ffn(gu1, dn1, 0)
            for n, U in enumerate(range(U_TOK, U_CONV)):
                src = wkiwi if n == 1 else wtok[(0, None, 1, 2, 3, 4)[n]]
                load(U, 0, U % 2, src, unit_n[U])
            for n, U in enumerate(range(U_CONV, U_OUT)):
                load(U, 0, U % 2, wconv[n], 2048)
            for n, U in enumerate(range(U_OUT, U_FFN2)):
                load(U, 0, U % 2, wout[n], 2048)
            sp.wait_ge(k_ready, 1)
            sp.wait_ge(ki_ready, 1)
            sp.wait_ge(conv_done, 4)
            sp.wait_ge(tok_evac, NJ)
            sp.dma_start(k_out, zkv[:, :, 0:128]).then_inc(kv_stored, 16)
            sp.dma_start(v_out, zkv[:, :, 128:256]).then_inc(kv_stored, 16)
            sp.dma_start(ik_out, zki[:, :, 0:HD]).then_inc(kv_stored, 16)
            sp.dma_start(conv_out, cstate[:, :, :, :]).then_inc(kv_stored, 16)
            ffn(gu2, dn2, U_FFN2)
            for c in range(C):
                sp.wait_ge(res_added, C + c + 1)
                sp.dma_start(y_out[:, c, :], x[:, c, :]).then_inc(y_stored, 16)
            sp.wait_ge(kv_stored, 64)
            sp.wait_ge(y_stored, 16 * C)

        @block.tensor
        def _(pe):
            def three(out, ah, al, bh, bl, first, last):
                pe.matmul(out, ah, bh, start=first, stop=False)
                pe.matmul(out, ah, bl, start=False, stop=False)
                return pe.matmul(out, al, bh, start=False, stop=last)

            def token_halves(banks, ah, al, bh, bl, first, last):
                outs = [ps[:, b, 0:HALF] for b in banks]
                cols = [slice(0, HALF), slice(HALF, TOK)]
                for o, c in zip(outs, cols):
                    pe.matmul(o, ah, bh[:, c], start=first, stop=False)
                for o, c in zip(outs, cols):
                    pe.matmul(o, ah, bl[:, c], start=False, stop=False)
                for o, c in zip(outs, cols):
                    last_mm = pe.matmul(o, al, bh[:, c], start=False, stop=last)
                return last_mm

            def column_sums(stage):
                pe.wait_ge(sq_added, C * (stage + 1))
                for t in range(TT):
                    mm = pe.matmul(ps[:, 7, t:t + 1], sqacc[:, t * P:(t + 1) * P], ones[:, 0:1],
                                   start=True, stop=True)
                mm.then_inc(colsum_done, 1)

            def broadcast_rstd(stage):
                pe.wait_ge(diag_ready, stage + 1)
                pe.matmul(ps[:, 6, :], ones[:, :], sq[:, 0:512], start=True, stop=True)
                pe.matmul(ps[:, 7, 0:P], ones[:, :], sq[:, 512:TOK], start=True, stop=True)\
                    .then_inc(bcast_done, 1)

            def weight(w, slot, i):
                return w[:, slot, i * P:(i + 1) * P]

            def glu_part(slot, m, c):
                b = 4 * slot + 2 * m
                return token_halves((b, b + 1), weight(wh, slot, 8 * m + c), weight(wl, slot, 8 * m + c),
                                    xh[:, c, :], xl[:, c, :], c == 0, c == C - 1)

            def glu_unit(slot):
                for m in range(2):
                    for c in range(C):
                        mm = glu_part(slot, m, c)
                mm.then_inc(unit_done, 1)

            def down_unit(slot, first, last):
                for f in range(2):
                    for j in range(4):
                        mm = token_halves((2 * j, 2 * j + 1), weight(wh, slot, 4 * f + j),
                                          weight(wl, slot, 4 * f + j),
                                          hh[:, slot, f * TOK:(f + 1) * TOK],
                                          hl[:, slot, f * TOK:(f + 1) * TOK],
                                          first and f == 0, last and f == 1)
                mm.then_inc(unit_done, 1)

            def ffn(k):
                stage, base = 2 * k, U_FFN2 * k
                pe.wait_ge(lo_ready, base + 1)
                for cs in (range(0, 4), range(4, 8)):
                    for m in range(2):
                        for c in cs:
                            if m == 0:
                                pe.wait_ge(xh_ready, C * stage + c + 1)
                                pe.wait_ge(xl_ready, C * stage + c + 1)
                            mm = glu_part(0, m, c)
                mm.then_inc(unit_done, 1)
                column_sums(stage)
                pe.wait_ge(lo_ready, base + 2)
                for c in range(4):
                    glu_part(1, 0, c)
                broadcast_rstd(stage)
                for c in range(4, C):
                    glu_part(1, 0, c)
                pe.wait_ge(rbc_ready, stage + 1)
                for c in range(C):
                    mm = glu_part(1, 1, c)
                mm.then_inc(unit_done, 1)
                with pe.Fori(1, GU // 2) as i:
                    for s in range(2):
                        pe.wait_ge(lo_ready, base + 2 * i + s + 1)
                        pe.wait_ge(glu_free, GU * k + 2 * i + s - 1)
                        glu_unit(s)

                def down(v, first=False, last=False, slot=0):
                    pe.wait_ge(lo_ready, base + GU + v + 1)
                    pe.wait_ge(hl_ready, DN * k + v + 1)
                    down_unit(slot, first, last)

                pe.wait_ge(glu_free, GU * (k + 1))
                down(0, first=True, slot=0)
                with pe.Fori(0, 4) as i:
                    down(2 * i + 1, slot=1)
                    down(2 * i + 2, slot=0)
                down(9, slot=1)
                down(10, last=True, slot=0)
                pe.wait_ge(res_added, C * k + 4)
                down(11, first=True, slot=1)
                with pe.Fori(0, 4) as i:
                    down(2 * i + 12, slot=0)
                    down(2 * i + 13, slot=1)
                down(20, slot=0)
                down(21, last=True, slot=1)

            def tok_unit_weight(w, U, c):
                n = unit_n[U] // 8
                return w[:, U % 2, c * n:(c + 1) * n]

            def tok_part(U, t, cs):
                J = 5 * (U - U_TOK) + t
                n = unit_n[U] // 8
                for c in cs:
                    mm = three(ps[:, J % 4, 0:n], xh[:, c, t * P:(t + 1) * P], xl[:, c, t * P:(t + 1) * P],
                               tok_unit_weight(wh, U, c), tok_unit_weight(wl, U, c), c == 0, c == C - 1)
                return mm

            def tok_job_of(U, t):
                J = 5 * (U - U_TOK) + t
                if J >= 4:
                    pe.wait_ge(tok_evac, J - 3)
                tok_part(U, t, range(C)).then_inc(tok_job, 1)

            def tok_unit(U):
                pe.wait_ge(lo_ready, U + 1)
                for t in range(TT):
                    tok_job_of(U, t)

            def turn_token_tile(job, pieces):
                wait_bank_free(pe, job)
                for i, piece in enumerate(pieces):
                    mm = pe.transpose(ps[:, bank(job), i * P:(i + 1) * P], piece, ident)
                mm.then_inc(bank_full[bank(job)], 1)

            def dots(t, h):
                job = ("dot", t, h)
                j, r = h // 2, HD * (h % 2)
                wait_bank_free(pe, job)
                pe.matmul(ps[:, bank(job), 0:width[t]], qit[r:r + HD, j, t * P:(t + 1) * P],
                          kit[r:r + HD, 0:width[t]], start=True, stop=True)\
                    .then_inc(bank_full[bank(job)], 1)

            def dots_sample(b):
                job = ("dot", 4, b)
                wait_bank_free(pe, job)
                for r in (0, HD):
                    q = qit_k[r:r + HD, 4 * SEQ + b * HD:4 * SEQ + (b + 1) * HD]
                    pe.matmul(ps[r:r + HD, bank(job), 0:PAST], q, ikct[r:r + HD, b, :], start=True, stop=True)
                    mm = pe.matmul(ps[r:r + HD, bank(job), PAST:SD], q, kit[r:r + HD, SEQ:TOK],
                                   start=True, stop=True)
                mm.then_inc(bank_full[bank(job)], 1)

            def sum_heads(b):
                wait_bank_read(pe, ("dot", 4, b))
                mm = pe.matmul(ps[:, bank("decsum"), 0:SD], spread[:, 112 - NT * b:240 - NT * b],
                               rp[:, b % 2, 0:SD], start=(b == 0), stop=(b == NB - 1))
                mm.then_inc(dec_relu_used, 1)
                if b == NB - 1:
                    pe.matmul(ps[:, bank("decsum"), SD:SD + 1], ident, ones[:, 0:1], start=True, stop=True)\
                        .then_inc(bank_full[bank("decsum")], 1)

            def proj(b):
                U = U_CONV + b // 2 if b < NPROJ else U_OUT + (b - NPROJ) // 4
                pe.wait_ge(lo_ready, U + 1)
                if b < 2:
                    pe.wait_ge(tok_evac, NJ)
                else:
                    pe.wait_ge(proj_evac, b - 1)
                banks = (2 * (b % 2), 2 * (b % 2) + 1)
                if b < NPROJ:
                    for c in range(C):
                        i = 8 * (b % 2) + c
                        mm = token_halves(banks, weight(wh, U % 2, i), weight(wl, U % 2, i), xh[:, c, :],
                                          xl[:, c, :], c == 0, c == C - 1)
                else:
                    first_chunk = 4 * ((b - NPROJ) // NOUT)
                    for c in range(4):
                        i = 4 * c + (b - NPROJ) % 4
                        mm = token_halves(banks, weight(wh, U % 2, i), weight(wl, U % 2, i),
                                          xh[:, first_chunk + c, :], xl[:, first_chunk + c, :],
                                          c == 0, c == 3)
                mm.then_inc(proj_job, 1)

            def logits(n):
                t, m = ITEMS[n]
                job = ("logit", n)
                if t:
                    pe.wait_ge(mask_ready, ATT_TILES.index(t) + 1)
                else:
                    pe.wait_ge(mask0_ready, 1)
                wait_bank_free(pe, job)
                out = ps[:, bank(job), 0:width[t]]
                if t == 4:
                    pe.matmul(out, bft[:, m, :], masks[t], start=True, stop=False)
                    for r in (0, HD):
                        q = q_all[r:r + HD, 4 * SEQ + m * HD:4 * SEQ + (m + 1) * HD]
                        pe.matmul(ps[r:r + HD, bank(job), 0:PAST], q, kct[r:r + HD, m, :],
                                  start=False, stop=False)
                        mm = pe.matmul(ps[r:r + HD, bank(job), PAST:SD], q, kt[r:r + HD, SEQ:TOK],
                                       start=False, stop=True)
                else:
                    g, r = m // 2, HD * (m % 2)
                    pe.matmul(out, ident_bf, masks[t], start=True, stop=False)
                    mm = pe.matmul(out, qt[r:r + HD, g, t * P:(t + 1) * P], kt[r:r + HD, 0:width[t]],
                                   start=False, stop=True)
                mm.then_inc(bank_full[bank(job)], 1)

            def turn_weights(n):
                pe.wait_ge(p_ready, n + 1)
                turn_token_tile(("turn", n), [rp[:, n % 2, k * P:(k + 1) * P]
                                              for k in range(width[ITEMS[n][0]] // P)])

            def weigh_values(n):
                t, m = ITEMS[n]
                if m == 0:
                    wait_bank_free(pe, ("pv", t))
                wait_bank_read(pe, ("turn", n))
                blocks = width[t] // P
                if t == 4:
                    for r in (0, HD):
                        for k in range(blocks):
                            v = vc[:, m, k, r:r + HD] if k < 2 else zkv[:, 4, P + r:P + r + HD]
                            mm = pe.matmul(ps[r:r + HD, 7, m * HD:(m + 1) * HD], v,
                                           wt[:, n % 2, k * P + r:k * P + r + HD],
                                           start=(k == 0), stop=(k == blocks - 1))
                else:
                    g, r = m // 2, HD * (m % 2)
                    for k in range(blocks):
                        mm = pe.matmul(ps[r:r + HD, 7, g * P:(g + 1) * P], zkv[:, k, P + r:P + r + HD],
                                       wt[:, n % 2, k * P:(k + 1) * P],
                                       start=(k == 0), stop=(k == blocks - 1))
                mm.then_inc(pv_done, 1)

            pe.wait_ge(consts_in, 16 * 5)
            pe.wait_ge(ones_set, 3)
            ffn(0)

            pe.wait_ge(lo_ready, U_TOK + 1)
            for cs in (range(0, 4), range(4, 8)):
                for t in range(4):
                    if t == 0:
                        pe.wait_ge(xh_ready, C + cs[-1] + 1)
                        pe.wait_ge(xl_ready, C + cs[-1] + 1)
                    if cs[0] == 0:
                        pe.wait_ge(res_added, 4 + t // 2 + 1)
                    mm = tok_part(U_TOK, t, cs)
                    if cs[0] == 4:
                        mm.then_inc(tok_job, 1)
                    if cs[0] == 4 and t == 2:
                        column_sums(1)
            tok_job_of(U_TOK, 4)
            tok_unit(U_TOK + 1)
            broadcast_rstd(1)
            tok_unit(U_TOK + 2)
            tok_unit(U_TOK + 3)
            pe.wait_ge(rbc_ready, 2)
            pe.wait_ge(ki_ready, 1)
            turn_token_tile("tki0", [zki[:, t, :] for t in range(4)])
            turn_token_tile("tki1", [zki[:, 4, :]])
            pe.wait_ge(wfold_ready, 1)
            wait_bank_free(pe, "wcol")
            pe.matmul(ps[:, 6, 0:NB], wfold[:, :], same_b, start=True, stop=True).then_inc(bank_full[6], 1)
            pe.wait_ge(qi_ready, 1)
            for t in range(TT):
                turn_token_tile(f"tqi{t}", [zq[:, t, j * P:(j + 1) * P] for j in range(4)])
            for job in ("tki0", "tki1", "tqi3", "tqi4"):
                wait_bank_read(pe, job)
            for t in DOT_TILES:
                for h in range(8):
                    dots(t, h)
            tok_unit(U_TOK + 4)
            tok_unit(U_TOK + 5)
            pe.wait_ge(ikc_in, 32)
            dots_sample(0)
            dots_sample(1)
            for b in range(NB):
                if b + 2 < NB:
                    dots_sample(b + 2)
                sum_heads(b)
            for h in range(8):
                dots(1, h)
            proj(0)
            proj(1)
            proj(2)
            pe.wait_ge(k_ready, 1)
            turn_token_tile("tk0", [zkv[:, t, 0:P] for t in range(4)])
            turn_token_tile("tk1", [zkv[:, 4, 0:P]])
            proj(3)
            pe.wait_ge(q_ready, 1)
            for t in range(TT):
                turn_token_tile(f"tq{t}", [zq[:, t, j * P:(j + 1) * P] for j in range(4)])
            for b in range(4, NPROJ):
                proj(b)
            for job in ("tk0", "tk1", "tq3", "tq4"):
                wait_bank_read(pe, job)
            pe.wait_ge(kc_in, 16)
            pe.wait_ge(vc_in, 16)
            logits(0)
            logits(1)
            for n in range(len(ITEMS)):
                turn_weights(n)
                if n + 2 < len(ITEMS):
                    logits(n + 2)
                if n % 5 == 1:
                    if n == 1:
                        pe.wait_ge(cvl_ready, 4)
                    proj(NPROJ + n // 5)
                weigh_values(n)
            wait_bank_read(pe, ("pv", ATT_TILES[-1]))
            for b in range(NPROJ + NOUT, NPROJ + 2 * NOUT):
                proj(b)
            ffn(1)

        @block.scalar
        def _(act):
            def copy(out, in_, scale=1.0):
                return nc.scalar.activation(out, in_, ACT.Copy, scale=scale)

            def split_hi(U, k, slot, n):
                act.wait_ge(raw_in[slot], 16 * (k + 1))
                copy(wh[:, slot, 0:n], raw[:, slot, 0:n]).then_inc(hi_ready, 1)

            def operand_hi(stage, c):
                copy(xh[:, c, :], x[:, c, :], scale=gain(stage, c)).then_inc(xh_ready, 1)

            def square(stage, c):
                if stage and c == 0:
                    act.wait_ge(bcast_done, stage)
                if C * stage + c:
                    act.wait_ge(sq_added, C * stage + c)
                nc.scalar.activation(sq[:, :], x[:, c, :], ACT.Square).then_inc(sq_ready, 1)

            def rstd_out(stage):
                act.wait_ge(bcast_done, stage + 1)
                copy(rbc[:, :], ps[:, 6:8, :].rearrange("p a b -> p (a b)")[:, 0:TOK]).then_inc(rbc_ready, 1)

            def mixer_hi(U):
                wait_unit_used(act, U - 2)
                split_hi(U, U // 2, U % 2, unit_n.get(U, 2048))

            def ffn(k):
                base = U_FFN2 * k
                if k == 0:
                    act.wait_ge(consts_in, 16 * 5)
                for c in range(C):
                    if k == 0:
                        act.wait_ge(x_in[c // 2], 16)
                    else:
                        act.wait_ge(proj_evac, NPROJ + NOUT + c + 1)
                        if c >= 4:
                            act.wait_ge(proj_job, NPROJ + 2 * NOUT)
                    operand_hi(2 * k, c)
                    if k == 0 and c in (0, C - 1):
                        split_hi(c // 7, 0, c // 7, 2048)
                if k:
                    mixer_hi(base + 1)
                for c in range(C):
                    square(2 * k, c)
                rstd_out(2 * k)

                def glu_step(u, half, s, n):
                    act.wait_ge(unit_done, UF * k + u + 1)
                    split_hi(None, base // 2 + half + 1, s, n)
                    act.wait_ge(glu_g_ready, GU * k + u + 1)
                    nc.scalar.activation(glu_t[:, :], glu_g[:, :], ACT.Tanh, scale=0.5).then_inc(tanh_ready, 1)

                def hidden_hi(pair, tile_pair, s):
                    copy(hh[:, s, :], hid[:, bass.ds(tile_pair * 2 * TOK, 2 * TOK)]).then_inc(hh_ready, 1)

                with act.Fori(0, GU // 2 - 1) as i:
                    for s in range(2):
                        glu_step(2 * i + s, i, s, 2048)
                act.wait_ge(hid_ready, GU * k + 2)
                for s in range(2):
                    glu_step(GU - 2 + s, GU // 2 - 1, s, 1024)
                    act.wait_ge(hid_ready, GU * k + 2 * s + 2)
                    hidden_hi(s, s, s)

                def down_step(v, half, s, tile_pair):
                    act.wait_ge(unit_done, UF * k + GU + v + 1)
                    split_hi(None, (base + GU) // 2 + half + 1, s, 1024)
                    hidden_hi(None, tile_pair, s)

                with act.Fori(0, 4) as i:
                    for s in range(2):
                        down_step(2 * i + s, i, s, 2 * i + s + 2)
                act.wait_ge(hid_ready, GU * (k + 1))
                down_step(8, 4, 0, 10)
                down_step(9, 4, 1, 0)
                down_step(10, 5, 0, 1)
                if k == 0:
                    for c in range(4):
                        act.wait_ge(res_added, c + 1)
                        operand_hi(1, c)
                    for c in range(4):
                        square(1, c)
                down_step(11, 5, 1, 2)
                with act.Fori(0, 4) as i:
                    for s in range(2):
                        down_step(2 * i + 12 + s, i + 6, s, 2 * i + s + 3)
                if k == 0:
                    mixer_hi(U_TOK)
                    mixer_hi(U_TOK + 1)

            def tok_out(U, t):
                J = 5 * (U - U_TOK) + t
                act.wait_ge(tok_job, J + 1)
                s, p = rstd[:, t:t + 1], ps[:, J % 4, :]
                i = U - U_TOK
                if i == 1:
                    copy(zki[:, t, 0:HD], p[:, 0:HD], scale=s)
                    copy(zwi[:, t, :], p[:, HD:HD + 8], scale=s).then_inc(tok_evac, 1)
                else:
                    dst = {0: zq[:, t, 0:256], 2: zq[:, t, 256:512], 3: zkv[:, t, :],
                           4: zq[:, t, 0:256], 5: zq[:, t, 256:512]}[i]
                    copy(dst, p[:, 0:256], scale=s).then_inc(tok_evac, 1)

            def turned_out(job, dst, n):
                wait_bank_full(act, job)
                src = ps[:, bank(job), 0:n * P]
                if len(dst.shape) == 3:
                    src = src.rearrange("p (j t) -> p j t", j=n)
                elif len(dst.shape) == 4:
                    src = src.rearrange("p (j b t) -> p j b t", j=n, b=NB)
                copy(dst, src).then_inc(bank_free[bank(job)], 1)

            def relu_out(t, h, n):
                job = ("dot", t, h)
                wait_bank_full(act, job)
                if n >= 2:
                    act.wait_ge(relu_used, n - 1)
                nc.scalar.activation(rp[:, n % 2, 0:width[t]], ps[:, bank(job), 0:width[t]], ACT.Relu)\
                    .then_inc(bank_free[bank(job)], 1)

            def exp_out(n):
                t, m = ITEMS[n]
                act.wait_ge(max_ready, n + 1)
                if n >= 2:
                    wait_bank_full(act, ("turn", n - 2))
                job = ("logit", n)
                nc.scalar.activation(rp[:, n % 2, 0:width[t]], ps[:, bank(job), 0:width[t]], ACT.Exp,
                                     bias=stat[:, n:n + 1], accum_out=stat[:, 40 + n:41 + n])\
                    .then_inc(bank_free[bank(job)], 1)

            def weights_out(n):
                t, m = ITEMS[n]
                job = ("turn", n)
                wait_bank_full(act, job)
                if n >= 2:
                    act.wait_ge(pv_done, n - 1)
                copy(wt[:, n % 2, 0:width[t]], ps[:, 6, 0:width[t]]).then_inc(bank_free[6], 1)

            def attended_hi(i):
                t = ATT_TILES[i]
                act.wait_ge(pv_done, 8 * (i + 1))
                copy(attended(xh, t), pv_bank(t)).then_inc(att_h_ready, 1)

            for i in range(4):
                act.dma_start(x[:, 2 * i:2 * i + 2, :], xt[:, 2 * i:2 * i + 2, :]).then_inc(x_in[i], 16)
                if i == 0:
                    for dst, src in ((sm[:, :], small), (tab[:, :], tables), (gn[:, :, :], gains),
                                     (bft[:, :, :], bf_tables), (cpast[:, :, :, :], conv_past)):
                        act.dma_start(dst, src).then_inc(consts_in, 16)
            ffn(0)

            for c in range(4, C):
                act.wait_ge(res_added, c + 1)
                operand_hi(1, c)
            for c in range(4, C):
                square(1, c)
            act.wait_ge(res_added, 8)
            for r in (0, HD):
                act.dma_start(ikct[r:r + HD, :, :], ikcache).then_inc(ikc_in, 16)
            act.wait_ge(rstd_ready, 2)
            for t in range(TT):
                tok_out(U_TOK, t)
            mixer_hi(U_TOK + 2)
            for t in range(TT):
                tok_out(U_TOK + 1, t)
            mixer_hi(U_TOK + 3)
            rstd_out(1)
            for t in range(TT):
                tok_out(U_TOK + 2, t)
            mixer_hi(U_TOK + 4)
            for t in range(TT):
                tok_out(U_TOK + 3, t)
            mixer_hi(U_TOK + 5)

            turned_out("tki0", kit[:, 0:SEQ], 4)
            turned_out("tki1", kit[:, SEQ:TOK], 1)
            for t in range(TT):
                turned_out(f"tqi{t}", qit[:, :, t * P:(t + 1) * P] if t < 4 else qit_s, 4)
            n = 0
            for t in DOT_TILES:
                for h in range(8):
                    relu_out(t, h, n)
                    n += 1
            for t in range(TT):
                tok_out(U_TOK + 4, t)
            mixer_hi(U_CONV)
            for t in range(TT):
                tok_out(U_TOK + 5, t)
            mixer_hi(U_CONV + 1)
            for h in range(8):
                relu_out(1, h, n)
                n += 1
            act.wait_ge(relu_used, 24)
            act.dma_start(kct, kcache).then_inc(kc_in, 16)
            act.dma_start(vc, vcache).then_inc(vc_in, 16)
            mixer_hi(U_CONV + 2)
            turned_out("tk0", kt[:, 0:SEQ], 4)
            turned_out("tk1", kt[:, SEQ:TOK], 1)
            for t in range(TT):
                turned_out(f"tq{t}", qt[:, :, t * P:(t + 1) * P] if t < 4 else qt_s, 4)
            for U in range(U_CONV + 3, U_OUT + 2):
                mixer_hi(U)
            act.wait_ge(proj_job, NPROJ)
            for i in range(4):
                act.wait_ge(conv_done, i + 1)
                copy(xh[:, i, :], conv_o[:, i, :]).then_inc(cvh_ready, 1)
            exp_out(0)
            exp_out(1)
            for n in range(len(ITEMS)):
                weights_out(n)
                if n + 2 < len(ITEMS):
                    exp_out(n + 2)
                if n % 8 == 7:
                    attended_hi(n // 8)
                if n in (20, 39):
                    mixer_hi(U_OUT + (2 if n == 20 else 3))
            mixer_hi(U_FFN2)
            act.wait_ge(kv_stored, 64)
            ffn(1)

        @block.vector
        def _(dve):
            chained = [0]

            def link(ins):
                chained[0] += 1
                ins.then_inc(dchain, 1)
                dve.wait_ge(dchain, chained[0])

            def split_lo(n_ready, slot, n):
                dve.wait_ge(hi_ready, n_ready)
                dve.tensor_tensor(wl[:, slot, 0:n], raw[:, slot, 0:n], wh[:, slot, 0:n].bitcast(F32),
                                  ALU.subtract).then_inc(lo_ready, 1)

            def mixer_lo(U):
                split_lo(U + 1, U % 2, unit_n.get(U, 2048))

            def operand_lo(stage, c):
                dve.wait_ge(xh_ready, C * stage + c + 1)
                dve.scalar_tensor_tensor(out=xl[:, c, :], in0=x[:, c, :], scalar=gain(stage, c),
                                         in1=xh[:, c, :].bitcast(F32), op0=ALU.mult, op1=ALU.subtract)\
                    .then_inc(xl_ready, 1)

            def mean_squares(stage):
                dve.wait_ge(colsum_done, stage + 1)
                dve.tensor_scalar(var[:, :], ps[:, 7, 0:TT], 1.0 / D, EPS, ALU.mult, ALU.add)\
                    .then_inc(var_ready, 1)

            def diagonals(stage):
                dve.wait_ge(rstd_ready, stage + 1)
                dve.tensor_tensor(sq[:, :].rearrange("p (t m) -> p t m", t=TT),
                                  ident.unsqueeze(1).broadcast_to([P, TT, P]),
                                  rstd[:, :].unsqueeze(2).broadcast_to([P, TT, P]), ALU.mult)\
                    .then_inc(diag_ready, 1)

            def both(b):
                return ps[:, b:b + 2, 0:HALF]

            def halves(ap):
                return ap.rearrange("p (a b) -> p a b", a=2)

            def add_residual(c, b, scale):
                dve.scalar_tensor_tensor(out=halves(x[:, c, :]), in0=both(b), scalar=scale,
                                         in1=halves(x[:, c, :]), op0=ALU.mult, op1=ALU.add)\
                    .then_inc(res_added, 1)

            def ffn(k):
                base = U_FFN2 * k
                for c in range(C):
                    operand_lo(2 * k, c)
                    if c in (0, C - 1) and k == 0:
                        split_lo(c // 7 + 1, c // 7, 2048)
                if k:
                    mixer_lo(base + 1)
                mean_squares(2 * k)
                diagonals(2 * k)
                dve.wait_ge(rbc_ready, 2 * k + 1)

                def glu_step(u, s, n, first=False):
                    e = GU * k + u
                    if not first:
                        dve.wait_ge(hid_ready, e)
                    dve.wait_ge(unit_done, UF * k + u + 1)
                    dve.tensor_tensor(halves(glu_g[:, :]), both(4 * s), halves(rbc[:, :]), ALU.mult)\
                        .then_inc(glu_g_ready, 1)
                    dve.tensor_tensor(halves(glu_u[:, :]), both(4 * s + 2), halves(rbc[:, :]), ALU.mult)\
                        .then_inc(glu_free, 1)
                    split_lo(base + u + 3, s, n)
                    dve.wait_ge(tanh_ready, e + 1)
                    dve.scalar_tensor_tensor(out=glu_g[:, :], in0=glu_t[:, :], scalar=1.0, in1=glu_g[:, :],
                                             op0=ALU.add, op1=ALU.mult).then_inc(glu_m_ready, 1)
                    dve.wait_ge(glu_free, e + 1)
                    dve.wait_ge(glu_m_ready, e + 1)
                    dve.tensor_tensor(hid[:, bass.ds(u * TOK, TOK)], glu_g[:, :], glu_u[:, :], ALU.mult)\
                        .then_inc(hid_ready, 1)

                def hidden_lo(pair, tile_pair, s):
                    dve.wait_ge(hh_ready, DN * k + pair + 1)
                    dve.tensor_tensor(hl[:, s, :], hid[:, bass.ds(tile_pair * 2 * TOK, 2 * TOK)],
                                      hh[:, s, :].bitcast(F32), ALU.subtract).then_inc(hl_ready, 1)

                glu_step(0, 0, 2048, first=(k == 0))
                glu_step(1, 1, 2048)
                with dve.Fori(1, GU // 2 - 1) as i:
                    for s in range(2):
                        glu_step(2 * i + s, s, 2048)
                for s in range(2):
                    glu_step(GU - 2 + s, s, 1024)
                    hidden_lo(s, s, s)

                def down_step(v, s, tile_pair):
                    split_lo(base + GU + v + 3, s, 1024)
                    hidden_lo(v + 2, tile_pair, s)

                def add_half(first_chunk, v):
                    dve.wait_ge(unit_done, UF * k + GU + v + 1)
                    for j in range(4):
                        add_residual(first_chunk + j, 2 * j, 0.25)

                with dve.Fori(0, 4) as i:
                    for s in range(2):
                        down_step(2 * i + s, s, 2 * i + s + 2)
                down_step(8, 0, 10)
                down_step(9, 1, 0)
                add_half(0, 10)
                down_step(10, 0, 1)
                if k == 0:
                    for c in range(4):
                        operand_lo(1, c)
                down_step(11, 1, 2)
                with dve.Fori(0, 4) as i:
                    for s in range(2):
                        down_step(2 * i + 12 + s, s, 2 * i + s + 3)
                if k == 0:
                    mixer_lo(U_TOK)
                add_half(4, 21)
                if k == 0:
                    mixer_lo(U_TOK + 1)

            def rotate(z, n, ready):
                x1, x2 = z[:, :, :, 0:ROT], z[:, :, :, ROT:2 * ROT]
                cos = cos_t.unsqueeze(2).broadcast_to([P, TT, n, ROT])
                sin = sin_t.unsqueeze(2).broadcast_to([P, TT, n, ROT])
                a, b, c, d = [r[:, 0:TT * n * ROT].rearrange("p (t n r) -> p t n r", t=TT, n=n) for r in rot]
                dve.tensor_tensor(a, x1, cos, ALU.mult)
                dve.tensor_tensor(b, x2, sin, ALU.mult)
                dve.tensor_tensor(c, x1, sin, ALU.mult)
                link(dve.tensor_tensor(d, x2, cos, ALU.mult))
                dve.tensor_tensor(x1, a, b, ALU.subtract)
                ins = dve.tensor_tensor(x2, c, d, ALU.add)
                if ready is None:
                    link(ins)
                else:
                    ins.then_inc(ready, 1)

            def head_norm(z, n, g, ss_ready, rs_count, pieces):
                for t0, tn in pieces:
                    s = sq[:, 0:tn * n * HD].rearrange("p (t n d) -> p t n d", t=tn, n=n)
                    link(dve.tensor_tensor(s, z[:, t0:t0 + tn], z[:, t0:t0 + tn], ALU.mult))
                    link(dve.tensor_reduce(head_ss[:, t0 * n:(t0 + tn) * n].rearrange("p (t n) -> p t n", t=tn),
                                           s, AX.X, ALU.add))
                ss = head_ss[:, 0:TT * n]
                dve.tensor_scalar(ss, ss, 1.0 / HD, EPS, ALU.mult, ALU.add).then_inc(ss_ready, 1)
                dve.wait_ge(head_rs_ready, rs_count)
                rs = head_rs[:, 0:TT * n].rearrange("p (t n) -> p t n", t=TT).unsqueeze(3)
                link(dve.tensor_tensor(z, z, rs.broadcast_to([P, TT, n, HD]), ALU.mult))
                link(dve.tensor_tensor(z, z, g.unsqueeze(1).unsqueeze(1).broadcast_to([P, TT, n, HD]), ALU.mult))

            relus = [0]

            def add_head(t, h):
                n = relus[0]
                relus[0] += 1
                wait_bank_read(dve, ("dot", t, h))
                r, w, s = rp[:, n % 2, 0:width[t]], zwi[:, t, h:h + 1], scores[t]
                if h == 0:
                    ins = dve.tensor_scalar(s, r, w, None, ALU.mult)
                else:
                    dve.wait_ge(relu_used, n)
                    ins = dve.scalar_tensor_tensor(out=s, in0=r, scalar=w, in1=s, op0=ALU.mult, op1=ALU.add)
                ins.then_inc(relu_used, 1)

            def close_scores(t):
                link(dve.memset(scores[t][0:64, width[t] - 64:width[t]], NEVER))

            def top_rounds(t, n):
                for _ in range(n):
                    link(dve.max(top8[:, :], scores[t]))
                    link(dve.match_replace(scores[t], top8[:, :], scores[t], TAKEN))

            def mask_of(t):
                dve.tensor_scalar(masks[t], scores[t][:, 0:width[t]], TAKEN, OFF, ALU.is_gt, ALU.mult)\
                    .then_inc(mask_ready, 1)

            def proj_out(b):
                dve.wait_ge(proj_job, b + 1)
                src = both(2 * (b % 2))
                if b >= NPROJ:
                    c = (b - NPROJ) % NOUT
                    dve.scalar_tensor_tensor(out=halves(x[:, c, :]), in0=src, scalar=1.0,
                                             in1=halves(x[:, c, :]), op0=ALU.mult, op1=ALU.add)\
                        .then_inc(proj_evac, 1)
                    return
                i, part = b // 3, b % 3
                if part == 0:
                    dve.tensor_tensor(halves(conv_g[:, :]), src, halves(rbc[:, :]), ALU.mult)\
                        .then_inc(proj_evac, 1)
                elif part == 1:
                    if i:
                        dve.wait_ge(conv_done, i)
                    dve.wait_ge(proj_evac, b)
                    dve.tensor_tensor(halves(conv_v[:, :]), src, halves(conv_g[:, :]), ALU.mult)\
                        .then_inc(proj_evac, 1)
                else:
                    dve.tensor_tensor(halves(conv_b[:, :]), src, halves(rbc[:, :]), ALU.mult)\
                        .then_inc(proj_evac, 1)

            def neg_max(n):
                t, m = ITEMS[n]
                job = ("logit", n)
                wait_bank_full(dve, job)
                dve.tensor_reduce(stat[:, n:n + 1], ps[:, bank(job), 0:width[t]], AX.X, ALU.max, negate=True)\
                    .then_inc(max_ready, 1)

            def normalise(n):
                t, m = ITEMS[n]
                job = ("logit", n)
                wait_bank_read(dve, job)
                link(dve.reciprocal(stat[:, 80 + n:81 + n], stat[:, 40 + n:41 + n]))
                dve.tensor_scalar(rp[:, n % 2, 0:width[t]], rp[:, n % 2, 0:width[t]], stat[:, 80 + n:81 + n],
                                  None, ALU.mult).then_inc(p_ready, 1)

            dve.wait_ge(consts_in, 16 * 5)
            ffn(0)

            for c in range(4, C):
                operand_lo(1, c)
            mean_squares(1)
            diagonals(1)
            mixer_lo(U_TOK + 2)
            mixer_lo(U_TOK + 3)
            link(dve.tensor_scalar(gn[:, 0, :], gn[:, 0, :], HD ** -0.5, None, ALU.mult))
            dve.wait_ge(tok_evac, 10)
            dve.wait_ge(bcast_done, 2)
            link(dve.tensor_scalar(zwi[:, :, :], zwi[:, :, :], 8 ** -0.5 * HD ** -0.5, None, ALU.mult))
            dve.tensor_tensor(wfold[:, :].rearrange("p (r j t) -> p r j t", r=2, j=4),
                              zwi[:, 4, :].rearrange("p (j r) -> p r j", r=2).unsqueeze(3)
                              .broadcast_to([P, 2, 4, NT]),
                              same_t.unsqueeze(1).unsqueeze(1).broadcast_to([P, 2, 4, NT]), ALU.mult)\
                .then_inc(wfold_ready, 1)
            ki4 = zki[:, :, 0:HD].unsqueeze(2)
            head_norm(ki4, 1, gn[:, 2, :], ki_ss_ready, 1, [(0, 5)])
            rotate(ki4, 1, None)
            dve.tensor_copy(zki[:, :, HD:P], zki[:, :, 0:HD]).then_inc(ki_ready, 1)
            dve.wait_ge(tok_evac, 15)
            heads8 = zq[:, :, :].rearrange("p t (n d) -> p t n d", n=8)
            rotate(heads8, 8, qi_ready)
            mixer_lo(U_TOK + 4)
            mixer_lo(U_TOK + 5)
            wait_bank_full(dve, "wcol")
            dve.tensor_copy(wcols[:, :], ps[:, 6, 0:NB]).then_inc(bank_free[6], 1)
            for h in range(8):
                add_head(3, h)
            for h in range(8):
                add_head(2, h)
            dve.wait_ge(relu_used, 16)
            close_scores(3)
            close_scores(2)
            top_rounds(3, 8)
            mixer_lo(U_CONV)
            top_rounds(3, 8)
            mask_of(3)

            def weigh_sample(b):
                job = ("dot", 4, b)
                wait_bank_full(dve, job)
                if b == 0:
                    wait_bank_read(dve, "wcol")
                else:
                    if b >= 2:
                        dve.wait_ge(dec_relu_used, b - 1)
                dve.tensor_scalar(rp[:, b % 2, 0:SD], ps[:, bank(job), 0:SD], 0.0, wcols[:, b:b + 1],
                                  ALU.max, ALU.mult).then_inc(bank_free[bank(job)], 1)

            for b in range(NB):
                weigh_sample(b)
            wait_bank_full(dve, "decsum")
            dve.wait_ge(score_fill, 1)
            dve.tensor_copy(scores[4][:, 0:PAST], ps[:, 7, 0:PAST])
            dve.tensor_tensor(scores[4][:, PAST:SD], ps[:, 7, PAST:SD], other_b, ALU.add)\
                .then_inc(bank_free[7], 1)
            for h in range(8):
                add_head(1, h)
            dve.wait_ge(relu_used, 24)
            close_scores(1)
            mixer_lo(U_CONV + 1)
            dve.wait_ge(tok_evac, NJ)
            k4 = zkv[:, :, 0:P].rearrange("p t (n d) -> p t n d", n=2)
            head_norm(k4, 2, gn[:, 1, :], k_ss_ready, 2, [(0, 5)])
            rotate(k4, 2, k_ready)
            proj_out(0)
            proj_out(1)
            mixer_lo(U_CONV + 2)
            dve.wait_ge(k_ready, 1)
            head_norm(heads8, 8, gn[:, 0, :], q_ss_ready, 3, [(t, 1) for t in range(TT)])
            proj_out(2)
            rotate(heads8, 8, q_ready)
            proj_out(3)
            mixer_lo(U_CONV + 3)
            wait_bank_read(dve, "decsum")
            top_rounds(4, 5)
            proj_out(4)
            top_rounds(4, 4)
            mask_of(4)
            proj_out(5)
            mixer_lo(U_CONV + 4)
            top_rounds(2, 8)
            proj_out(6)
            top_rounds(2, 8)
            mask_of(2)
            proj_out(7)
            mixer_lo(U_CONV + 5)
            top_rounds(1, 8)
            proj_out(8)
            top_rounds(1, 8)
            mask_of(1)
            proj_out(9)
            mixer_lo(U_OUT)
            proj_out(10)
            proj_out(11)
            mixer_lo(U_OUT + 1)
            for i in range(4):
                dve.wait_ge(cvh_ready, i + 1)
                dve.tensor_tensor(xl[:, i, :], conv_o[:, i, :], xh[:, i, :].bitcast(F32), ALU.subtract)\
                    .then_inc(cvl_ready, 1)
            neg_max(0)
            neg_max(1)
            for n in range(len(ITEMS)):
                normalise(n)
                if n + 2 < len(ITEMS):
                    neg_max(n + 2)
                if n % 5 == 1:
                    proj_out(NPROJ + n // 5)
                if n % 8 == 7:
                    t = ATT_TILES[n // 8]
                    dve.wait_ge(att_h_ready, n // 8 + 1)
                    dve.tensor_tensor(attended(xl, t), pv_bank(t), attended(xh, t).bitcast(F32),
                                      ALU.subtract).then_inc(bank_free[7], 1)
                if n in (20, 39):
                    mixer_lo(U_OUT + (2 if n == 20 else 3))
            for b in range(NPROJ + NOUT, NPROJ + 2 * NOUT):
                proj_out(b)
                if b == NPROJ + NOUT + 3:
                    mixer_lo(U_FFN2)
            ffn(1)

        @block.gpsimd
        def _(pool):
            chained = [0]

            def link(ins):
                chained[0] += 1
                ins.then_inc(pchain, 1)
                pool.wait_ge(pchain, chained[0])

            def root(out, in_):
                return pool.tensor_tensor(out, in_, half_pow[:, 0:in_.shape[1]], ALU.pow)

            def add_squares(stage, c):
                pool.wait_ge(sq_ready, C * stage + c + 1)
                if c == 0:
                    ins = pool.tensor_copy(sqacc[:, :], sq[:, :])
                else:
                    pool.wait_ge(sq_added, C * stage + c)
                    ins = pool.tensor_tensor(sqacc[:, :], sqacc[:, :], sq[:, :], ALU.add)
                ins.then_inc(sq_added, 1)

            def norm_factors(stage):
                for c in range(C):
                    add_squares(stage, c)
                pool.wait_ge(var_ready, stage + 1)
                root(rstd[:, :], var[:, :]).then_inc(rstd_ready, 1)

            pool.memset(ones[:, :], 1.0).then_inc(ones_set, 1)
            pool.memset(half_pow[:, :], -0.5).then_inc(ones_set, 1)
            pool.memset(cstate[:, :, :, :], 0.0).then_inc(ones_set, 1)
            pool.wait_ge(ones_set, 3)
            norm_factors(0)
            norm_factors(1)
            pool.wait_ge(res_added, C)
            pool.memset(scores[4][:, SD:SD + PAD], -NEVER).then_inc(score_fill, 1)
            link(pool.memset(conv_u[:, 0:2], 0.0))
            link(pool.memset(masks[0], 0.0))
            pool.memset(masks[0][0:64, 64:128], OFF).then_inc(mask0_ready, 1)
            for n, ready in ((TT, ki_ss_ready), (2 * TT, k_ss_ready), (8 * TT, q_ss_ready)):
                pool.wait_ge(ready, 1)
                root(head_rs[:, 0:n], head_ss[:, 0:n]).then_inc(head_rs_ready, 1)

            u_samples = conv_u[:, 2 + SEQ:].rearrange("p (b t) -> p b t", b=NB)
            samples = lambda ap: ap.rearrange("p (b t) -> p b t", b=NB)

            def conv(i):
                link(pool.tensor_copy(u_samples[:, :, 0:2], cpast[:, i, :, :]))
                pool.wait_ge(proj_evac, 3 * i + 2)
                pool.tensor_tensor(conv_u[:, 2:2 + SEQ], conv_v[:, 0:SEQ], rbc[:, 0:SEQ], ALU.mult)
                link(pool.tensor_tensor(u_samples[:, :, 2:], samples(conv_v[:, SEQ:TOK]),
                                        samples(rbc[:, SEQ:TOK]), ALU.mult))
                pool.tensor_copy(cstate[:, i, 0, :], conv_u[:, SEQ:SEQ + 2])
                pool.tensor_copy(cstate[:, i, 1:, :], u_samples[:, :, NT:])
                for j in range(3):
                    dst = conv_o[:, i, :] if j == 0 else conv_v[:, :]
                    pool.tensor_scalar(dst[:, 0:SEQ], conv_u[:, j:j + SEQ], conv_w(i, j), 1.0, ALU.mult,
                                       ALU.mult)
                    link(pool.tensor_scalar(samples(dst[:, SEQ:TOK]), u_samples[:, :, j:j + NT],
                                            conv_w(i, j), 1.0, ALU.mult, ALU.mult))
                    if j:
                        link(pool.tensor_tensor(conv_o[:, i, :], conv_o[:, i, :], conv_v[:, :], ALU.add))
                pool.wait_ge(proj_evac, 3 * i + 3)
                pool.tensor_tensor(conv_o[:, i, :], conv_o[:, i, :], conv_b[:, :], ALU.mult)\
                    .then_inc(conv_done, 1)

            for i in range(4):
                conv(i)
            norm_factors(2)


def rotation_tables():
    pos = np.concatenate([np.arange(SEQ), PAST + np.arange(NB * NT) % NT]).astype(np.float32)
    inv = np.float32(500000.0) ** (-np.arange(ROT, dtype=np.float32) * np.float32(2.0 / (2 * ROT)))
    ang = pos[:, None] * inv[None, :].astype(np.float32)
    lay = lambda a: a.astype(np.float32).reshape(TT, P, ROT).transpose(1, 0, 2).reshape(P, TT * ROT)
    return lay(np.cos(ang)), lay(np.sin(ang))


def tables():
    p = np.arange(P)
    cos, sin = rotation_tables()
    same_t = (p[:, None] % NT == np.arange(NT)[None, :]).astype(np.float32)
    spread = np.zeros((P, 240), np.float32)
    spread[:, 112:128] = same_t
    same_b = (p[:, None] // NT == np.arange(NB)[None, :]).astype(np.float32)
    other = np.where(p[:, None] // NT == p[None, :] // NT, 0.0, OFF).astype(np.float32)
    return np.concatenate([np.eye(P, dtype=np.float32), cos, sin, same_t, spread, same_b, other], axis=1)


def bf_tables():
    p = np.arange(P)
    expand = (p[:, None, None] // NT == np.arange(NB)[None, :, None]) & (
        p[:, None, None] % NT == p[None, None, :] % NT)
    return np.concatenate([expand, np.eye(P, dtype=bool)[:, None, :]], axis=1).astype(mybir.dt.np(BF16))


def lay_out(i):
    a = {k: np.asarray(v) for k, v in i.items()}
    x_all = np.concatenate([a["x_prompt"].reshape(SEQ, D), a["x_sample"].reshape(NB * NT, D)])

    def gate_up(g, u):
        both = np.stack([g[0], u[0]]).reshape(2, C, P, NF, P)
        return both.transpose(3, 2, 0, 1, 4).reshape(NF, P, 2 * C * P)

    def down(w):
        return w[0].reshape(NF // 2, 2, P, 2, 4, P).transpose(3, 0, 2, 1, 4, 5).reshape(DN, P, 8 * P)

    w_in = a["w_in"][0]
    gb, gc, xv = (w_in[:, 512 * n:512 * (n + 1)] for n in range(3))
    q = w_in[:, 1536:2048].reshape(D, 2, NG, HD).transpose(0, 2, 1, 3).reshape(D, 512)
    kv, qi, kiwi = w_in[:, 2048:2304], w_in[:, 2304:2816], w_in[:, 2816:2888]
    cols = lambda w: w.reshape(C, P, -1).transpose(1, 0, 2).reshape(P, -1)
    tiles = [w[:, P * n:P * (n + 1)] for n in range(4) for w in (gc, xv, gb)]
    w_out = a["w_out"][0]
    att = w_out[512:].reshape(2, NG, HD, D).transpose(1, 0, 2, 3).reshape(512, D)
    w_o = np.stack([w_out[:512], att]).reshape(2, 4, P, 2, 4, P).transpose(0, 3, 2, 1, 4, 5)
    norms = np.concatenate([a[n].reshape(C, P).T for n in ("ffn1_norm", "mix_norm", "ffn2_norm")], axis=1)
    conv_w = a["conv_w"][0].reshape(3, 4, P).transpose(2, 1, 0).reshape(P, 12)
    gains = np.stack([a["q_norm"][0], a["k_norm"][0], a["idx_k_norm"][0]])
    return {
        "xt": x_all.reshape(TOK, C, P).transpose(2, 1, 0),
        "gu1": gate_up(a["ffn1_w_gate"], a["ffn1_w_up"]), "dn1": down(a["ffn1_w_down"]),
        "gu2": gate_up(a["ffn2_w_gate"], a["ffn2_w_up"]), "dn2": down(a["ffn2_w_down"]),
        "wtok": np.stack([cols(w) for w in (qi[:, :256], qi[:, 256:], kv, q[:, :256], q[:, 256:])]),
        "wkiwi": cols(kiwi),
        "wconv": np.stack([np.concatenate([cols(tiles[2 * n]), cols(tiles[2 * n + 1])], axis=1)
                           for n in range(6)]),
        "wout": w_o.reshape(4, P, 16 * P),
        "small": np.concatenate([norms, conv_w], axis=1),
        "gains": np.broadcast_to(gains[None], (P, 3, HD)),
        "kcache": a["cache_k"][0].transpose(2, 3, 0, 1).reshape(P, NB, PAST),
        "vcache": a["cache_v"][0].reshape(NB, 2, P, P).transpose(2, 0, 1, 3),
        "ikcache": a["cache_idx_k"][0].transpose(2, 0, 1),
        "conv_past": a["state_conv"][0].reshape(NB, 2, 4, P).transpose(3, 2, 0, 1),
        "tables": tables(), "bf_tables": bf_tables(),
    }


OUTS = {"y_out": (P, C, TOK), "k_out": (P, TT, P), "v_out": (P, TT, P), "ik_out": (P, TT, HD),
        "conv_out": (P, 4, NB + 1, 2)}


def build(nc, arrays):
    args = {n: nc.dram_tensor(n, v.shape, mybir.dt.from_np(v.dtype), kind="ExternalInput").ap()
            for n, v in arrays.items()}
    args |= {n: nc.dram_tensor(n, s, F32, kind="ExternalOutput").ap() for n, s in OUTS.items()}
    trunk(nc, **args)
    return nc


def kernel(**inputs):
    import concourse.bacc as bacc
    from concourse.bass_utils import run_bass_kernel_spmd

    arrays = {n: np.ascontiguousarray(v) for n, v in lay_out(inputs).items()}
    nc = build(bacc.Bacc("TRN2", target_bir_lowering=False, num_devices=1), arrays)
    r = run_bass_kernel_spmd(nc, [arrays], core_ids=[0]).results[0]
    y = r["y_out"].transpose(2, 1, 0).reshape(TOK, D)
    rows = lambda a: a.transpose(1, 0, 2).reshape(TOK, -1)
    k, v, ik = rows(r["k_out"]), rows(r["v_out"]), rows(r["ik_out"])
    state = r["conv_out"].transpose(2, 3, 1, 0).reshape(NB + 1, 2, 512)
    return (y[:SEQ].reshape(1, SEQ, D), y[SEQ:].reshape(NB, NT, D),
            k[:SEQ].reshape(1, 1, SEQ, 2, HD), v[:SEQ].reshape(1, 1, SEQ, 2, HD),
            ik[:SEQ].reshape(1, 1, SEQ, HD), state[:1].reshape(1, 1, 2, 512),
            k[SEQ:].reshape(1, NB, NT, 2, HD), v[SEQ:].reshape(1, NB, NT, 2, HD),
            ik[SEQ:].reshape(1, NB, NT, HD), state[1:].reshape(1, NB, 2, 512))
```

```python
from contextlib import ExitStack

import numpy as np

import concourse.bass as bass
from concourse import mybir

F32 = mybir.dt.float32
F32R = mybir.dt.float32r
BF16 = mybir.dt.bfloat16
ALU = mybir.AluOpType
ACT = mybir.ActivationFunctionType
AX = mybir.AxisListType

P = 128
D = 1024
C = D // P
F = 2816
NF = F // P
SEQ, NB, NT, PAST = 512, 8, 16, 256
TOK = SEQ + NB * NT
TT = TOK // P
HALF = TOK // 2
HD = 64
NG = 4
ROT = 8
KP = 128
KD = 68
PAD = 4
EPS = 1e-6
SD = PAST + P
TAKEN = -3.4e38
NEVER = -3.0e38
OFF = -1.0e30
GU, DN = NF, NF
UF = GU + DN
U_TOK, U_CONV, U_OUT, U_FFN2 = UF, UF + 6, UF + 12, UF + 16
TOK_N = (210, 210, 210, 210, 256, 256)
NJ = 5 * 6
NPROJ, NOUT = 12, 8


def trunk(nc, xt, gu1, dn1, gu2, dn2, wtok, wconv, wout, small, gains, kcache, vcache, ikcache,
          conv_past, tables, bf_tables, y_out, k_out, v_out, ik_out, conv_out):
    with ExitStack() as ctx:
        def sb(name, shape, dt=F32):
            return ctx.enter_context(nc.sbuf_tensor(name, shape, dt))

        def sem(name):
            return ctx.enter_context(nc.semaphore(name))

        ps = ctx.enter_context(nc.psum_tensor("ps", [P, 8, 512], F32))
        x = sb("x", [P, C, TOK])
        xh = sb("xh", [P, C, TOK], F32R)
        xl = sb("xl", [P, C, TOK], F32R)
        raw = sb("raw", [P, 2, 2048])
        wh = sb("wh", [P, 2, 2048], F32R)
        wl = sb("wl", [P, 2, 2048], F32R)
        rbc = sb("rbc", [P, TOK])
        sqacc = sb("sqacc", [P, TOK])
        sq = sb("sq", [P, TOK])
        ones = sb("ones", [P, P])
        half_pow = sb("half_pow", [P, 40])
        var = sb("var", [P, TT])
        rstd = sb("rstd", [P, TT])
        sm = sb("sm", [P, 36])
        gn = sb("gn", [P, 3, HD])
        tab = sb("tab", [P, 128 + 40 + 40 + 16 + 240 + 8 + 128])
        bft = sb("bft", [P, 9, P], BF16)
        cpast = sb("cpast", [P, 4, NB, 2])
        cstate = sb("cstate", [P, 4, NB + 1, 2])
        ident = tab[:, 0:128]
        cos_t = tab[:, 128:168].rearrange("p (t r) -> p t r", t=TT)
        sin_t = tab[:, 168:208].rearrange("p (t r) -> p t r", t=TT)
        same_t = tab[:, 208:224]
        spread = tab[:, 224:464]
        same_b = tab[:, 464:472]
        other_b = tab[:, 472:600]
        ident_bf = bft[:, 8, :]
        gain = lambda s, c: sm[:, 8 * s + c:8 * s + c + 1]
        conv_w = lambda i, j: sm[:, 24 + 3 * i + j:25 + 3 * i + j]

        with ExitStack() as ffn_scope:
            fs = lambda name, shape, dt=F32: ffn_scope.enter_context(nc.sbuf_tensor(name, shape, dt))
            hid = fs("hid", [P, NF * TOK])
            glu_g = fs("glu_g", [P, TOK])
            glu_t = fs("glu_t", [P, TOK])
            glu_u = fs("glu_u", [P, TOK])
            hh = fs("hh", [P, 2, 2 * TOK], F32R)
            hl = fs("hl", [P, 2, 2 * TOK], F32R)
        sq_odd = glu_u
        zq = sb("zq", [P, TT, 512])
        zkv = sb("zkv", [P, TT, 256])
        zki = sb("zki", [P, TT, P])
        zwi = sb("zwi", [P, TT, 8])
        qit_k = sb("qit_k", [P, 4 * TOK])
        q_all = sb("q_all", [P, NG * TOK])
        kt = sb("kt", [P, TOK])
        kit = sb("kit", [P, TOK])
        ikc_v = sb("ikc_v", [P, 2048])
        score = sb("score", [P, 256 + 384 + 512 + SD + PAD])
        mask = sb("mask", [P, 128 + 256 + 384 + 512 + SD], BF16)
        rp = sb("rp", [P, 2, 512])
        conv_g = sb("conv_g", [P, TOK])
        conv_v = sb("conv_v", [P, TOK])
        conv_b = sb("conv_b", [P, TOK])
        conv_u = sb("conv_u", [P, 2 + SEQ + NB * (NT + 2)])
        conv_o = sb("conv_o", [P, 4, TOK])
        stat = sb("stat", [P, 3 * 40])
        head_ss = sb("head_ss", [P, 55])
        head_rs = sb("head_rs", [P, 55])
        wcols = sb("wcols", [P, NB])
        wfold = sb("wfold", [P, P])
        top8 = sb("top8", [P, 8])

        qit = qit_k[:, 0:4 * SEQ].rearrange("p (j t) -> p j t", j=4)
        qit_s = qit_k[:, 4 * SEQ:].rearrange("p (b j t) -> p j b t", b=NB, j=4)
        qt = q_all[:, 0:4 * SEQ].rearrange("p (j t) -> p j t", j=4)
        qt_s = q_all[:, 4 * SEQ:].rearrange("p (b j t) -> p j b t", b=NB, j=4)
        kct = qit_k[:, 0:2048].rearrange("p (b s) -> p b s", b=NB)
        ikct = ikc_v[:, :].rearrange("p (b s) -> p b s", b=NB)
        vc = ikc_v[:, :].rearrange("p (b k d) -> p b k d", b=NB, k=2)
        wt = zq[:, :, :].rearrange("p t n -> p (t n)")[:, 0:1024].rearrange("p (s n) -> p s n", s=2)
        rot = [(sqacc if n < 2 else sq)[:, 320 * (n % 2):320 * (n % 2) + 320] for n in range(4)]
        score_at = {1: 0, 2: 256, 3: 640, 4: 1152}
        width = {0: 128, 1: 256, 2: 384, 3: 512, 4: SD}
        scores = {t: score[:, a:a + width[t] + (PAD if t == 4 else 0)] for t, a in score_at.items()}
        mask_at = {0: 0, 1: 128, 2: 384, 3: 768, 4: 1280}
        masks = {t: mask[:, a:a + width[t]] for t, a in mask_at.items()}

        x_in = [sem(f"x_in{i}") for i in range(4)]
        consts_in = sem("consts_in")
        ones_set = sem("ones_set")
        small_in = sem("small_in")
        raw_in = [sem("raw_in0"), sem("raw_in1")]
        part_in = [sem(f"part_in{i}") for i in range(4)]
        part_hi = sem("part_hi")
        part_lo = sem("part_lo")
        hi_ready = sem("hi_ready")
        lo_ready = sem("lo_ready")
        unit_done = sem("unit_done")
        xh_ready = sem("xh_ready")
        xl_ready = sem("xl_ready")
        sq_ready = sem("sq_ready")
        sq_added = sem("sq_added")
        colsum_done = sem("colsum_done")
        var_ready = sem("var_ready")
        rstd_ready = sem("rstd_ready")
        diag_ready = sem("diag_ready")
        bcast_done = sem("bcast_done")
        rbc_ready = sem("rbc_ready")
        glu_g_ready = sem("glu_g_ready")
        glu_free = sem("glu_free")
        tanh_ready = sem("tanh_ready")
        glu_m_ready = sem("glu_m_ready")
        hid_ready = sem("hid_ready")
        hh_ready = sem("hh_ready")
        hl_ready = sem("hl_ready")
        res_added = sem("res_added")
        tok_job = sem("tok_job")
        tok_evac = sem("tok_evac")
        proj_job = sem("proj_job")
        proj_evac = sem("proj_evac")
        bank_full = {b: sem(f"bank{b}_full") for b in range(4, 8)}
        bank_free = {b: sem(f"bank{b}_free") for b in range(4, 8)}
        ikc_in = sem("ikc_in")
        kc_in = sem("kc_in")
        vc_in = sem("vc_in")
        dchain = sem("vector_chain")
        pchain = sem("gpsimd_chain")
        ki_ss_ready = sem("ki_ss_ready")
        k_ss_ready = sem("k_ss_ready")
        q_ss_ready = sem("q_ss_ready")
        head_rs_ready = sem("head_rs_ready")
        ki_ready = sem("ki_ready")
        qi_ready = sem("qi_ready")
        k_ready = sem("k_ready")
        q_ready = sem("q_ready")
        wfold_ready = sem("wfold_ready")
        relu_used = sem("relu_used")
        dec_relu_used = sem("dec_relu_used")
        score_fill = sem("score_fill")
        mask0_ready = sem("mask0_ready")
        mask_ready = sem("mask_ready")
        conv_done = sem("conv_done")
        cvh_ready = sem("cvh_ready")
        cvl_ready = sem("cvl_ready")
        max_ready = sem("max_ready")
        p_ready = sem("p_ready")
        pv_done = sem("pv_done")
        att_h_ready = sem("att_h_ready")
        kv_stored = sem("kv_stored")
        y_stored = sem("y_stored")

        bank_use, uses = {}, {b: 0 for b in range(4, 8)}

        def place(job, bank):
            bank_use[job] = (bank, uses[bank])
            uses[bank] += 1

        DOT_TILES = (3, 2)
        ATT_TILES = (3, 4, 2, 1, 0)
        ITEMS = [(t, n) for t in ATT_TILES for n in range(8)]
        for n, job in enumerate(["tki0", "tki1", "tqi0", "tqi1", "tqi2", "tqi3", "tqi4"]):
            place(job, 4 + n % 2)
        place("wcol", 6)
        for n, (t, h) in enumerate([(t, h) for t in DOT_TILES for h in range(8)]):
            place(("dot", t, h), 4 + n % 3)
        for b in range(NB):
            place(("dot", 4, b), 4 + b % 3)
        place("decsum", 7)
        for h in range(8):
            place(("dot", 1, h), 4 + h % 3)
        for n, job in enumerate(["tk0", "tk1", "tq0", "tq1", "tq2", "tq3", "tq4"]):
            place(job, 4 + n % 2)
        for n, item in enumerate(ITEMS):
            place(("logit", n), 4 + n % 2)
            place(("turn", n), 6)
            if item[1] == 7:
                place(("pv", item[0]), 7)

        def parts_by(n):
            if n < 14:
                return min(4 * (n + 1), 32)
            return 32 + (32 * (n - 13) + 25) // 26

        def jobs_by(n):
            parts = parts_by(n)
            return 8 + parts // 8 if parts <= 32 else 12 + (parts - 32) // 4

        def item_of(job):
            return next(n for n in range(len(ITEMS)) if jobs_by(n) > job)

        OUT_SPLITS = {item_of(9): U_OUT, 10: U_OUT + 1, item_of(15): U_OUT + 2, item_of(19): U_OUT + 3}
        CONV_SPLITS = {8: 0, 9: 1, 11: 2, 12: 3}

        def part_cols(i):
            a = 1024 * (i % 2) + 512 * (i // 2)
            return slice(a, a + 512)

        def first_part(buf, i):
            return buf[:, 0, part_cols(i)]

        def wait_bank_free(eng, job):
            b, k = bank_use[job]
            if k:
                eng.wait_ge(bank_free[b], k)

        def wait_bank_full(eng, job):
            b, k = bank_use[job]
            eng.wait_ge(bank_full[b], k + 1)

        def wait_bank_read(eng, job):
            b, k = bank_use[job]
            eng.wait_ge(bank_free[b], k + 1)

        def bank(job):
            return bank_use[job][0]

        def wait_unit_used(eng, U):
            if U < U_TOK:
                eng.wait_ge(unit_done, U + 1)
            elif U < U_CONV:
                eng.wait_ge(tok_job, 5 * (U - U_TOK) + 5)
            elif U < U_OUT:
                eng.wait_ge(proj_job, 2 * (U - U_CONV) + 2)
            else:
                eng.wait_ge(proj_job, NPROJ + 4 * (U - U_OUT) + 4)

        def pv_bank(t):
            if t == 4:
                return ps[:, 7, :].rearrange("p (b g t) -> p b g t", b=NB, g=NG)
            return ps[:, 7, :].rearrange("p (g t) -> p g t", g=NG)

        def attended(buf, t):
            if t == 4:
                return buf[:, 4:8, SEQ:TOK].rearrange("p g (b t) -> p b g t", b=NB)
            return buf[:, 4:8, t * P:(t + 1) * P]

        unit_n = {U_TOK + i: 8 * n for i, n in enumerate(TOK_N)}

        block = ctx.enter_context(nc.Block())

        @block.sync
        def _(sp):
            def load(U, k, slot, src, n, wait=True):
                if wait:
                    sp.wait_ge(lo_ready, U - 1)
                sp.dma_start(raw[:, slot, 0:n], src).then_inc(raw_in[slot], 16)

            def ffn(gu, dn, base):
                first = 0
                if base == 0:
                    for i in range(4):
                        sp.dma_start(first_part(raw, i), gu[0][:, part_cols(i)]).then_inc(part_in[i], 16)
                    load(1, 0, 1, gu[1], 2048, wait=False)
                    first = 1
                with sp.Fori(first, GU // 2) as i:
                    for s in range(2):
                        load(base + 2 * i + s, 0, s, gu[2 * i + s], 2048)
                with sp.Fori(0, DN // 2) as i:
                    for s in range(2):
                        load(base + GU + 2 * i + s, 0, s, dn[2 * i + s], 1024)

            ffn(gu1, dn1, 0)
            for n, U in enumerate(range(U_TOK, U_CONV)):
                load(U, 0, U % 2, wtok[n, :, 0:unit_n[U]], unit_n[U])
            for n, U in enumerate(range(U_CONV, U_OUT)):
                load(U, 0, U % 2, wconv[n], 2048)
            for n, U in enumerate(range(U_OUT, U_FFN2)):
                load(U, 0, U % 2, wout[n], 2048)
            sp.wait_ge(k_ready, 1)
            sp.wait_ge(ki_ready, 1)
            sp.wait_ge(conv_done, 4)
            sp.wait_ge(tok_evac, NJ)
            sp.dma_start(k_out, zkv[:, :, 0:128]).then_inc(kv_stored, 16)
            sp.dma_start(v_out, zkv[:, :, 128:256]).then_inc(kv_stored, 16)
            sp.dma_start(ik_out, zki[:, :, 0:HD]).then_inc(kv_stored, 16)
            sp.dma_start(conv_out, cstate[:, :, :, :]).then_inc(kv_stored, 16)
            ffn(gu2, dn2, U_FFN2)
            for c in range(C):
                sp.wait_ge(res_added, C + c + 1)
                sp.dma_start(y_out[:, c, :], x[:, c, :]).then_inc(y_stored, 16)
            sp.wait_ge(kv_stored, 64)
            sp.wait_ge(y_stored, 16 * C)

        @block.tensor
        def _(pe):
            def three(out, ah, al, bh, bl, first, last):
                pe.matmul(out, ah, bh, start=first, stop=False)
                pe.matmul(out, ah, bl, start=False, stop=False)
                return pe.matmul(out, al, bh, start=False, stop=last)

            def token_halves(banks, ah, al, bh, bl, first, last):
                outs = [ps[:, b, 0:HALF] for b in banks]
                cols = [slice(0, HALF), slice(HALF, TOK)]
                for o, c in zip(outs, cols):
                    pe.matmul(o, ah, bh[:, c], start=first, stop=False)
                for o, c in zip(outs, cols):
                    pe.matmul(o, ah, bl[:, c], start=False, stop=False)
                for o, c in zip(outs, cols):
                    last_mm = pe.matmul(o, al, bh[:, c], start=False, stop=last)
                return last_mm

            def column_sums(stage):
                pe.wait_ge(sq_added, (C - 1) * (stage + 1))
                for t in range(TT):
                    mm = pe.matmul(ps[:, 7, t:t + 1], sqacc[:, t * P:(t + 1) * P], ones[:, 0:1],
                                   start=True, stop=True)
                mm.then_inc(colsum_done, 1)

            def broadcast_rstd(stage):
                pe.wait_ge(diag_ready, stage + 1)
                pe.matmul(ps[:, 6, :], ones[:, :], sq[:, 0:512], start=True, stop=True)
                pe.matmul(ps[:, 7, 0:P], ones[:, :], sq[:, 512:TOK], start=True, stop=True)\
                    .then_inc(bcast_done, 1)

            def weight(w, slot, i):
                return w[:, slot, i * P:(i + 1) * P]

            def glu_part(slot, m, c):
                b = 4 * slot + 2 * m
                return token_halves((b, b + 1), weight(wh, slot, 8 * m + c), weight(wl, slot, 8 * m + c),
                                    xh[:, c, :], xl[:, c, :], c == 0, c == C - 1)

            def glu_unit(slot):
                for m in range(2):
                    for c in range(C):
                        mm = glu_part(slot, m, c)
                mm.then_inc(unit_done, 1)

            def down_unit(slot, first, last, bank_waits=None):
                for f in range(2):
                    for j in range(4):
                        if first and f == 0:
                            pe.wait_ge(*bank_waits[j])
                        mm = token_halves((2 * j, 2 * j + 1), weight(wh, slot, 4 * f + j),
                                          weight(wl, slot, 4 * f + j),
                                          hh[:, slot, f * TOK:(f + 1) * TOK],
                                          hl[:, slot, f * TOK:(f + 1) * TOK],
                                          first and f == 0, last and f == 1)
                mm.then_inc(unit_done, 1)

            def ffn(k):
                stage, base = 2 * k, U_FFN2 * k
                if k:
                    pe.wait_ge(lo_ready, base + 1)
                for part, (cs, m) in enumerate((cs, m) for cs in (range(0, 4), range(4, 8)) for m in range(2)):
                    if k == 0:
                        pe.wait_ge(*((part_lo, part + 1) if part < 3 else (lo_ready, 1)))
                    if k and cs[0] == 0:
                        pe.wait_ge(proj_evac, NPROJ + 2 * NOUT - 1 + m)
                    for c in cs:
                        if m == 0:
                            pe.wait_ge(xh_ready, C * stage + c + 1)
                            pe.wait_ge(xl_ready, C * stage + c + 1)
                        mm = glu_part(0, m, c)
                mm.then_inc(unit_done, 1)
                column_sums(stage)
                pe.wait_ge(lo_ready, base + 2)
                for c in range(4):
                    glu_part(1, 0, c)
                broadcast_rstd(stage)
                for c in range(4, C):
                    glu_part(1, 0, c)
                pe.wait_ge(rbc_ready, stage + 1)
                for c in range(C):
                    mm = glu_part(1, 1, c)
                mm.then_inc(unit_done, 1)
                with pe.Fori(1, GU // 2) as i:
                    for s in range(2):
                        pe.wait_ge(lo_ready, base + 2 * i + s + 1)
                        pe.wait_ge(glu_free, GU * k + 2 * i + s - 1)
                        glu_unit(s)

                def down(v, first=False, last=False, slot=0, bank_waits=None):
                    pe.wait_ge(lo_ready, base + GU + v + 1)
                    pe.wait_ge(hl_ready, DN * k + v + 1)
                    down_unit(slot, first, last, bank_waits)

                down(0, first=True, slot=0, bank_waits=[(glu_free, GU * (k + 1) - (j < 2)) for j in range(4)])
                with pe.Fori(0, 4) as i:
                    down(2 * i + 1, slot=1)
                    down(2 * i + 2, slot=0)
                down(9, slot=1)
                down(10, last=True, slot=0)
                down(11, first=True, slot=1, bank_waits=[(res_added, C * k + j + 1) for j in range(4)])
                with pe.Fori(0, 4) as i:
                    down(2 * i + 12, slot=0)
                    down(2 * i + 13, slot=1)
                down(20, slot=0)
                down(21, last=True, slot=1)

            def tok_unit_weight(w, U, c):
                n = unit_n[U] // 8
                return w[:, U % 2, c * n:(c + 1) * n]

            def tok_part(U, t, cs):
                J = 5 * (U - U_TOK) + t
                n = unit_n[U] // 8
                for c in cs:
                    mm = three(ps[:, J % 4, 0:n], xh[:, c, t * P:(t + 1) * P], xl[:, c, t * P:(t + 1) * P],
                               tok_unit_weight(wh, U, c), tok_unit_weight(wl, U, c), c == 0, c == C - 1)
                return mm

            def tok_job_of(U, t):
                J = 5 * (U - U_TOK) + t
                if J >= 4:
                    pe.wait_ge(tok_evac, J - 3)
                tok_part(U, t, range(C)).then_inc(tok_job, 1)

            def tok_unit(U):
                pe.wait_ge(lo_ready, U + 1)
                for t in range(TT):
                    tok_job_of(U, t)

            def turn_token_tile(job, pieces):
                wait_bank_free(pe, job)
                for i, piece in enumerate(pieces):
                    mm = pe.transpose(ps[:, bank(job), i * P:(i + 1) * P], piece, ident)
                mm.then_inc(bank_full[bank(job)], 1)

            def dots(t, h):
                job = ("dot", t, h)
                j, r = h // 2, HD * (h % 2)
                wait_bank_free(pe, job)
                pe.matmul(ps[:, bank(job), 0:width[t]], qit[r:r + HD, j, t * P:(t + 1) * P],
                          kit[r:r + HD, 0:width[t]], start=True, stop=True)\
                    .then_inc(bank_full[bank(job)], 1)

            def dots_sample(b):
                job = ("dot", 4, b)
                wait_bank_free(pe, job)
                for r in (0, HD):
                    q = qit_k[r:r + HD, 4 * SEQ + b * HD:4 * SEQ + (b + 1) * HD]
                    pe.matmul(ps[r:r + HD, bank(job), 0:PAST], q, ikct[r:r + HD, b, :], start=True, stop=True)
                    mm = pe.matmul(ps[r:r + HD, bank(job), PAST:SD], q, kit[r:r + HD, SEQ:TOK],
                                   start=True, stop=True)
                mm.then_inc(bank_full[bank(job)], 1)

            def sum_heads(b):
                wait_bank_read(pe, ("dot", 4, b))
                mm = pe.matmul(ps[:, bank("decsum"), 0:SD], spread[:, 112 - NT * b:240 - NT * b],
                               rp[:, b % 2, 0:SD], start=(b == 0), stop=(b == NB - 1))
                mm.then_inc(dec_relu_used, 1)
                if b == NB - 1:
                    pe.matmul(ps[:, bank("decsum"), SD:SD + 1], ident, ones[:, 0:1], start=True, stop=True)\
                        .then_inc(bank_full[bank("decsum")], 1)

            def proj_part(b, c):
                U = U_CONV + b // 2 if b < NPROJ else U_OUT + (b - NPROJ) // 4
                if c == 0:
                    pe.wait_ge(lo_ready, U + 1)
                    if b < 2:
                        pe.wait_ge(tok_evac, NJ)
                    else:
                        pe.wait_ge(proj_evac, b - 1)
                banks = (2 * (b % 2), 2 * (b % 2) + 1)
                if b < NPROJ:
                    i, chunk, last = 8 * (b % 2) + c, c, c == C - 1
                else:
                    i, chunk, last = 4 * c + (b - NPROJ) % 4, 4 * ((b - NPROJ) // NOUT) + c, c == 3
                mm = token_halves(banks, weight(wh, U % 2, i), weight(wl, U % 2, i), xh[:, chunk, :],
                                  xl[:, chunk, :], c == 0, last)
                if last:
                    mm.then_inc(proj_job, 1)

            def proj(b):
                for c in range(C if b < NPROJ else 4):
                    proj_part(b, c)

            def logits(n):
                t, m = ITEMS[n]
                job = ("logit", n)
                if t:
                    pe.wait_ge(mask_ready, ATT_TILES.index(t) + 1)
                else:
                    pe.wait_ge(mask0_ready, 1)
                wait_bank_free(pe, job)
                out = ps[:, bank(job), 0:width[t]]
                if t == 4:
                    pe.matmul(out, bft[:, m, :], masks[t], start=True, stop=False)
                    for r in (0, HD):
                        q = q_all[r:r + HD, 4 * SEQ + m * HD:4 * SEQ + (m + 1) * HD]
                        pe.matmul(ps[r:r + HD, bank(job), 0:PAST], q, kct[r:r + HD, m, :],
                                  start=False, stop=False)
                        mm = pe.matmul(ps[r:r + HD, bank(job), PAST:SD], q, kt[r:r + HD, SEQ:TOK],
                                       start=False, stop=True)
                else:
                    g, r = m // 2, HD * (m % 2)
                    pe.matmul(out, ident_bf, masks[t], start=True, stop=False)
                    mm = pe.matmul(out, qt[r:r + HD, g, t * P:(t + 1) * P], kt[r:r + HD, 0:width[t]],
                                   start=False, stop=True)
                mm.then_inc(bank_full[bank(job)], 1)

            def turn_weights(n):
                pe.wait_ge(p_ready, n + 1)
                turn_token_tile(("turn", n), [rp[:, n % 2, k * P:(k + 1) * P]
                                              for k in range(width[ITEMS[n][0]] // P)])

            def weigh_values(n):
                t, m = ITEMS[n]
                if m == 0:
                    wait_bank_free(pe, ("pv", t))
                wait_bank_read(pe, ("turn", n))
                blocks = width[t] // P
                if t == 4:
                    for r in (0, HD):
                        for k in range(blocks):
                            v = vc[:, m, k, r:r + HD] if k < 2 else zkv[:, 4, P + r:P + r + HD]
                            mm = pe.matmul(ps[r:r + HD, 7, m * HD:(m + 1) * HD], v,
                                           wt[:, n % 2, k * P + r:k * P + r + HD],
                                           start=(k == 0), stop=(k == blocks - 1))
                else:
                    g, r = m // 2, HD * (m % 2)
                    for k in range(blocks):
                        mm = pe.matmul(ps[r:r + HD, 7, g * P:(g + 1) * P], zkv[:, k, P + r:P + r + HD],
                                       wt[:, n % 2, k * P:(k + 1) * P],
                                       start=(k == 0), stop=(k == blocks - 1))
                mm.then_inc(pv_done, 1)

            pe.wait_ge(ones_set, 3)
            ffn(0)

            pe.wait_ge(lo_ready, U_TOK + 1)
            for cs in (range(0, 4), range(4, 8)):
                for t in range(4):
                    if t == 0:
                        pe.wait_ge(xh_ready, C + cs[-1] + 1)
                        pe.wait_ge(xl_ready, C + cs[-1] + 1)
                    if cs[0] == 0:
                        pe.wait_ge(res_added, 4 + t // 2 + 1)
                    mm = tok_part(U_TOK, t, cs)
                    if cs[0] == 4:
                        mm.then_inc(tok_job, 1)
                    if cs[0] == 4 and t == 2:
                        column_sums(1)
            tok_job_of(U_TOK, 4)
            tok_unit(U_TOK + 1)
            broadcast_rstd(1)
            tok_unit(U_TOK + 2)
            tok_unit(U_TOK + 3)
            pe.wait_ge(rbc_ready, 2)
            pe.wait_ge(consts_in, 16 * 4)
            pe.wait_ge(ki_ready, 1)
            turn_token_tile("tki0", [zki[:, t, :] for t in range(4)])
            turn_token_tile("tki1", [zki[:, 4, :]])
            pe.wait_ge(wfold_ready, 1)
            wait_bank_free(pe, "wcol")
            pe.matmul(ps[:, 6, 0:NB], wfold[:, :], same_b, start=True, stop=True).then_inc(bank_full[6], 1)
            pe.wait_ge(qi_ready, 1)
            for t in range(TT):
                turn_token_tile(f"tqi{t}", [zq[:, t, j * P:(j + 1) * P] for j in range(4)])
            for job in ("tki0", "tki1", "tqi3", "tqi4"):
                wait_bank_read(pe, job)
            for t in DOT_TILES:
                for h in range(8):
                    dots(t, h)
            tok_unit(U_TOK + 4)
            tok_unit(U_TOK + 5)
            proj(0)
            pe.wait_ge(ikc_in, 32)
            dots_sample(0)
            dots_sample(1)
            for b in range(NB):
                if b + 2 < NB:
                    dots_sample(b + 2)
                proj_part(1, b)
                sum_heads(b)
            for h in range(8):
                dots(1, h)
            proj(2)
            proj(3)
            pe.wait_ge(k_ready, 1)
            turn_token_tile("tk0", [zkv[:, t, 0:P] for t in range(4)])
            turn_token_tile("tk1", [zkv[:, 4, 0:P]])
            proj(4)
            pe.wait_ge(q_ready, 1)
            for t in range(TT):
                turn_token_tile(f"tq{t}", [zq[:, t, j * P:(j + 1) * P] for j in range(4)])
            for b in range(5, 8):
                proj(b)
            for job in ("tk0", "tk1", "tq3", "tq4"):
                wait_bank_read(pe, job)
            pe.wait_ge(kc_in, 16)
            pe.wait_ge(vc_in, 16)
            logits(0)
            logits(1)
            for n in range(len(ITEMS)):
                turn_weights(n)
                if n + 2 < len(ITEMS):
                    logits(n + 2)
                for i in range(parts_by(n - 1), parts_by(n)):
                    if i == 32:
                        pe.wait_ge(cvl_ready, 4)
                    proj_part(8 + i // 8, i % 8) if i < 32 else proj_part(12 + (i - 32) // 4, i % 4)
                weigh_values(n)
            wait_bank_read(pe, ("pv", ATT_TILES[-1]))
            for b in range(NPROJ + NOUT, NPROJ + 2 * NOUT):
                proj(b)
            ffn(1)

        @block.scalar
        def _(act):
            def copy(out, in_, scale=1.0):
                return nc.scalar.activation(out, in_, ACT.Copy, scale=scale)

            def split_hi(U, k, slot, n):
                act.wait_ge(raw_in[slot], 16 * (k + slot))
                copy(wh[:, slot, 0:n], raw[:, slot, 0:n]).then_inc(hi_ready, 1)

            def operand_hi(stage, c):
                copy(xh[:, c, :], x[:, c, :], scale=gain(stage, c)).then_inc(xh_ready, 1)

            def square(stage, c):
                if stage and c == 0:
                    act.wait_ge(bcast_done, stage)
                if c > 2:
                    act.wait_ge(sq_added, (C - 1) * stage + c - 2)
                dst = sqacc if c == 0 else (sq, sq_odd)[c % 2]
                nc.scalar.activation(dst[:, :], x[:, c, :], ACT.Square).then_inc(sq_ready, 1)

            def rstd_out(stage):
                act.wait_ge(bcast_done, stage + 1)
                copy(rbc[:, :], ps[:, 6:8, :].rearrange("p a b -> p (a b)")[:, 0:TOK]).then_inc(rbc_ready, 1)

            def mixer_hi(U):
                wait_unit_used(act, U - 2)
                split_hi(U, U // 2, U % 2, unit_n.get(U, 2048))

            def ffn(k):
                base = U_FFN2 * k
                if k == 0:
                    act.wait_ge(small_in, 16)
                for c in range(C):
                    if k == 0:
                        act.wait_ge(x_in[c // 2], 16)
                    else:
                        act.wait_ge(proj_evac, NPROJ + NOUT + c + 1)
                        if c >= 4:
                            act.wait_ge(proj_job, NPROJ + 2 * NOUT)
                    operand_hi(2 * k, c)
                    if k == 0 and c in (0, 1, 4, 5):
                        i = (0, 1, None, None, 2, 3)[c]
                        act.wait_ge(part_in[i], 16)
                        copy(first_part(wh, i), first_part(raw, i)).then_inc(part_hi if i < 3 else hi_ready, 1)
                if k:
                    for c in range(C):
                        square(2 * k, c)
                    mixer_hi(base + 1)
                else:
                    for c in range(4):
                        square(0, c)
                    split_hi(1, 0, 1, 2048)
                    for c in range(4, C):
                        square(0, c)
                rstd_out(2 * k)

                def glu_step(u, half, s, n):
                    act.wait_ge(unit_done, UF * k + u + 1)
                    split_hi(None, base // 2 + half + 1, s, n)
                    act.wait_ge(glu_g_ready, GU * k + u + 1)
                    nc.scalar.activation(glu_t[:, :], glu_g[:, :], ACT.Tanh, scale=0.5).then_inc(tanh_ready, 1)

                def hidden_hi(pair, tile_pair, s):
                    copy(hh[:, s, :], hid[:, bass.ds(tile_pair * 2 * TOK, 2 * TOK)]).then_inc(hh_ready, 1)

                with act.Fori(0, GU // 2 - 1) as i:
                    for s in range(2):
                        glu_step(2 * i + s, i, s, 2048)
                act.wait_ge(hid_ready, GU * k + 2)
                for s in range(2):
                    glu_step(GU - 2 + s, GU // 2 - 1, s, 1024)
                    act.wait_ge(hid_ready, GU * k + 2 * s + 2)
                    hidden_hi(s, s, s)

                def down_step(v, half, s, tile_pair):
                    act.wait_ge(unit_done, UF * k + GU + v + 1)
                    split_hi(None, (base + GU) // 2 + half + 1, s, 1024)
                    hidden_hi(None, tile_pair, s)

                with act.Fori(0, 4) as i:
                    for s in range(2):
                        down_step(2 * i + s, i, s, 2 * i + s + 2)
                act.wait_ge(hid_ready, GU * (k + 1))
                down_step(8, 4, 0, 10)
                down_step(9, 4, 1, 0)
                down_step(10, 5, 0, 1)
                if k == 0:
                    for c in range(4):
                        act.wait_ge(res_added, c + 1)
                        operand_hi(1, c)
                    for c in range(4):
                        square(1, c)
                down_step(11, 5, 1, 2)
                with act.Fori(0, 4) as i:
                    for s in range(2):
                        down_step(2 * i + 12 + s, i + 6, s, 2 * i + s + 3)
                if k == 0:
                    mixer_hi(U_TOK)
                    mixer_hi(U_TOK + 1)

            def tok_out(U, t):
                J = 5 * (U - U_TOK) + t
                act.wait_ge(tok_job, J + 1)
                s, p = rstd[:, t:t + 1], ps[:, J % 4, :]
                i = U - U_TOK
                pieces = {0: [(0, 64, zki[:, t, 0:HD]), (64, 72, zwi[:, t, :]), (72, 210, zq[:, t, 0:138])],
                          1: [(0, 210, zq[:, t, 138:348])],
                          2: [(0, 164, zq[:, t, 348:512]), (164, 210, zkv[:, t, 0:46])],
                          3: [(0, 210, zkv[:, t, 46:256])],
                          4: [(0, 256, zq[:, t, 0:256])], 5: [(0, 256, zq[:, t, 256:512])]}[i]
                for a, b, dst in pieces:
                    ins = copy(dst, p[:, a:b], scale=s)
                ins.then_inc(tok_evac, 1)

            def turned_out(job, dst, n):
                wait_bank_full(act, job)
                src = ps[:, bank(job), 0:n * P]
                if len(dst.shape) == 3:
                    src = src.rearrange("p (j t) -> p j t", j=n)
                elif len(dst.shape) == 4:
                    src = src.rearrange("p (j b t) -> p j b t", j=n, b=NB)
                copy(dst, src).then_inc(bank_free[bank(job)], 1)

            def relu_out(t, h, n):
                job = ("dot", t, h)
                wait_bank_full(act, job)
                if n >= 2:
                    act.wait_ge(relu_used, n - 1)
                nc.scalar.activation(rp[:, n % 2, 0:width[t]], ps[:, bank(job), 0:width[t]], ACT.Relu)\
                    .then_inc(bank_free[bank(job)], 1)

            def exp_out(n):
                t, m = ITEMS[n]
                act.wait_ge(max_ready, n + 1)
                if n >= 2:
                    wait_bank_full(act, ("turn", n - 2))
                job = ("logit", n)
                nc.scalar.activation(rp[:, n % 2, 0:width[t]], ps[:, bank(job), 0:width[t]], ACT.Exp,
                                     bias=stat[:, n:n + 1], accum_out=stat[:, 40 + n:41 + n])\
                    .then_inc(bank_free[bank(job)], 1)

            def weights_out(n):
                t, m = ITEMS[n]
                job = ("turn", n)
                wait_bank_full(act, job)
                if n >= 2:
                    act.wait_ge(pv_done, n - 1)
                copy(wt[:, n % 2, 0:width[t]], ps[:, 6, 0:width[t]]).then_inc(bank_free[6], 1)

            def conv_hi(i):
                act.wait_ge(conv_done, i + 1)
                copy(xh[:, i, :], conv_o[:, i, :]).then_inc(cvh_ready, 1)

            def attended_hi(i):
                t = ATT_TILES[i]
                act.wait_ge(pv_done, 8 * (i + 1))
                copy(attended(xh, t), pv_bank(t)).then_inc(att_h_ready, 1)

            for i in range(4):
                act.dma_start(x[:, 2 * i:2 * i + 2, :], xt[:, 2 * i:2 * i + 2, :]).then_inc(x_in[i], 16)
                if i == 0:
                    act.dma_start(sm[:, :], small).then_inc(small_in, 16)
            for dst, src in ((tab[:, :], tables), (gn[:, :, :], gains), (bft[:, :, :], bf_tables),
                             (cpast[:, :, :, :], conv_past)):
                act.dma_start(dst, src).then_inc(consts_in, 16)
            ffn(0)

            for c in range(4, C):
                act.wait_ge(res_added, c + 1)
                operand_hi(1, c)
            for c in range(4, C):
                square(1, c)
            act.wait_ge(res_added, 8)
            for r in (0, HD):
                act.dma_start(ikct[r:r + HD, :, :], ikcache).then_inc(ikc_in, 16)
            act.wait_ge(rstd_ready, 2)
            for t in range(TT):
                tok_out(U_TOK, t)
            mixer_hi(U_TOK + 2)
            for t in range(TT):
                tok_out(U_TOK + 1, t)
            mixer_hi(U_TOK + 3)
            rstd_out(1)
            for t in range(TT):
                tok_out(U_TOK + 2, t)
            mixer_hi(U_TOK + 4)
            for t in range(TT):
                tok_out(U_TOK + 3, t)
            mixer_hi(U_TOK + 5)

            turned_out("tki0", kit[:, 0:SEQ], 4)
            turned_out("tki1", kit[:, SEQ:TOK], 1)
            for t in range(TT):
                turned_out(f"tqi{t}", qit[:, :, t * P:(t + 1) * P] if t < 4 else qit_s, 4)
            n = 0
            for t in DOT_TILES:
                for h in range(8):
                    relu_out(t, h, n)
                    n += 1
            for t in range(TT):
                tok_out(U_TOK + 4, t)
            mixer_hi(U_CONV)
            for t in range(TT):
                tok_out(U_TOK + 5, t)
            mixer_hi(U_CONV + 1)
            for h in range(8):
                relu_out(1, h, n)
                n += 1
            act.wait_ge(relu_used, 24)
            act.dma_start(kct, kcache).then_inc(kc_in, 16)
            act.dma_start(vc, vcache).then_inc(vc_in, 16)
            mixer_hi(U_CONV + 2)
            mixer_hi(U_CONV + 3)
            turned_out("tk0", kt[:, 0:SEQ], 4)
            turned_out("tk1", kt[:, SEQ:TOK], 1)
            for t in range(TT):
                turned_out(f"tq{t}", qt[:, :, t * P:(t + 1) * P] if t < 4 else qt_s, 4)
            mixer_hi(U_CONV + 4)
            mixer_hi(U_CONV + 5)
            exp_out(0)
            exp_out(1)
            for n in range(len(ITEMS)):
                weights_out(n)
                if n + 2 < len(ITEMS):
                    exp_out(n + 2)
                if n in OUT_SPLITS:
                    mixer_hi(OUT_SPLITS[n])
                if n in CONV_SPLITS:
                    act.wait_ge(proj_job, NPROJ)
                    conv_hi(CONV_SPLITS[n])
                if n % 8 == 7:
                    attended_hi(n // 8)
            mixer_hi(U_FFN2)
            act.wait_ge(kv_stored, 64)
            ffn(1)

        @block.vector
        def _(dve):
            chained = [0]

            def link(ins):
                chained[0] += 1
                ins.then_inc(dchain, 1)
                dve.wait_ge(dchain, chained[0])

            def split_lo(n_ready, slot, n):
                dve.wait_ge(hi_ready, n_ready)
                dve.tensor_tensor(wl[:, slot, 0:n], raw[:, slot, 0:n], wh[:, slot, 0:n].bitcast(F32),
                                  ALU.subtract).then_inc(lo_ready, 1)

            def mixer_lo(U):
                split_lo(U + 1, U % 2, unit_n.get(U, 2048))

            def operand_lo(stage, c):
                dve.wait_ge(xh_ready, C * stage + c + 1)
                dve.scalar_tensor_tensor(out=xl[:, c, :], in0=x[:, c, :], scalar=gain(stage, c),
                                         in1=xh[:, c, :].bitcast(F32), op0=ALU.mult, op1=ALU.subtract)\
                    .then_inc(xl_ready, 1)

            def mean_squares(stage):
                dve.wait_ge(colsum_done, stage + 1)
                dve.tensor_scalar(var[:, :], ps[:, 7, 0:TT], 1.0 / D, EPS, ALU.mult, ALU.add)\
                    .then_inc(var_ready, 1)

            def diagonals(stage):
                dve.wait_ge(rstd_ready, stage + 1)
                if stage == 0:
                    dve.wait_ge(consts_in, 16 * 4)
                dve.tensor_tensor(sq[:, :].rearrange("p (t m) -> p t m", t=TT),
                                  ident.unsqueeze(1).broadcast_to([P, TT, P]),
                                  rstd[:, :].unsqueeze(2).broadcast_to([P, TT, P]), ALU.mult)\
                    .then_inc(diag_ready, 1)

            def both(b):
                return ps[:, b:b + 2, 0:HALF]

            def halves(ap):
                return ap.rearrange("p (a b) -> p a b", a=2)

            def add_residual(c, b, scale):
                dve.scalar_tensor_tensor(out=halves(x[:, c, :]), in0=both(b), scalar=scale,
                                         in1=halves(x[:, c, :]), op0=ALU.mult, op1=ALU.add)\
                    .then_inc(res_added, 1)

            def ffn(k):
                base = U_FFN2 * k
                if k == 0:
                    for c in range(C):
                        operand_lo(0, c)
                        if c in (0, 1, 4, 5):
                            i = (0, 1, None, None, 2, 3)[c]
                            dve.wait_ge(*((part_hi, i + 1) if i < 3 else (hi_ready, 1)))
                            dve.tensor_tensor(first_part(wl, i), first_part(raw, i),
                                              first_part(wh, i).bitcast(F32), ALU.subtract)\
                                .then_inc(part_lo if i < 3 else lo_ready, 1)
                    split_lo(2, 1, 2048)
                else:
                    for c in range(4, C):
                        operand_lo(2, c)
                mean_squares(2 * k)
                diagonals(2 * k)
                if k:
                    mixer_lo(base + 1)
                dve.wait_ge(rbc_ready, 2 * k + 1)

                def glu_step(u, s, n, first=False):
                    e = GU * k + u
                    if not first:
                        dve.wait_ge(hid_ready, e)
                    dve.wait_ge(unit_done, UF * k + u + 1)
                    dve.tensor_tensor(halves(glu_g[:, :]), both(4 * s), halves(rbc[:, :]), ALU.mult)\
                        .then_inc(glu_g_ready, 1)
                    dve.tensor_tensor(halves(glu_u[:, :]), both(4 * s + 2), halves(rbc[:, :]), ALU.mult)\
                        .then_inc(glu_free, 1)
                    split_lo(base + u + 3, s, n)
                    dve.wait_ge(tanh_ready, e + 1)
                    dve.scalar_tensor_tensor(out=glu_g[:, :], in0=glu_t[:, :], scalar=1.0, in1=glu_g[:, :],
                                             op0=ALU.add, op1=ALU.mult).then_inc(glu_m_ready, 1)
                    dve.wait_ge(glu_free, e + 1)
                    dve.wait_ge(glu_m_ready, e + 1)
                    dve.tensor_tensor(hid[:, bass.ds(u * TOK, TOK)], glu_g[:, :], glu_u[:, :], ALU.mult)\
                        .then_inc(hid_ready, 1)

                def hidden_lo(pair, tile_pair, s):
                    dve.wait_ge(hh_ready, DN * k + pair + 1)
                    dve.tensor_tensor(hl[:, s, :], hid[:, bass.ds(tile_pair * 2 * TOK, 2 * TOK)],
                                      hh[:, s, :].bitcast(F32), ALU.subtract).then_inc(hl_ready, 1)

                glu_step(0, 0, 2048, first=(k == 0))
                glu_step(1, 1, 2048)
                with dve.Fori(1, GU // 2 - 1) as i:
                    for s in range(2):
                        glu_step(2 * i + s, s, 2048)
                for s in range(2):
                    glu_step(GU - 2 + s, s, 1024)
                    hidden_lo(s, s, s)

                def down_step(v, s, tile_pair):
                    split_lo(base + GU + v + 3, s, 1024)
                    hidden_lo(v + 2, tile_pair, s)

                def add_half(first_chunk, v):
                    dve.wait_ge(unit_done, UF * k + GU + v + 1)
                    for j in range(4):
                        add_residual(first_chunk + j, 2 * j, 0.25)

                with dve.Fori(0, 4) as i:
                    for s in range(2):
                        down_step(2 * i + s, s, 2 * i + s + 2)
                down_step(8, 0, 10)
                down_step(9, 1, 0)
                add_half(0, 10)
                down_step(10, 0, 1)
                if k == 0:
                    for c in range(4):
                        operand_lo(1, c)
                down_step(11, 1, 2)
                with dve.Fori(0, 4) as i:
                    for s in range(2):
                        down_step(2 * i + 12 + s, s, 2 * i + s + 3)
                if k == 0:
                    mixer_lo(U_TOK)
                add_half(4, 21)
                if k == 0:
                    mixer_lo(U_TOK + 1)

            def rotate(z, n, ready):
                x1, x2 = z[:, :, :, 0:ROT], z[:, :, :, ROT:2 * ROT]
                cos = cos_t.unsqueeze(2).broadcast_to([P, TT, n, ROT])
                sin = sin_t.unsqueeze(2).broadcast_to([P, TT, n, ROT])
                a, b, c, d = [r[:, 0:TT * n * ROT].rearrange("p (t n r) -> p t n r", t=TT, n=n) for r in rot]
                dve.tensor_tensor(a, x1, cos, ALU.mult)
                dve.tensor_tensor(b, x2, sin, ALU.mult)
                dve.tensor_tensor(c, x1, sin, ALU.mult)
                link(dve.tensor_tensor(d, x2, cos, ALU.mult))
                dve.tensor_tensor(x1, a, b, ALU.subtract)
                ins = dve.tensor_tensor(x2, c, d, ALU.add)
                if ready is None:
                    link(ins)
                else:
                    ins.then_inc(ready, 1)

            def head_squares(z, n, at, ss_ready, pieces):
                for t0, tn in pieces:
                    s = sq[:, 0:tn * n * HD].rearrange("p (t n d) -> p t n d", t=tn, n=n)
                    link(dve.tensor_tensor(s, z[:, t0:t0 + tn], z[:, t0:t0 + tn], ALU.mult))
                    ss = head_ss[:, at + t0 * n:at + (t0 + tn) * n]
                    link(dve.tensor_reduce(ss.rearrange("p (t n) -> p t n", t=tn), s, AX.X, ALU.add))
                ss = head_ss[:, at:at + TT * n]
                dve.tensor_scalar(ss, ss, 1.0 / HD, EPS, ALU.mult, ALU.add).then_inc(ss_ready, 1)

            def head_scale(z, n, at, g, rs_count):
                dve.wait_ge(head_rs_ready, rs_count)
                rs = head_rs[:, at:at + TT * n].rearrange("p (t n) -> p t n", t=TT).unsqueeze(3)
                link(dve.tensor_tensor(z, z, rs.broadcast_to([P, TT, n, HD]), ALU.mult))
                link(dve.tensor_tensor(z, z, g.unsqueeze(1).unsqueeze(1).broadcast_to([P, TT, n, HD]), ALU.mult))

            relus = [0]

            def add_head(t, h):
                n = relus[0]
                relus[0] += 1
                wait_bank_read(dve, ("dot", t, h))
                r, w, s = rp[:, n % 2, 0:width[t]], zwi[:, t, h:h + 1], scores[t]
                if h == 0:
                    ins = dve.tensor_scalar(s, r, w, None, ALU.mult)
                else:
                    dve.wait_ge(relu_used, n)
                    ins = dve.scalar_tensor_tensor(out=s, in0=r, scalar=w, in1=s, op0=ALU.mult, op1=ALU.add)
                ins.then_inc(relu_used, 1)

            def close_scores(t):
                link(dve.memset(scores[t][0:64, width[t] - 64:width[t]], NEVER))

            def top_rounds(t, n):
                for _ in range(n):
                    link(dve.max(top8[:, :], scores[t]))
                    link(dve.match_replace(scores[t], top8[:, :], scores[t], TAKEN))

            def mask_of(t):
                dve.tensor_scalar(masks[t], scores[t][:, 0:width[t]], TAKEN, OFF, ALU.is_gt, ALU.mult)\
                    .then_inc(mask_ready, 1)

            def proj_out(b):
                dve.wait_ge(proj_job, b + 1)
                src = both(2 * (b % 2))
                if b >= NPROJ:
                    c = (b - NPROJ) % NOUT
                    dve.scalar_tensor_tensor(out=halves(x[:, c, :]), in0=src, scalar=1.0,
                                             in1=halves(x[:, c, :]), op0=ALU.mult, op1=ALU.add)\
                        .then_inc(proj_evac, 1)
                    return
                i, part = b // 3, b % 3
                if part == 0:
                    dve.tensor_tensor(halves(conv_g[:, :]), src, halves(rbc[:, :]), ALU.mult)\
                        .then_inc(proj_evac, 1)
                elif part == 1:
                    if i:
                        dve.wait_ge(conv_done, i)
                    dve.wait_ge(proj_evac, b)
                    dve.tensor_tensor(halves(conv_v[:, :]), src, halves(conv_g[:, :]), ALU.mult)\
                        .then_inc(proj_evac, 1)
                else:
                    dve.tensor_tensor(halves(conv_b[:, :]), src, halves(rbc[:, :]), ALU.mult)\
                        .then_inc(proj_evac, 1)

            def conv_lo(i):
                dve.wait_ge(cvh_ready, i + 1)
                dve.tensor_tensor(xl[:, i, :], conv_o[:, i, :], xh[:, i, :].bitcast(F32), ALU.subtract)\
                    .then_inc(cvl_ready, 1)

            def neg_max(n):
                t, m = ITEMS[n]
                job = ("logit", n)
                wait_bank_full(dve, job)
                dve.tensor_reduce(stat[:, n:n + 1], ps[:, bank(job), 0:width[t]], AX.X, ALU.max, negate=True)\
                    .then_inc(max_ready, 1)

            def normalise(n):
                t, m = ITEMS[n]
                job = ("logit", n)
                wait_bank_read(dve, job)
                link(dve.reciprocal(stat[:, 80 + n:81 + n], stat[:, 40 + n:41 + n]))
                dve.tensor_scalar(rp[:, n % 2, 0:width[t]], rp[:, n % 2, 0:width[t]], stat[:, 80 + n:81 + n],
                                  None, ALU.mult).then_inc(p_ready, 1)

            ffn(0)

            for c in range(4, C):
                operand_lo(1, c)
            mean_squares(1)
            diagonals(1)
            mixer_lo(U_TOK + 2)
            mixer_lo(U_TOK + 3)
            link(dve.tensor_scalar(gn[:, 0, :], gn[:, 0, :], HD ** -0.5, None, ALU.mult))
            dve.wait_ge(tok_evac, 5)
            dve.wait_ge(bcast_done, 2)
            link(dve.tensor_scalar(zwi[:, :, :], zwi[:, :, :], 8 ** -0.5 * HD ** -0.5, None, ALU.mult))
            dve.tensor_tensor(wfold[:, :].rearrange("p (r j t) -> p r j t", r=2, j=4),
                              zwi[:, 4, :].rearrange("p (j r) -> p r j", r=2).unsqueeze(3)
                              .broadcast_to([P, 2, 4, NT]),
                              same_t.unsqueeze(1).unsqueeze(1).broadcast_to([P, 2, 4, NT]), ALU.mult)\
                .then_inc(wfold_ready, 1)
            ki4 = zki[:, :, 0:HD].unsqueeze(2)
            head_squares(ki4, 1, 0, ki_ss_ready, [(0, 5)])
            head_scale(ki4, 1, 0, gn[:, 2, :], 1)
            rotate(ki4, 1, None)
            dve.tensor_copy(zki[:, :, HD:P], zki[:, :, 0:HD]).then_inc(ki_ready, 1)
            dve.wait_ge(tok_evac, 15)
            heads8 = zq[:, :, :].rearrange("p t (n d) -> p t n d", n=8)
            rotate(heads8, 8, qi_ready)
            mixer_lo(U_TOK + 4)
            mixer_lo(U_TOK + 5)
            wait_bank_full(dve, "wcol")
            dve.tensor_copy(wcols[:, :], ps[:, 6, 0:NB]).then_inc(bank_free[6], 1)
            for h in range(8):
                add_head(3, h)
            for h in range(8):
                add_head(2, h)
            dve.wait_ge(relu_used, 16)
            close_scores(3)
            close_scores(2)
            top_rounds(3, 8)
            mixer_lo(U_CONV)
            top_rounds(3, 6)
            dve.wait_ge(tok_evac, NJ)
            k4 = zkv[:, :, 0:P].rearrange("p t (n d) -> p t n d", n=2)
            head_squares(k4, 2, TT, k_ss_ready, [(0, 5)])
            head_squares(heads8, 8, 3 * TT, q_ss_ready, [(t, 1) for t in range(TT)])

            def weigh_sample(b):
                job = ("dot", 4, b)
                wait_bank_full(dve, job)
                if b == 0:
                    wait_bank_read(dve, "wcol")
                else:
                    if b >= 2:
                        dve.wait_ge(dec_relu_used, b - 1)
                dve.tensor_scalar(rp[:, b % 2, 0:SD], ps[:, bank(job), 0:SD], 0.0, wcols[:, b:b + 1],
                                  ALU.max, ALU.mult).then_inc(bank_free[bank(job)], 1)

            for b in range(NB):
                weigh_sample(b)
                if b == 0:
                    proj_out(0)
                elif b == 1:
                    top_rounds(3, 2)
                    mask_of(3)
                elif b == 3:
                    mixer_lo(U_CONV + 1)
                elif b == 5:
                    head_scale(k4, 2, TT, gn[:, 1, :], 2)
                elif b == 6:
                    rotate(k4, 2, k_ready)
            wait_bank_full(dve, "decsum")
            dve.wait_ge(score_fill, 1)
            dve.tensor_copy(scores[4][:, 0:PAST], ps[:, 7, 0:PAST])
            dve.tensor_tensor(scores[4][:, PAST:SD], ps[:, 7, PAST:SD], other_b, ALU.add)\
                .then_inc(bank_free[7], 1)
            for h in range(8):
                add_head(1, h)
            dve.wait_ge(relu_used, 24)
            close_scores(1)
            proj_out(1)
            mixer_lo(U_CONV + 2)
            dve.wait_ge(k_ready, 1)
            head_scale(heads8, 8, 3 * TT, gn[:, 0, :], 3)
            proj_out(2)
            rotate(heads8, 8, q_ready)
            top_rounds(4, 1)
            proj_out(3)
            mixer_lo(U_CONV + 3)
            top_rounds(4, 3)
            proj_out(4)
            top_rounds(4, 5)
            mask_of(4)
            proj_out(5)
            mixer_lo(U_CONV + 4)
            top_rounds(2, 3)
            proj_out(6)
            top_rounds(2, 5)
            proj_out(7)
            mixer_lo(U_CONV + 5)
            neg_max(0)
            neg_max(1)
            normalise(0)
            for n in range(len(ITEMS)):
                if n + 1 < len(ITEMS):
                    normalise(n + 1)
                if n + 2 < len(ITEMS):
                    neg_max(n + 2)
                if n < 8:
                    top_rounds(2, 1)
                    if n == 7:
                        mask_of(2)
                if 6 <= n < 22:
                    top_rounds(1, 1)
                    if n == 21:
                        mask_of(1)
                for b in range(jobs_by(n - 1), jobs_by(n)):
                    proj_out(b)
                if n in OUT_SPLITS:
                    mixer_lo(OUT_SPLITS[n])
                if n in CONV_SPLITS:
                    conv_lo(CONV_SPLITS[n])
                if n % 8 == 7:
                    t = ATT_TILES[n // 8]
                    dve.wait_ge(att_h_ready, n // 8 + 1)
                    dve.tensor_tensor(attended(xl, t), pv_bank(t), attended(xh, t).bitcast(F32),
                                      ALU.subtract).then_inc(bank_free[7], 1)
            for b in range(NPROJ + NOUT, NPROJ + 2 * NOUT):
                proj_out(b)
                if b == NPROJ + NOUT + 3:
                    mixer_lo(U_FFN2)
                if b >= NPROJ + NOUT + 4:
                    operand_lo(2, b - (NPROJ + NOUT + 4))
            ffn(1)

        @block.gpsimd
        def _(pool):
            chained = [0]

            def link(ins):
                chained[0] += 1
                ins.then_inc(pchain, 1)
                pool.wait_ge(pchain, chained[0])

            def root(out, in_):
                return pool.tensor_tensor(out, in_, half_pow[:, 0:in_.shape[1]], ALU.pow)

            def add_squares(stage, c):
                pool.wait_ge(sq_ready, C * stage + c + 1)
                if (C - 1) * stage + c - 1:
                    pool.wait_ge(sq_added, (C - 1) * stage + c - 1)
                pool.tensor_tensor(sqacc[:, :], sqacc[:, :], (sq, sq_odd)[c % 2][:, :], ALU.add)\
                    .then_inc(sq_added, 1)

            def norm_factors(stage):
                for c in range(1, C):
                    add_squares(stage, c)
                pool.wait_ge(var_ready, stage + 1)
                root(rstd[:, :], var[:, :]).then_inc(rstd_ready, 1)

            pool.memset(ones[:, :], 1.0).then_inc(ones_set, 1)
            pool.memset(half_pow[:, :], -0.5).then_inc(ones_set, 1)
            pool.memset(cstate[:, :, :, :], 0.0).then_inc(ones_set, 1)
            pool.wait_ge(ones_set, 3)
            norm_factors(0)
            norm_factors(1)
            pool.wait_ge(res_added, C)
            pool.memset(scores[4][:, SD:SD + PAD], -NEVER).then_inc(score_fill, 1)
            link(pool.memset(conv_u[:, 0:2], 0.0))
            link(pool.memset(masks[0], 0.0))
            pool.memset(masks[0][0:64, 64:128], OFF).then_inc(mask0_ready, 1)
            for at, n, ready in ((0, TT, ki_ss_ready), (TT, 2 * TT, k_ss_ready), (3 * TT, 8 * TT, q_ss_ready)):
                pool.wait_ge(ready, 1)
                root(head_rs[:, at:at + n], head_ss[:, at:at + n]).then_inc(head_rs_ready, 1)

            u_samples = conv_u[:, 2 + SEQ:].rearrange("p (b t) -> p b t", b=NB)
            samples = lambda ap: ap.rearrange("p (b t) -> p b t", b=NB)

            def conv(i):
                link(pool.tensor_copy(u_samples[:, :, 0:2], cpast[:, i, :, :]))
                pool.wait_ge(proj_evac, 3 * i + 2)
                pool.tensor_tensor(conv_u[:, 2:2 + SEQ], conv_v[:, 0:SEQ], rbc[:, 0:SEQ], ALU.mult)
                link(pool.tensor_tensor(u_samples[:, :, 2:], samples(conv_v[:, SEQ:TOK]),
                                        samples(rbc[:, SEQ:TOK]), ALU.mult))
                pool.tensor_copy(cstate[:, i, 0, :], conv_u[:, SEQ:SEQ + 2])
                pool.tensor_copy(cstate[:, i, 1:, :], u_samples[:, :, NT:])
                for j in range(3):
                    dst = conv_o[:, i, :] if j == 0 else conv_v[:, :]
                    pool.tensor_scalar(dst[:, 0:SEQ], conv_u[:, j:j + SEQ], conv_w(i, j), 1.0, ALU.mult,
                                       ALU.mult)
                    link(pool.tensor_scalar(samples(dst[:, SEQ:TOK]), u_samples[:, :, j:j + NT],
                                            conv_w(i, j), 1.0, ALU.mult, ALU.mult))
                    if j:
                        link(pool.tensor_tensor(conv_o[:, i, :], conv_o[:, i, :], conv_v[:, :], ALU.add))
                pool.wait_ge(proj_evac, 3 * i + 3)
                pool.tensor_tensor(conv_o[:, i, :], conv_o[:, i, :], conv_b[:, :], ALU.mult)\
                    .then_inc(conv_done, 1)

            for i in range(4):
                conv(i)
            norm_factors(2)


def rotation_tables():
    pos = np.concatenate([np.arange(SEQ), PAST + np.arange(NB * NT) % NT]).astype(np.float32)
    inv = np.float32(500000.0) ** (-np.arange(ROT, dtype=np.float32) * np.float32(2.0 / (2 * ROT)))
    ang = pos[:, None] * inv[None, :].astype(np.float32)
    lay = lambda a: a.astype(np.float32).reshape(TT, P, ROT).transpose(1, 0, 2).reshape(P, TT * ROT)
    return lay(np.cos(ang)), lay(np.sin(ang))


def tables():
    p = np.arange(P)
    cos, sin = rotation_tables()
    same_t = (p[:, None] % NT == np.arange(NT)[None, :]).astype(np.float32)
    spread = np.zeros((P, 240), np.float32)
    spread[:, 112:128] = same_t
    same_b = (p[:, None] // NT == np.arange(NB)[None, :]).astype(np.float32)
    other = np.where(p[:, None] // NT == p[None, :] // NT, 0.0, OFF).astype(np.float32)
    return np.concatenate([np.eye(P, dtype=np.float32), cos, sin, same_t, spread, same_b, other], axis=1)


def bf_tables():
    p = np.arange(P)
    expand = (p[:, None, None] // NT == np.arange(NB)[None, :, None]) & (
        p[:, None, None] % NT == p[None, None, :] % NT)
    return np.concatenate([expand, np.eye(P, dtype=bool)[:, None, :]], axis=1).astype(mybir.dt.np(BF16))


def lay_out(i):
    a = {k: np.asarray(v) for k, v in i.items()}
    x_all = np.concatenate([a["x_prompt"].reshape(SEQ, D), a["x_sample"].reshape(NB * NT, D)])

    def gate_up(g, u):
        both = np.stack([g[0], u[0]]).reshape(2, C, P, NF, P)
        return both.transpose(3, 2, 0, 1, 4).reshape(NF, P, 2 * C * P)

    def down(w):
        return w[0].reshape(NF // 2, 2, P, 2, 4, P).transpose(3, 0, 2, 1, 4, 5).reshape(DN, P, 8 * P)

    w_in = a["w_in"][0]
    gb, gc, xv = (w_in[:, 512 * n:512 * (n + 1)] for n in range(3))
    q = w_in[:, 1536:2048].reshape(D, 2, NG, HD).transpose(0, 2, 1, 3).reshape(D, 512)
    tok = np.concatenate([w_in[:, 2816:2888], w_in[:, 2304:2816], w_in[:, 2048:2304], q], axis=1)
    starts = np.cumsum((0,) + TOK_N)
    filled = lambda w: np.concatenate([w, np.zeros((P, 2048 - w.shape[1]), w.dtype)], axis=1)
    cols = lambda w: w.reshape(C, P, -1).transpose(1, 0, 2).reshape(P, -1)
    tiles = [w[:, P * n:P * (n + 1)] for n in range(4) for w in (gc, xv, gb)]
    w_out = a["w_out"][0]
    att = w_out[512:].reshape(2, NG, HD, D).transpose(1, 0, 2, 3).reshape(512, D)
    w_o = np.stack([w_out[:512], att]).reshape(2, 4, P, 2, 4, P).transpose(0, 3, 2, 1, 4, 5)
    norms = np.concatenate([a[n].reshape(C, P).T for n in ("ffn1_norm", "mix_norm", "ffn2_norm")], axis=1)
    conv_w = a["conv_w"][0].reshape(3, 4, P).transpose(2, 1, 0).reshape(P, 12)
    gains = np.stack([a["q_norm"][0], a["k_norm"][0], a["idx_k_norm"][0]])
    return {
        "xt": x_all.reshape(TOK, C, P).transpose(2, 1, 0),
        "gu1": gate_up(a["ffn1_w_gate"], a["ffn1_w_up"]), "dn1": down(a["ffn1_w_down"]),
        "gu2": gate_up(a["ffn2_w_gate"], a["ffn2_w_up"]), "dn2": down(a["ffn2_w_down"]),
        "wtok": np.stack([filled(cols(tok[:, s:s + n])) for s, n in zip(starts, TOK_N)]),
        "wconv": np.stack([np.concatenate([cols(tiles[2 * n]), cols(tiles[2 * n + 1])], axis=1)
                           for n in range(6)]),
        "wout": w_o.reshape(4, P, 16 * P),
        "small": np.concatenate([norms, conv_w], axis=1),
        "gains": np.broadcast_to(gains[None], (P, 3, HD)),
        "kcache": a["cache_k"][0].transpose(2, 3, 0, 1).reshape(P, NB, PAST),
        "vcache": a["cache_v"][0].reshape(NB, 2, P, P).transpose(2, 0, 1, 3),
        "ikcache": a["cache_idx_k"][0].transpose(2, 0, 1),
        "conv_past": a["state_conv"][0].reshape(NB, 2, 4, P).transpose(3, 2, 0, 1),
        "tables": tables(), "bf_tables": bf_tables(),
    }


OUTS = {"y_out": (P, C, TOK), "k_out": (P, TT, P), "v_out": (P, TT, P), "ik_out": (P, TT, HD),
        "conv_out": (P, 4, NB + 1, 2)}


def build(nc, arrays):
    args = {n: nc.dram_tensor(n, v.shape, mybir.dt.from_np(v.dtype), kind="ExternalInput").ap()
            for n, v in arrays.items()}
    args |= {n: nc.dram_tensor(n, s, F32, kind="ExternalOutput").ap() for n, s in OUTS.items()}
    trunk(nc, **args)
    return nc


def kernel(**inputs):
    import concourse.bacc as bacc
    from concourse.bass_utils import run_bass_kernel_spmd

    arrays = {n: np.ascontiguousarray(v) for n, v in lay_out(inputs).items()}
    nc = build(bacc.Bacc("TRN2", target_bir_lowering=False, num_devices=1), arrays)
    r = run_bass_kernel_spmd(nc, [arrays], core_ids=[0]).results[0]
    y = r["y_out"].transpose(2, 1, 0).reshape(TOK, D)
    rows = lambda a: a.transpose(1, 0, 2).reshape(TOK, -1)
    k, v, ik = rows(r["k_out"]), rows(r["v_out"]), rows(r["ik_out"])
    state = r["conv_out"].transpose(2, 3, 1, 0).reshape(NB + 1, 2, 512)
    return (y[:SEQ].reshape(1, SEQ, D), y[SEQ:].reshape(NB, NT, D),
            k[:SEQ].reshape(1, 1, SEQ, 2, HD), v[:SEQ].reshape(1, 1, SEQ, 2, HD),
            ik[:SEQ].reshape(1, 1, SEQ, HD), state[:1].reshape(1, 1, 2, 512),
            k[SEQ:].reshape(1, NB, NT, 2, HD), v[SEQ:].reshape(1, NB, NT, 2, HD),
            ik[SEQ:].reshape(1, NB, NT, HD), state[1:].reshape(1, NB, 2, 512))
```

```python
from contextlib import ExitStack

import numpy as np

import concourse.bass as bass
from concourse import mybir

F32 = mybir.dt.float32
F32R = mybir.dt.float32r
BF16 = mybir.dt.bfloat16
ALU = mybir.AluOpType
ACT = mybir.ActivationFunctionType
AX = mybir.AxisListType

P = 128
D = 1024
C = D // P
F = 2816
NF = F // P
SEQ, NB, NT, PAST = 512, 8, 16, 256
TOK = SEQ + NB * NT
TT = TOK // P
HALF = TOK // 2
HD = 64
NG = 4
ROT = 8
KP = 128
KD = 68
PAD = 4
EPS = 1e-6
SD = PAST + P
TAKEN = -3.4e38
NEVER = -3.0e38
OFF = -1.0e30
GU, DN = NF, NF
UF = GU + DN
U_TOK, U_CONV, U_OUT, U_FFN2 = UF, UF + 6, UF + 12, UF + 16
TOK_N = (420, 420, 512)
NJ = TT * len(TOK_N)
TOK_BANKS = (0, 1, 2, 3, 4, 5, 0, 1, 2, 3, 7, 0, 1, 2, 3)
X_PARTS = ((0, 1), (1, 2), (2, 4), (4, 6), (6, 8))
WARM_UP = 16
NPROJ, NOUT = 12, 8


def trunk(nc, xt, gu1, dn1, gu2, dn2, wtok, wconv, wout, small, gains, kcache, vcache, ikcache,
          conv_past, tables, bf_tables, y_out, k_out, v_out, ik_out, conv_out):
    with ExitStack() as ctx:
        def sb(name, shape, dt=F32):
            return ctx.enter_context(nc.sbuf_tensor(name, shape, dt))

        def sem(name):
            return ctx.enter_context(nc.semaphore(name))

        ps = ctx.enter_context(nc.psum_tensor("ps", [P, 8, 512], F32))
        x = sb("x", [P, C, TOK])
        xh = sb("xh", [P, C, TOK], F32R)
        xl = sb("xl", [P, C, TOK], F32R)
        raw = sb("raw", [P, 2, 2048])
        wh = sb("wh", [P, 2, 2048], F32R)
        wl = sb("wl", [P, 2, 2048], F32R)
        rbc = sb("rbc", [P, TOK])
        sqacc = sb("sqacc", [P, TOK])
        sq = sb("sq", [P, TOK])
        ones = sb("ones", [P, P])
        half_pow = sb("half_pow", [P, 40])
        var = sb("var", [P, TT])
        rstd = sb("rstd", [P, TT])
        sm = sb("sm", [P, 36])
        gn = sb("gn", [P, 3, HD])
        tab = sb("tab", [P, 128 + 40 + 40 + 16 + 240 + 8 + 128])
        bft = sb("bft", [P, 9, P], BF16)
        cpast = sb("cpast", [P, 4, NB, 2])
        cstate = sb("cstate", [P, 4, NB + 1, 2])
        ident = tab[:, 0:128]
        cos_t = tab[:, 128:168].rearrange("p (t r) -> p t r", t=TT)
        sin_t = tab[:, 168:208].rearrange("p (t r) -> p t r", t=TT)
        same_t = tab[:, 208:224]
        spread = tab[:, 224:464]
        same_b = tab[:, 464:472]
        other_b = tab[:, 472:600]
        ident_bf = bft[:, 8, :]
        gain = lambda s, c: sm[:, 8 * s + c:8 * s + c + 1]
        conv_w = lambda i, j: sm[:, 24 + 3 * i + j:25 + 3 * i + j]

        with ExitStack() as ffn_scope:
            fs = lambda name, shape, dt=F32: ffn_scope.enter_context(nc.sbuf_tensor(name, shape, dt))
            hid = fs("hid", [P, NF * TOK])
            glu_g = fs("glu_g", [P, TOK])
            glu_t = fs("glu_t", [P, TOK])
            glu_u = fs("glu_u", [P, TOK])
            hh = fs("hh", [P, 2, 2 * TOK], F32R)
            hl = fs("hl", [P, 2, 2 * TOK], F32R)
        sq_odd = glu_u
        zq = sb("zq", [P, TT, 512])
        zkv = sb("zkv", [P, TT, 256])
        zki = sb("zki", [P, TT, P])
        zwi = sb("zwi", [P, TT, 8])
        qit_k = sb("qit_k", [P, 4 * TOK])
        q_all = sb("q_all", [P, NG * TOK])
        kt = sb("kt", [P, TOK])
        kit = sb("kit", [P, TOK])
        ikc_v = sb("ikc_v", [P, 2048])
        score = sb("score", [P, 256 + 384 + 512 + SD + PAD])
        mask = sb("mask", [P, 128 + 256 + 384 + 512 + SD], BF16)
        rp = sb("rp", [P, 2, 512])
        conv_g = sb("conv_g", [P, TOK])
        conv_v = sb("conv_v", [P, TOK])
        conv_b = sb("conv_b", [P, TOK])
        conv_u = sb("conv_u", [P, 2 + SEQ + NB * (NT + 2)])
        conv_o = sb("conv_o", [P, 4, TOK])
        stat = sb("stat", [P, 3 * 40])
        head_ss = sb("head_ss", [P, 55])
        head_rs = sb("head_rs", [P, 55])
        wcols = sb("wcols", [P, NB])
        wfold = sb("wfold", [P, P])
        top8 = sb("top8", [P, 8])

        qit = qit_k[:, 0:4 * SEQ].rearrange("p (j t) -> p j t", j=4)
        qit_s = qit_k[:, 4 * SEQ:].rearrange("p (b j t) -> p j b t", b=NB, j=4)
        qt = q_all[:, 0:4 * SEQ].rearrange("p (j t) -> p j t", j=4)
        qt_s = q_all[:, 4 * SEQ:].rearrange("p (b j t) -> p j b t", b=NB, j=4)
        kct = qit_k[:, 0:2048].rearrange("p (b s) -> p b s", b=NB)
        ikct = ikc_v[:, :].rearrange("p (b s) -> p b s", b=NB)
        vc = ikc_v[:, :].rearrange("p (b k d) -> p b k d", b=NB, k=2)
        wt = zq[:, :, :].rearrange("p t n -> p (t n)")[:, 0:1024].rearrange("p (s n) -> p s n", s=2)
        rot = [(sqacc if n < 2 else sq)[:, 320 * (n % 2):320 * (n % 2) + 320] for n in range(4)]
        score_at = {1: 0, 2: 256, 3: 640, 4: 1152}
        width = {0: 128, 1: 256, 2: 384, 3: 512, 4: SD}
        scores = {t: score[:, a:a + width[t] + (PAD if t == 4 else 0)] for t, a in score_at.items()}
        mask_at = {0: 0, 1: 128, 2: 384, 3: 768, 4: 1280}
        masks = {t: mask[:, a:a + width[t]] for t, a in mask_at.items()}

        x_in = [sem(f"x_in{i}") for i in range(len(X_PARTS))]
        consts_in = sem("consts_in")
        ones_set = sem("ones_set")
        small_in = sem("small_in")
        raw_in = [sem("raw_in0"), sem("raw_in1")]
        part_in = [sem(f"part_in{i}") for i in range(4)]
        part_hi = sem("part_hi")
        quarter_lo = sem("quarter_lo")
        part_lo = sem("part_lo")
        quarter_hi = sem("quarter_hi")
        hi_ready = sem("hi_ready")
        lo_ready = sem("lo_ready")
        unit_done = sem("unit_done")
        down_done = sem("down_done")
        xh_ready = sem("xh_ready")
        xl_ready = sem("xl_ready")
        sq_ready = sem("sq_ready")
        sq_added = sem("sq_added")
        colsum_done = sem("colsum_done")
        var_ready = sem("var_ready")
        rstd_ready = sem("rstd_ready")
        diag_ready = sem("diag_ready")
        bcast_done = sem("bcast_done")
        rbc_ready = sem("rbc_ready")
        glu_g_ready = sem("glu_g_ready")
        glu_free = sem("glu_free")
        tanh_ready = sem("tanh_ready")
        glu_m_ready = sem("glu_m_ready")
        hid_ready = sem("hid_ready")
        hh_ready = sem("hh_ready")
        hl_ready = sem("hl_ready")
        res_added = sem("res_added")
        tok_job = sem("tok_job")
        tok_evac = sem("tok_evac")
        proj_job = sem("proj_job")
        proj_evac = sem("proj_evac")
        bank_full = {b: sem(f"bank{b}_full") for b in range(4, 8)}
        bank_free = {b: sem(f"bank{b}_free") for b in range(4, 8)}
        ikc_in = sem("ikc_in")
        kc_in = sem("kc_in")
        vc_in = sem("vc_in")
        dchain = sem("vector_chain")
        pchain = sem("gpsimd_chain")
        ki_ss_ready = sem("ki_ss_ready")
        k_ss_ready = sem("k_ss_ready")
        q_ss_ready = sem("q_ss_ready")
        head_rs_ready = sem("head_rs_ready")
        ki_ready = sem("ki_ready")
        qi_ready = sem("qi_ready")
        k_ready = sem("k_ready")
        q_ready = sem("q_ready")
        wfold_ready = sem("wfold_ready")
        relu_used = sem("relu_used")
        dec_relu_used = sem("dec_relu_used")
        score_fill = sem("score_fill")
        mask0_ready = sem("mask0_ready")
        mask_ready = sem("mask_ready")
        conv_done = sem("conv_done")
        cvh_ready = sem("cvh_ready")
        cvl_ready = sem("cvl_ready")
        max_ready = sem("max_ready")
        p_ready = sem("p_ready")
        pv_done = sem("pv_done")
        att_h_ready = sem("att_h_ready")
        kv_stored = sem("kv_stored")
        y_stored = sem("y_stored")

        bank_use, uses = {}, {b: 0 for b in range(4, 8)}

        def place(job, bank):
            bank_use[job] = (bank, uses[bank])
            uses[bank] += 1

        DOT_TILES = (3, 2)
        ATT_TILES = (3, 4, 2, 1, 0)
        ITEMS = [(t, n) for t in ATT_TILES for n in range(8)]
        for n, job in enumerate(["tki0", "tki1", "tqi0", "tqi1", "tqi2", "tqi3", "tqi4"]):
            place(job, 4 + n % 2)
        place("wcol", 6)
        for n, (t, h) in enumerate([(t, h) for t in DOT_TILES for h in range(8)]):
            place(("dot", t, h), 4 + n % 3)
        for b in range(NB):
            place(("dot", 4, b), 4 + b % 3)
        place("decsum", 7)
        for h in range(8):
            place(("dot", 1, h), 4 + h % 3)
        for n, job in enumerate(["tk0", "tk1", "tq0", "tq1", "tq2", "tq3", "tq4"]):
            place(job, 4 + n % 2)
        for n, item in enumerate(ITEMS):
            place(("logit", n), 4 + n % 2)
            place(("turn", n), 6)
            if item[1] == 7:
                place(("pv", item[0]), 7)

        def parts_by(n):
            if n < 10:
                return min(4 * (n + 1), 32)
            return 32 + (28 * (n - 9) + 29) // 30

        def jobs_by(n):
            parts = parts_by(n)
            return 8 + parts // 8 if parts <= 32 else 12 + (parts - 32) // 4

        def item_of(job):
            return next(n for n in range(len(ITEMS)) if jobs_by(n) > job)

        PROJ_SPLITS = {0: U_CONV + 5, item_of(9): U_OUT}
        QUARTERS = {14 + q: (U_OUT + 1, q) for q in range(4)}
        QUARTERS |= {item_of(15) + q: (U_OUT + 2, q) for q in range(4)}
        ROUNDS = {4: {0: 1, 1: 2, 2: 2, 3: 1, 4: 2, 5: 1},
                  2: {5: 1, 6: 2, 7: 1, 10: 1, 11: 1, 12: 1, 13: 1},
                  1: {n: 1 for n in (0, 1, 2, 3, 4, 5, 6, 7, 14, 15, 16, 17, 18, 19, 20, 21)}}
        CONV_SPLITS = {8: (0, 1), 9: (2, 3)}

        def x_part(c):
            return next(i for i, (a, b) in enumerate(X_PARTS) if a <= c < b)

        def load_x(eng, i):
            a, b = X_PARTS[i]
            eng.dma_start(x[:, a:b, :], xt[:, a:b, :]).then_inc(x_in[i], 16)

        def part_cols(i):
            a = 1024 * (i % 2) + 512 * (i // 2)
            return slice(a, a + 512)

        def quarter(buf, U, q):
            return buf[:, U % 2, 512 * q:512 * (q + 1)]

        def first_part(buf, i):
            return buf[:, 0, part_cols(i)]

        def wait_bank_free(eng, job):
            b, k = bank_use[job]
            if k:
                eng.wait_ge(bank_free[b], k)

        def wait_bank_full(eng, job):
            b, k = bank_use[job]
            eng.wait_ge(bank_full[b], k + 1)

        def wait_bank_read(eng, job):
            b, k = bank_use[job]
            eng.wait_ge(bank_free[b], k + 1)

        def bank(job):
            return bank_use[job][0]

        def wait_unit_used(eng, U):
            if U < U_TOK:
                eng.wait_ge(unit_done, U + 1)
            elif U < U_CONV:
                eng.wait_ge(tok_job, 5 * (U - U_TOK) + 5)
            elif U < U_OUT:
                eng.wait_ge(proj_job, 2 * (U - U_CONV) + 2)
            else:
                eng.wait_ge(proj_job, NPROJ + 4 * (U - U_OUT) + 4)

        def pv_bank(t):
            if t == 4:
                return ps[:, 7, :].rearrange("p (b g t) -> p b g t", b=NB, g=NG)
            return ps[:, 7, :].rearrange("p (g t) -> p g t", g=NG)

        def attended(buf, t):
            if t == 4:
                return buf[:, 4:8, SEQ:TOK].rearrange("p g (b t) -> p b g t", b=NB)
            return buf[:, 4:8, t * P:(t + 1) * P]

        def unit_n(U):
            return 4 * TOK_N[(U - U_TOK) // 2] if U < U_CONV else 2048

        block = ctx.enter_context(nc.Block())

        @block.sync
        def _(sp):
            def load(U, slot, src, n, wait=True):
                if wait:
                    sp.wait_ge(lo_ready, U - 1)
                sp.dma_start(raw[:, slot, 0:n], src).then_inc(raw_in[slot], 16)

            def ffn(gu, dn, base):
                first = 0
                if base == 0:
                    for i in range(4):
                        sp.dma_start(first_part(raw, i), gu[0][:, part_cols(i)]).then_inc(part_in[i], 16)
                        if i:
                            load_x(sp, i + 1)
                    load(1, 1, gu[1], 2048, wait=False)
                    for dst, src in ((tab[:, :], tables), (gn[:, :, :], gains), (bft[:, :, :], bf_tables),
                                     (cpast[:, :, :, :], conv_past)):
                        sp.dma_start(dst, src).then_inc(consts_in, 16)
                    first = 1
                with sp.Fori(first, GU // 2) as i:
                    for s in range(2):
                        load(base + 2 * i + s, s, gu[2 * i + s], 2048)
                with sp.Fori(0, DN // 2) as i:
                    for s in range(2):
                        load(base + GU + 2 * i + s, s, dn[2 * i + s], 1024)

            ffn(gu1, dn1, 0)
            for n, U in enumerate(range(U_TOK, U_CONV)):
                load(U, U % 2, wtok[n, :, 0:unit_n(U)], unit_n(U))
            for n, U in enumerate(range(U_CONV, U_OUT)):
                load(U, U % 2, wconv[n], 2048)
            for n, U in enumerate(range(U_OUT, U_FFN2)):
                load(U, U % 2, wout[n], 2048)
            sp.wait_ge(k_ready, 1)
            sp.wait_ge(ki_ready, 1)
            sp.wait_ge(conv_done, 4)
            sp.wait_ge(tok_evac, NJ)
            sp.dma_start(k_out, zkv[:, :, 0:128]).then_inc(kv_stored, 16)
            sp.dma_start(v_out, zkv[:, :, 128:256]).then_inc(kv_stored, 16)
            sp.dma_start(ik_out, zki[:, :, 0:HD]).then_inc(kv_stored, 16)
            sp.dma_start(conv_out, cstate[:, :, :, :]).then_inc(kv_stored, 16)
            ffn(gu2, dn2, U_FFN2)
            for c in range(C):
                sp.wait_ge(res_added, C + c + 1)
                sp.dma_start(y_out[:, c, :], x[:, c, :]).then_inc(y_stored, 16)
            sp.wait_ge(kv_stored, 64)
            sp.wait_ge(y_stored, 16 * C)

        @block.tensor
        def _(pe):
            def three(out, ah, al, bh, bl, first, last):
                pe.matmul(out, ah, bh, start=first, stop=False)
                pe.matmul(out, ah, bl, start=False, stop=False)
                return pe.matmul(out, al, bh, start=False, stop=last)

            def token_halves(banks, ah, al, bh, bl, first, last):
                outs = [ps[:, b, 0:HALF] for b in banks]
                cols = [slice(0, HALF), slice(HALF, TOK)]
                for o, c in zip(outs, cols):
                    pe.matmul(o, ah, bh[:, c], start=first, stop=False)
                for o, c in zip(outs, cols):
                    pe.matmul(o, ah, bl[:, c], start=False, stop=False)
                for o, c in zip(outs, cols):
                    last_mm = pe.matmul(o, al, bh[:, c], start=False, stop=last)
                return last_mm

            def column_sums(stage):
                pe.wait_ge(sq_added, (C - 1) * (stage + 1))
                for t in range(TT):
                    mm = pe.matmul(ps[:, 7, t:t + 1], sqacc[:, t * P:(t + 1) * P], ones[:, 0:1],
                                   start=True, stop=True)
                mm.then_inc(colsum_done, 1)

            def broadcast_rstd(stage):
                pe.wait_ge(diag_ready, stage + 1)
                pe.matmul(ps[:, 6, :], ones[:, :], sq[:, 0:512], start=True, stop=True)
                pe.matmul(ps[:, 7, 0:P], ones[:, :], sq[:, 512:TOK], start=True, stop=True)\
                    .then_inc(bcast_done, 1)

            def weight(w, slot, i):
                return w[:, slot, i * P:(i + 1) * P]

            def glu_part(slot, m, c):
                b = 4 * slot + 2 * m
                return token_halves((b, b + 1), weight(wh, slot, 8 * m + c), weight(wl, slot, 8 * m + c),
                                    xh[:, c, :], xl[:, c, :], c == 0, c == C - 1)

            def glu_unit(slot):
                for m in range(2):
                    for c in range(C):
                        mm = glu_part(slot, m, c)
                mm.then_inc(unit_done, 1)

            def down_unit(slot, first, last, bank_waits=None):
                order = [(f, j) for f in range(2) for j in range(4)]
                if last:
                    order = [(f, j) for j in range(4) for f in range(2)]
                for f, j in order:
                    if first and f == 0:
                        pe.wait_ge(*bank_waits[j])
                    mm = token_halves((2 * j, 2 * j + 1), weight(wh, slot, 4 * f + j),
                                      weight(wl, slot, 4 * f + j),
                                      hh[:, slot, f * TOK:(f + 1) * TOK],
                                      hl[:, slot, f * TOK:(f + 1) * TOK],
                                      first and f == 0, last and f == 1)
                    if last and f == 1 and j < 3:
                        mm.then_inc(down_done, 1)
                mm.then_inc(unit_done, 1)

            def ffn(k):
                stage, base = 2 * k, U_FFN2 * k
                if k:
                    pe.wait_ge(lo_ready, base + 1)
                for part, (cs, m) in enumerate((cs, m) for cs in (range(0, 4), range(4, 8)) for m in range(2)):
                    if k == 0:
                        pe.wait_ge(*((part_lo, part + 1) if part < 3 else (lo_ready, 1)))
                    if k and cs[0] == 0:
                        pe.wait_ge(proj_evac, NPROJ + 2 * NOUT - 1 + m)
                    for c in cs:
                        if m == 0:
                            pe.wait_ge(xh_ready, C * stage + c + 1)
                            pe.wait_ge(xl_ready, C * stage + c + 1)
                        mm = glu_part(0, m, c)
                    if k and part == 2:
                        column_sums(stage)
                mm.then_inc(unit_done, 1)
                pe.wait_ge(lo_ready, base + 2)
                for c in range(C):
                    if k == 0 and c == 4:
                        column_sums(stage)
                    if c == (7, 4)[k]:
                        broadcast_rstd(stage)
                    glu_part(1, 0, c)
                pe.wait_ge(rbc_ready, stage + 1)
                for c in range(C):
                    mm = glu_part(1, 1, c)
                mm.then_inc(unit_done, 1)
                with pe.Fori(1, GU // 2) as i:
                    for s in range(2):
                        pe.wait_ge(lo_ready, base + 2 * i + s + 1)
                        pe.wait_ge(glu_free, GU * k + 2 * i + s - 1)
                        glu_unit(s)

                def down(v, first=False, last=False, slot=0, bank_waits=None):
                    pe.wait_ge(lo_ready, base + GU + v + 1)
                    pe.wait_ge(hl_ready, DN * k + v + 1)
                    down_unit(slot, first, last, bank_waits)

                down(0, first=True, slot=0, bank_waits=[(glu_free, GU * (k + 1) - (j < 2)) for j in range(4)])
                with pe.Fori(0, 4) as i:
                    down(2 * i + 1, slot=1)
                    down(2 * i + 2, slot=0)
                down(9, slot=1)
                down(10, last=True, slot=0)
                down(11, first=True, slot=1, bank_waits=[(res_added, C * k + j + 1) for j in range(4)])
                with pe.Fori(0, 4) as i:
                    down(2 * i + 12, slot=0)
                    down(2 * i + 13, slot=1)
                down(20, slot=0)
                down(21, last=True, slot=1)

            def tok_weight(w, U, i):
                n = TOK_N[(U - U_TOK) // 2]
                return w[:, U % 2, i * n:(i + 1) * n]

            def tok_half(g, half, t):
                U, J = U_TOK + 2 * g + half, TT * g + t
                for i in range(4):
                    c = 4 * half + i
                    mm = three(ps[:, TOK_BANKS[J], 0:TOK_N[g]], xh[:, c, t * P:(t + 1) * P],
                               xl[:, c, t * P:(t + 1) * P], tok_weight(wh, U, i), tok_weight(wl, U, i),
                               c == 0, c == C - 1)
                mm.then_inc(tok_job, 1)

            def tok_unit(g, half, tiles=range(TT)):
                pe.wait_ge(lo_ready, U_TOK + 2 * g + half + 1)
                for t in tiles:
                    bank_, J = TOK_BANKS[TT * g + t], TT * g + t
                    if half == 0 and bank_ in TOK_BANKS[:J]:
                        pe.wait_ge(tok_evac, J - TOK_BANKS[:J][::-1].index(bank_))
                    tok_half(g, half, t)

            def turn_token_tile(job, pieces):
                wait_bank_free(pe, job)
                for i, piece in enumerate(pieces):
                    mm = pe.transpose(ps[:, bank(job), i * P:(i + 1) * P], piece, ident)
                mm.then_inc(bank_full[bank(job)], 1)

            def dots(t, h):
                job = ("dot", t, h)
                j, r = h // 2, HD * (h % 2)
                wait_bank_free(pe, job)
                pe.matmul(ps[:, bank(job), 0:width[t]], qit[r:r + HD, j, t * P:(t + 1) * P],
                          kit[r:r + HD, 0:width[t]], start=True, stop=True)\
                    .then_inc(bank_full[bank(job)], 1)

            def dots_sample(b):
                job = ("dot", 4, b)
                wait_bank_free(pe, job)
                for r in (0, HD):
                    q = qit_k[r:r + HD, 4 * SEQ + b * HD:4 * SEQ + (b + 1) * HD]
                    pe.matmul(ps[r:r + HD, bank(job), 0:PAST], q, ikct[r:r + HD, b, :], start=True, stop=True)
                    mm = pe.matmul(ps[r:r + HD, bank(job), PAST:SD], q, kit[r:r + HD, SEQ:TOK],
                                   start=True, stop=True)
                mm.then_inc(bank_full[bank(job)], 1)

            def sum_heads(b):
                wait_bank_read(pe, ("dot", 4, b))
                if b == 0:
                    pe.wait_ge(tok_evac, NJ)
                mm = pe.matmul(ps[:, bank("decsum"), 0:SD], spread[:, 112 - NT * b:240 - NT * b],
                               rp[:, b % 2, 0:SD], start=(b == 0), stop=(b == NB - 1))
                mm.then_inc(dec_relu_used, 1)
                if b == NB - 1:
                    pe.matmul(ps[:, bank("decsum"), SD:SD + 1], ident, ones[:, 0:1], start=True, stop=True)\
                        .then_inc(bank_full[bank("decsum")], 1)

            def proj_part(b, c):
                U = U_CONV + b // 2 if b < NPROJ else U_OUT + (b - NPROJ) // 4
                if c == 0:
                    pe.wait_ge(lo_ready, U + 1)
                    if U in (U_OUT + 1, U_OUT + 2):
                        pe.wait_ge(quarter_lo, 3 * (U - U_OUT))
                    if b < 2:
                        pe.wait_ge(tok_evac, NJ - TOK_BANKS[::-1].index(2 * b + 1))
                    else:
                        pe.wait_ge(proj_evac, b - 1)
                banks = (2 * (b % 2), 2 * (b % 2) + 1)
                if b < NPROJ:
                    i, chunk, last = 8 * (b % 2) + c, c, c == C - 1
                else:
                    i, chunk, last = 4 * c + (b - NPROJ) % 4, 4 * ((b - NPROJ) // NOUT) + c, c == 3
                mm = token_halves(banks, weight(wh, U % 2, i), weight(wl, U % 2, i), xh[:, chunk, :],
                                  xl[:, chunk, :], c == 0, last)
                if last:
                    mm.then_inc(proj_job, 1)

            def proj(b):
                for c in range(C if b < NPROJ else 4):
                    proj_part(b, c)

            def logits(n):
                t, m = ITEMS[n]
                job = ("logit", n)
                if t:
                    pe.wait_ge(mask_ready, ATT_TILES.index(t) + 1)
                else:
                    pe.wait_ge(mask0_ready, 1)
                wait_bank_free(pe, job)
                out = ps[:, bank(job), 0:width[t]]
                if t == 4:
                    pe.matmul(out, bft[:, m, :], masks[t], start=True, stop=False)
                    for r in (0, HD):
                        q = q_all[r:r + HD, 4 * SEQ + m * HD:4 * SEQ + (m + 1) * HD]
                        pe.matmul(ps[r:r + HD, bank(job), 0:PAST], q, kct[r:r + HD, m, :],
                                  start=False, stop=False)
                        mm = pe.matmul(ps[r:r + HD, bank(job), PAST:SD], q, kt[r:r + HD, SEQ:TOK],
                                       start=False, stop=True)
                else:
                    g, r = m // 2, HD * (m % 2)
                    pe.matmul(out, ident_bf, masks[t], start=True, stop=False)
                    mm = pe.matmul(out, qt[r:r + HD, g, t * P:(t + 1) * P], kt[r:r + HD, 0:width[t]],
                                   start=False, stop=True)
                mm.then_inc(bank_full[bank(job)], 1)

            def turn_weights(n):
                pe.wait_ge(p_ready, n + 1)
                turn_token_tile(("turn", n), [rp[:, n % 2, k * P:(k + 1) * P]
                                              for k in range(width[ITEMS[n][0]] // P)])

            def weigh_values(n):
                t, m = ITEMS[n]
                if m == 0:
                    wait_bank_free(pe, ("pv", t))
                wait_bank_read(pe, ("turn", n))
                blocks = width[t] // P
                if t == 4:
                    for r in (0, HD):
                        for k in range(blocks):
                            v = vc[:, m, k, r:r + HD] if k < 2 else zkv[:, 4, P + r:P + r + HD]
                            mm = pe.matmul(ps[r:r + HD, 7, m * HD:(m + 1) * HD], v,
                                           wt[:, n % 2, k * P + r:k * P + r + HD],
                                           start=(k == 0), stop=(k == blocks - 1))
                else:
                    g, r = m // 2, HD * (m % 2)
                    for k in range(blocks):
                        mm = pe.matmul(ps[r:r + HD, 7, g * P:(g + 1) * P], zkv[:, k, P + r:P + r + HD],
                                       wt[:, n % 2, k * P:(k + 1) * P],
                                       start=(k == 0), stop=(k == blocks - 1))
                mm.then_inc(pv_done, 1)

            pe.wait_ge(ones_set, 3)
            for _ in range(WARM_UP):
                pe.matmul(ps[:, 7, 0:P], ones[:, :], ones[:, :], start=True, stop=True)
            ffn(0)

            pe.wait_ge(lo_ready, U_TOK + 1)
            pe.wait_ge(xh_ready, C + 4)
            pe.wait_ge(xl_ready, C + 4)
            for t in range(TT):
                pe.wait_ge(res_added, 4 + TOK_BANKS[t] // 2 + 1)
                tok_half(0, 0, t)
            pe.wait_ge(xh_ready, 2 * C)
            pe.wait_ge(xl_ready, 2 * C)
            pe.wait_ge(lo_ready, U_TOK + 2)
            pe.wait_ge(res_added, C)
            for t in range(TT):
                tok_half(0, 1, t)
                if t == 0:
                    column_sums(1)
            tok_unit(1, 0)
            broadcast_rstd(1)
            tok_unit(1, 1)
            pe.wait_ge(rbc_ready, 2)
            tok_unit(2, 0, (0, 1))
            pe.wait_ge(tok_evac, 6)
            pe.wait_ge(consts_in, 16 * 4)
            pe.wait_ge(ki_ready, 1)
            turn_token_tile("tki0", [zki[:, t, :] for t in range(4)])
            turn_token_tile("tki1", [zki[:, 4, :]])
            pe.wait_ge(wfold_ready, 1)
            wait_bank_free(pe, "wcol")
            pe.matmul(ps[:, 6, 0:NB], wfold[:, :], same_b, start=True, stop=True).then_inc(bank_full[6], 1)
            tok_unit(2, 0, (2,))
            pe.wait_ge(qi_ready, 1)
            for t in range(TT):
                turn_token_tile(f"tqi{t}", [zq[:, t, j * P:(j + 1) * P] for j in range(4)])
                if t % 2:
                    tok_unit(2, 0, (3 + t // 2,))
            tok_unit(2, 1, (0,))
            for job in ("tki0", "tki1", "tqi3", "tqi4"):
                wait_bank_read(pe, job)
            for t in DOT_TILES:
                for h in range(8):
                    dots(t, h)
            tok_unit(2, 1, range(1, TT))
            proj(0)
            pe.wait_ge(ikc_in, 32)
            dots_sample(0)
            dots_sample(1)
            for b in range(NB):
                if b + 2 < NB:
                    dots_sample(b + 2)
                proj_part(1, b)
                sum_heads(b)
            for h in range(8):
                dots(1, h)
            proj(2)
            proj(3)
            pe.wait_ge(k_ready, 1)
            turn_token_tile("tk0", [zkv[:, t, 0:P] for t in range(4)])
            turn_token_tile("tk1", [zkv[:, 4, 0:P]])
            proj(4)
            pe.wait_ge(q_ready, 1)
            for t in range(TT):
                turn_token_tile(f"tq{t}", [zq[:, t, j * P:(j + 1) * P] for j in range(4)])
            proj(5)
            for job in ("tk0", "tk1", "tq3", "tq4"):
                wait_bank_read(pe, job)
            pe.wait_ge(kc_in, 16)
            pe.wait_ge(vc_in, 16)
            proj(6)
            logits(0)
            logits(1)
            proj(7)

            def filler(i):
                if i == 32:
                    pe.wait_ge(cvl_ready, 4)
                if i < 32:
                    proj_part(8 + i // 8, i % 8)
                else:
                    proj_part(12 + (i - 32) // 4, i % 4)

            for n in range(len(ITEMS)):
                turn_weights(n)
                if n + 2 < len(ITEMS):
                    logits(n + 2)
                for i in range(parts_by(n - 1), parts_by(n)):
                    filler(i)
                weigh_values(n)
            for i in range(parts_by(len(ITEMS) - 1), 64):
                filler(i)
            wait_bank_read(pe, ("pv", ATT_TILES[-1]))
            for b in range(NPROJ + NOUT, NPROJ + 2 * NOUT):
                proj(b)
            ffn(1)

        @block.scalar
        def _(act):
            def copy(out, in_, scale=1.0):
                return nc.scalar.activation(out, in_, ACT.Copy, scale=scale)

            def split_hi(U, k, slot, n):
                act.wait_ge(raw_in[slot], 16 * (k + slot))
                copy(wh[:, slot, 0:n], raw[:, slot, 0:n]).then_inc(hi_ready, 1)

            def operand_hi(stage, c):
                copy(xh[:, c, :], x[:, c, :], scale=gain(stage, c)).then_inc(xh_ready, 1)

            def square(stage, c):
                if stage and c == 0:
                    act.wait_ge(bcast_done, stage)
                if c > 2:
                    act.wait_ge(sq_added, (C - 1) * stage + c - 2)
                dst = sqacc if c == 0 else (sq, sq_odd)[c % 2]
                nc.scalar.activation(dst[:, :], x[:, c, :], ACT.Square).then_inc(sq_ready, 1)

            def rstd_out(stage):
                act.wait_ge(bcast_done, stage + 1)
                copy(rbc[:, :], ps[:, 6:8, :].rearrange("p a b -> p (a b)")[:, 0:TOK]).then_inc(rbc_ready, 1)

            def mixer_hi(U):
                wait_unit_used(act, U - 2)
                split_hi(U, U // 2, U % 2, unit_n(U))

            def quarter_hi_of(U, q):
                if q == 0:
                    wait_unit_used(act, U - 2)
                    act.wait_ge(raw_in[U % 2], 16 * (U // 2 + U % 2))
                copy(quarter(wh, U, q), quarter(raw, U, q)).then_inc(quarter_hi if q < 3 else hi_ready, 1)

            def ffn(k):
                base = U_FFN2 * k
                if k == 0:
                    act.wait_ge(small_in, 16)
                for c in range(C):
                    if k == 0:
                        act.wait_ge(x_in[x_part(c)], 16)
                    else:
                        act.wait_ge(proj_evac, NPROJ + NOUT + c + 1)
                        if c >= 4:
                            act.wait_ge(proj_job, NPROJ + 2 * NOUT)
                    operand_hi(2 * k, c)
                    if k:
                        square(2 * k, c)
                    elif c in (3, 5):
                        square(0, (c - 3) // 2)
                    if k == 0 and c in (0, 1, 4, 5):
                        i = (0, 1, None, None, 2, 3)[c]
                        act.wait_ge(part_in[i], 16)
                        copy(first_part(wh, i), first_part(raw, i)).then_inc(part_hi if i < 3 else hi_ready, 1)
                if k:
                    mixer_hi(base + 1)
                else:
                    for c in range(2, 4):
                        square(0, c)
                    split_hi(1, 0, 1, 2048)
                    for c in range(4, C):
                        square(0, c)
                rstd_out(2 * k)

                def glu_step(u, half, s, n):
                    act.wait_ge(unit_done, UF * k + u + 1)
                    split_hi(None, base // 2 + half + 1, s, n)
                    act.wait_ge(glu_g_ready, GU * k + u + 1)
                    nc.scalar.activation(glu_t[:, :], glu_g[:, :], ACT.Tanh, scale=0.5).then_inc(tanh_ready, 1)

                def hidden_hi(pair, tile_pair, s):
                    copy(hh[:, s, :], hid[:, bass.ds(tile_pair * 2 * TOK, 2 * TOK)]).then_inc(hh_ready, 1)

                with act.Fori(0, GU // 2 - 1) as i:
                    for s in range(2):
                        glu_step(2 * i + s, i, s, 2048)
                act.wait_ge(hid_ready, GU * k + 2)
                for s in range(2):
                    glu_step(GU - 2 + s, GU // 2 - 1, s, 1024)
                    act.wait_ge(hid_ready, GU * k + 2 * s + 2)
                    hidden_hi(s, s, s)

                def down_step(v, half, s, tile_pair):
                    act.wait_ge(unit_done, UF * k + GU + v + 1)
                    split_hi(None, (base + GU) // 2 + half + 1, s, 1024)
                    hidden_hi(None, tile_pair, s)

                with act.Fori(0, 4) as i:
                    for s in range(2):
                        down_step(2 * i + s, i, s, 2 * i + s + 2)
                act.wait_ge(hid_ready, GU * (k + 1))
                down_step(8, 4, 0, 10)
                down_step(9, 4, 1, 0)
                down_step(10, 5, 0, 1)
                if k == 0:
                    for c in range(4):
                        act.wait_ge(res_added, c + 1)
                        operand_hi(1, c)
                    for c in range(4):
                        square(1, c)
                down_step(11, 5, 1, 2)
                with act.Fori(0, 4) as i:
                    for s in range(2):
                        down_step(2 * i + 12 + s, i + 6, s, 2 * i + s + 3)
                if k == 0:
                    mixer_hi(U_TOK)
                    mixer_hi(U_TOK + 1)

            def tok_out(g, t):
                act.wait_ge(tok_job, TT * (2 * g + 1) + t + 1)
                s, p = rstd[:, t:t + 1], ps[:, TOK_BANKS[TT * g + t], :]
                pieces = [[(0, 64, zki[:, t, 0:HD]), (64, 72, zwi[:, t, :]), (72, 420, zq[:, t, 0:348])],
                          [(0, 164, zq[:, t, 348:512]), (164, 420, zkv[:, t, :])],
                          [(0, 512, zq[:, t, :])]][g]
                for a, b, dst in pieces:
                    ins = copy(dst, p[:, a:b], scale=s)
                ins.then_inc(tok_evac, 1)

            def turned_out(job, dst, n):
                wait_bank_full(act, job)
                src = ps[:, bank(job), 0:n * P]
                if len(dst.shape) == 3:
                    src = src.rearrange("p (j t) -> p j t", j=n)
                elif len(dst.shape) == 4:
                    src = src.rearrange("p (j b t) -> p j b t", j=n, b=NB)
                copy(dst, src).then_inc(bank_free[bank(job)], 1)

            def relu_out(t, h, n):
                job = ("dot", t, h)
                wait_bank_full(act, job)
                if n >= 2:
                    act.wait_ge(relu_used, n - 1)
                nc.scalar.activation(rp[:, n % 2, 0:width[t]], ps[:, bank(job), 0:width[t]], ACT.Relu)\
                    .then_inc(bank_free[bank(job)], 1)

            def exp_out(n):
                t, m = ITEMS[n]
                act.wait_ge(max_ready, n + 1)
                if n >= 2:
                    wait_bank_full(act, ("turn", n - 2))
                job = ("logit", n)
                nc.scalar.activation(rp[:, n % 2, 0:width[t]], ps[:, bank(job), 0:width[t]], ACT.Exp,
                                     bias=stat[:, n:n + 1], accum_out=stat[:, 40 + n:41 + n])\
                    .then_inc(bank_free[bank(job)], 1)

            def weights_out(n):
                t, m = ITEMS[n]
                job = ("turn", n)
                wait_bank_full(act, job)
                if n >= 2:
                    act.wait_ge(pv_done, n - 1)
                copy(wt[:, n % 2, 0:width[t]], ps[:, 6, 0:width[t]]).then_inc(bank_free[6], 1)

            def conv_hi(i):
                act.wait_ge(conv_done, i + 1)
                copy(xh[:, i, :], conv_o[:, i, :]).then_inc(cvh_ready, 1)

            def attended_hi(i):
                t = ATT_TILES[i]
                act.wait_ge(pv_done, 8 * (i + 1))
                copy(attended(xh, t), pv_bank(t)).then_inc(att_h_ready, 1)

            load_x(act, 0)
            act.dma_start(sm[:, :], small).then_inc(small_in, 16)
            load_x(act, 1)
            ffn(0)

            for c in range(4, C):
                act.wait_ge(res_added, c + 1)
                operand_hi(1, c)
            for c in range(4, C):
                square(1, c)
            act.wait_ge(res_added, 8)
            for r in (0, HD):
                act.dma_start(ikct[r:r + HD, :, :], ikcache).then_inc(ikc_in, 16)
            mixer_hi(U_TOK + 2)
            act.wait_ge(rstd_ready, 2)
            for t in range(TT):
                tok_out(0, t)
            mixer_hi(U_TOK + 3)
            rstd_out(1)
            mixer_hi(U_TOK + 4)
            for t in range(TT):
                tok_out(1, t)
            mixer_hi(U_TOK + 5)
            turned_out("tki0", kit[:, 0:SEQ], 4)
            turned_out("tki1", kit[:, SEQ:TOK], 1)
            for t in range(TT):
                turned_out(f"tqi{t}", qit[:, :, t * P:(t + 1) * P] if t < 4 else qit_s, 4)
            n = 0
            for t in DOT_TILES:
                for h in range(8):
                    relu_out(t, h, n)
                    n += 1
            mixer_hi(U_CONV)
            for t in range(TT):
                tok_out(2, t)
            mixer_hi(U_CONV + 1)
            mixer_hi(U_CONV + 2)
            for h in range(8):
                relu_out(1, h, n)
                n += 1
            act.wait_ge(relu_used, 24)
            act.dma_start(kct, kcache).then_inc(kc_in, 16)
            act.dma_start(vc, vcache).then_inc(vc_in, 16)
            mixer_hi(U_CONV + 3)
            turned_out("tk0", kt[:, 0:SEQ], 4)
            turned_out("tk1", kt[:, SEQ:TOK], 1)
            for t in range(TT):
                turned_out(f"tq{t}", qt[:, :, t * P:(t + 1) * P] if t < 4 else qt_s, 4)
            mixer_hi(U_CONV + 4)
            exp_out(0)
            exp_out(1)
            for n in range(len(ITEMS)):
                weights_out(n)
                if n in PROJ_SPLITS:
                    mixer_hi(PROJ_SPLITS[n])
                if n in QUARTERS:
                    quarter_hi_of(*QUARTERS[n])
                if n in CONV_SPLITS:
                    act.wait_ge(proj_job, NPROJ)
                    for i in CONV_SPLITS[n]:
                        conv_hi(i)
                if n + 2 < len(ITEMS):
                    exp_out(n + 2)
                if n % 8 == 7:
                    attended_hi(n // 8)
            mixer_hi(U_OUT + 3)
            mixer_hi(U_FFN2)
            act.wait_ge(kv_stored, 64)
            ffn(1)

        @block.vector
        def _(dve):
            chained = [0]

            def link(ins):
                chained[0] += 1
                ins.then_inc(dchain, 1)
                dve.wait_ge(dchain, chained[0])

            def split_lo(n_ready, slot, n):
                dve.wait_ge(hi_ready, n_ready)
                dve.tensor_tensor(wl[:, slot, 0:n], raw[:, slot, 0:n], wh[:, slot, 0:n].bitcast(F32),
                                  ALU.subtract).then_inc(lo_ready, 1)

            def mixer_lo(U):
                split_lo(U + 1, U % 2, unit_n(U))

            def quarter_lo_of(U, q):
                dve.wait_ge(*((quarter_hi, 3 * (U - U_OUT - 1) + q + 1) if q < 3 else (hi_ready, U + 1)))
                ins = dve.tensor_tensor(quarter(wl, U, q), quarter(raw, U, q),
                                        quarter(wh, U, q).bitcast(F32), ALU.subtract)
                ins.then_inc(quarter_lo if q < 3 else lo_ready, 1)

            def operand_lo(stage, c):
                dve.wait_ge(xh_ready, C * stage + c + 1)
                dve.scalar_tensor_tensor(out=xl[:, c, :], in0=x[:, c, :], scalar=gain(stage, c),
                                         in1=xh[:, c, :].bitcast(F32), op0=ALU.mult, op1=ALU.subtract)\
                    .then_inc(xl_ready, 1)

            def mean_squares(stage):
                dve.wait_ge(colsum_done, stage + 1)
                dve.tensor_scalar(var[:, :], ps[:, 7, 0:TT], 1.0 / D, EPS, ALU.mult, ALU.add)\
                    .then_inc(var_ready, 1)

            def diagonals(stage):
                dve.wait_ge(rstd_ready, stage + 1)
                if stage == 0:
                    dve.wait_ge(consts_in, 16 * 4)
                dve.tensor_tensor(sq[:, :].rearrange("p (t m) -> p t m", t=TT),
                                  ident.unsqueeze(1).broadcast_to([P, TT, P]),
                                  rstd[:, :].unsqueeze(2).broadcast_to([P, TT, P]), ALU.mult)\
                    .then_inc(diag_ready, 1)

            def both(b):
                return ps[:, b:b + 2, 0:HALF]

            def halves(ap):
                return ap.rearrange("p (a b) -> p a b", a=2)

            def add_residual(c, b, scale):
                dve.scalar_tensor_tensor(out=halves(x[:, c, :]), in0=both(b), scalar=scale,
                                         in1=halves(x[:, c, :]), op0=ALU.mult, op1=ALU.add)\
                    .then_inc(res_added, 1)

            def ffn(k):
                base = U_FFN2 * k
                if k == 0:
                    for c in range(C):
                        operand_lo(0, c)
                        if c in (0, 1, 4, 5):
                            i = (0, 1, None, None, 2, 3)[c]
                            dve.wait_ge(*((part_hi, i + 1) if i < 3 else (hi_ready, 1)))
                            dve.tensor_tensor(first_part(wl, i), first_part(raw, i),
                                              first_part(wh, i).bitcast(F32), ALU.subtract)\
                                .then_inc(part_lo if i < 3 else lo_ready, 1)
                    split_lo(2, 1, 2048)
                else:
                    for c in range(4, C):
                        operand_lo(2, c)
                    mixer_lo(base + 1)
                mean_squares(2 * k)
                diagonals(2 * k)
                dve.wait_ge(rbc_ready, 2 * k + 1)

                def glu_step(u, s, n, first=False):
                    e = GU * k + u
                    if not first:
                        dve.wait_ge(hid_ready, e)
                    dve.wait_ge(unit_done, UF * k + u + 1)
                    dve.tensor_tensor(halves(glu_g[:, :]), both(4 * s), halves(rbc[:, :]), ALU.mult)\
                        .then_inc(glu_g_ready, 1)
                    dve.tensor_tensor(halves(glu_u[:, :]), both(4 * s + 2), halves(rbc[:, :]), ALU.mult)\
                        .then_inc(glu_free, 1)
                    split_lo(base + u + 3, s, n)
                    dve.wait_ge(tanh_ready, e + 1)
                    dve.scalar_tensor_tensor(out=glu_g[:, :], in0=glu_t[:, :], scalar=1.0, in1=glu_g[:, :],
                                             op0=ALU.add, op1=ALU.mult).then_inc(glu_m_ready, 1)
                    dve.wait_ge(glu_free, e + 1)
                    dve.wait_ge(glu_m_ready, e + 1)
                    dve.tensor_tensor(hid[:, bass.ds(u * TOK, TOK)], glu_g[:, :], glu_u[:, :], ALU.mult)\
                        .then_inc(hid_ready, 1)

                def hidden_lo(pair, tile_pair, s):
                    dve.wait_ge(hh_ready, DN * k + pair + 1)
                    dve.tensor_tensor(hl[:, s, :], hid[:, bass.ds(tile_pair * 2 * TOK, 2 * TOK)],
                                      hh[:, s, :].bitcast(F32), ALU.subtract).then_inc(hl_ready, 1)

                glu_step(0, 0, 2048, first=(k == 0))
                glu_step(1, 1, 2048)
                with dve.Fori(1, GU // 2 - 1) as i:
                    for s in range(2):
                        glu_step(2 * i + s, s, 2048)
                for s in range(2):
                    glu_step(GU - 2 + s, s, 1024)
                    hidden_lo(s, s, s)

                def down_step(v, s, tile_pair):
                    split_lo(base + GU + v + 3, s, 1024)
                    hidden_lo(v + 2, tile_pair, s)

                def add_half(half):
                    for j in range(4):
                        if j < 3:
                            dve.wait_ge(down_done, 3 * (2 * k + half) + j + 1)
                        else:
                            dve.wait_ge(unit_done, UF * k + GU + DN // 2 * (half + 1))
                        add_residual(4 * half + j, 2 * j, 0.25)

                with dve.Fori(0, 4) as i:
                    for s in range(2):
                        down_step(2 * i + s, s, 2 * i + s + 2)
                down_step(8, 0, 10)
                down_step(9, 1, 0)
                add_half(0)
                down_step(10, 0, 1)
                if k == 0:
                    for c in range(4):
                        operand_lo(1, c)
                down_step(11, 1, 2)
                with dve.Fori(0, 4) as i:
                    for s in range(2):
                        down_step(2 * i + 12 + s, s, 2 * i + s + 3)
                if k == 0:
                    mixer_lo(U_TOK)
                add_half(1)
                if k == 0:
                    mixer_lo(U_TOK + 1)

            def rotate(z, n, ready):
                x1, x2 = z[:, :, :, 0:ROT], z[:, :, :, ROT:2 * ROT]
                cos = cos_t.unsqueeze(2).broadcast_to([P, TT, n, ROT])
                sin = sin_t.unsqueeze(2).broadcast_to([P, TT, n, ROT])
                a, b, c, d = [r[:, 0:TT * n * ROT].rearrange("p (t n r) -> p t n r", t=TT, n=n) for r in rot]
                dve.tensor_tensor(a, x1, cos, ALU.mult)
                dve.tensor_tensor(b, x2, sin, ALU.mult)
                dve.tensor_tensor(c, x1, sin, ALU.mult)
                link(dve.tensor_tensor(d, x2, cos, ALU.mult))
                dve.tensor_tensor(x1, a, b, ALU.subtract)
                ins = dve.tensor_tensor(x2, c, d, ALU.add)
                if ready is None:
                    link(ins)
                else:
                    ins.then_inc(ready, 1)

            def squares_of(z, n, at, t0, tn):
                s = sq[:, 0:tn * n * HD].rearrange("p (t n d) -> p t n d", t=tn, n=n)
                link(dve.tensor_tensor(s, z[:, t0:t0 + tn], z[:, t0:t0 + tn], ALU.mult))
                ss = head_ss[:, at + t0 * n:at + (t0 + tn) * n]
                link(dve.tensor_reduce(ss.rearrange("p (t n) -> p t n", t=tn), s, AX.X, ALU.add))

            def mean_of_squares(n, at, ss_ready):
                ss = head_ss[:, at:at + TT * n]
                dve.tensor_scalar(ss, ss, 1.0 / HD, EPS, ALU.mult, ALU.add).then_inc(ss_ready, 1)

            def head_scale(z, n, at, g, rs_count):
                dve.wait_ge(head_rs_ready, rs_count)
                rs = head_rs[:, at:at + TT * n].rearrange("p (t n) -> p t n", t=TT).unsqueeze(3)
                link(dve.tensor_tensor(z, z, rs.broadcast_to([P, TT, n, HD]), ALU.mult))
                link(dve.tensor_tensor(z, z, g.unsqueeze(1).unsqueeze(1).broadcast_to([P, TT, n, HD]), ALU.mult))

            relus = [0]

            def add_head(t, h):
                n = relus[0]
                relus[0] += 1
                wait_bank_read(dve, ("dot", t, h))
                r, w, s = rp[:, n % 2, 0:width[t]], zwi[:, t, h:h + 1], scores[t]
                if h == 0:
                    ins = dve.tensor_scalar(s, r, w, None, ALU.mult)
                else:
                    dve.wait_ge(relu_used, n)
                    ins = dve.scalar_tensor_tensor(out=s, in0=r, scalar=w, in1=s, op0=ALU.mult, op1=ALU.add)
                ins.then_inc(relu_used, 1)

            def close_scores(t):
                link(dve.memset(scores[t][0:64, width[t] - 64:width[t]], NEVER))

            rounds_done = {t: 0 for t in scores}

            def top_rounds(t, n):
                rounds_done[t] += n
                for _ in range(n):
                    link(dve.max(top8[:, :], scores[t]))
                    link(dve.match_replace(scores[t], top8[:, :], scores[t], TAKEN))

            def mask_of(t):
                assert 8 * rounds_done[t] == (KD + PAD if t == 4 else KP)
                dve.tensor_scalar(masks[t], scores[t][:, 0:width[t]], TAKEN, OFF, ALU.is_gt, ALU.mult)\
                    .then_inc(mask_ready, 1)

            def proj_out(b):
                dve.wait_ge(proj_job, b + 1)
                src = both(2 * (b % 2))
                if b >= NPROJ:
                    c = (b - NPROJ) % NOUT
                    dve.scalar_tensor_tensor(out=halves(x[:, c, :]), in0=src, scalar=1.0,
                                             in1=halves(x[:, c, :]), op0=ALU.mult, op1=ALU.add)\
                        .then_inc(proj_evac, 1)
                    return
                i, part = b // 3, b % 3
                if part == 0:
                    dve.tensor_tensor(halves(conv_g[:, :]), src, halves(rbc[:, :]), ALU.mult)\
                        .then_inc(proj_evac, 1)
                elif part == 1:
                    if i:
                        dve.wait_ge(conv_done, i)
                    dve.wait_ge(proj_evac, b)
                    dve.tensor_tensor(halves(conv_v[:, :]), src, halves(conv_g[:, :]), ALU.mult)\
                        .then_inc(proj_evac, 1)
                else:
                    dve.tensor_tensor(halves(conv_b[:, :]), src, halves(rbc[:, :]), ALU.mult)\
                        .then_inc(proj_evac, 1)

            def conv_lo(i):
                dve.wait_ge(cvh_ready, i + 1)
                dve.tensor_tensor(xl[:, i, :], conv_o[:, i, :], xh[:, i, :].bitcast(F32), ALU.subtract)\
                    .then_inc(cvl_ready, 1)

            def neg_max(n):
                t, m = ITEMS[n]
                job = ("logit", n)
                wait_bank_full(dve, job)
                dve.tensor_reduce(stat[:, n:n + 1], ps[:, bank(job), 0:width[t]], AX.X, ALU.max, negate=True)\
                    .then_inc(max_ready, 1)

            def normalise(n):
                t, m = ITEMS[n]
                job = ("logit", n)
                wait_bank_read(dve, job)
                link(dve.reciprocal(stat[:, 80 + n:81 + n], stat[:, 40 + n:41 + n]))
                dve.tensor_scalar(rp[:, n % 2, 0:width[t]], rp[:, n % 2, 0:width[t]], stat[:, 80 + n:81 + n],
                                  None, ALU.mult).then_inc(p_ready, 1)

            ffn(0)

            for c in range(4, C):
                operand_lo(1, c)
            mean_squares(1)
            diagonals(1)
            mixer_lo(U_TOK + 2)
            mixer_lo(U_TOK + 3)
            link(dve.tensor_scalar(gn[:, 0, :], gn[:, 0, :], HD ** -0.5, None, ALU.mult))
            dve.wait_ge(tok_evac, 5)
            dve.wait_ge(bcast_done, 2)
            link(dve.tensor_scalar(zwi[:, :, :], zwi[:, :, :], 8 ** -0.5 * HD ** -0.5, None, ALU.mult))
            dve.tensor_tensor(wfold[:, :].rearrange("p (r j t) -> p r j t", r=2, j=4),
                              zwi[:, 4, :].rearrange("p (j r) -> p r j", r=2).unsqueeze(3)
                              .broadcast_to([P, 2, 4, NT]),
                              same_t.unsqueeze(1).unsqueeze(1).broadcast_to([P, 2, 4, NT]), ALU.mult)\
                .then_inc(wfold_ready, 1)
            ki4 = zki[:, :, 0:HD].unsqueeze(2)
            squares_of(ki4, 1, 0, 0, TT)
            mean_of_squares(1, 0, ki_ss_ready)
            head_scale(ki4, 1, 0, gn[:, 2, :], 1)
            rotate(ki4, 1, None)
            dve.tensor_copy(zki[:, :, HD:P], zki[:, :, 0:HD]).then_inc(ki_ready, 1)
            mixer_lo(U_TOK + 4)
            dve.wait_ge(tok_evac, 2 * TT)
            heads8 = zq[:, :, :].rearrange("p t (n d) -> p t n d", n=8)
            rotate(heads8, 8, qi_ready)
            mixer_lo(U_TOK + 5)
            wait_bank_full(dve, "wcol")
            dve.tensor_copy(wcols[:, :], ps[:, 6, 0:NB]).then_inc(bank_free[6], 1)
            for h in range(8):
                add_head(3, h)
            for h in range(8):
                add_head(2, h)
            dve.wait_ge(relu_used, 16)
            close_scores(3)
            close_scores(2)
            top_rounds(3, 4)
            mixer_lo(U_CONV)
            top_rounds(3, 5)
            dve.wait_ge(tok_evac, NJ)
            k4 = zkv[:, :, 0:P].rearrange("p t (n d) -> p t n d", n=2)
            squares_of(k4, 2, TT, 0, TT)
            mean_of_squares(2, TT, k_ss_ready)

            def weigh_sample(b):
                job = ("dot", 4, b)
                wait_bank_full(dve, job)
                if b == 0:
                    wait_bank_read(dve, "wcol")
                else:
                    if b >= 2:
                        dve.wait_ge(dec_relu_used, b - 1)
                dve.tensor_scalar(rp[:, b % 2, 0:SD], ps[:, bank(job), 0:SD], 0.0, wcols[:, b:b + 1],
                                  ALU.max, ALU.mult).then_inc(bank_free[bank(job)], 1)

            for b in range(NB):
                weigh_sample(b)
                if b == 0:
                    proj_out(0)
                elif b <= TT:
                    squares_of(heads8, 8, 3 * TT, b - 1, 1)
                elif b == TT + 1:
                    mean_of_squares(8, 3 * TT, q_ss_ready)
                    mixer_lo(U_CONV + 1)
            wait_bank_full(dve, "decsum")
            dve.wait_ge(score_fill, 1)
            dve.tensor_copy(scores[4][:, 0:PAST], ps[:, 7, 0:PAST])
            dve.tensor_tensor(scores[4][:, PAST:SD], ps[:, 7, PAST:SD], other_b, ALU.add)\
                .then_inc(bank_free[7], 1)
            for h in range(8):
                add_head(1, h)
            dve.wait_ge(relu_used, 24)
            close_scores(1)
            proj_out(1)
            mixer_lo(U_CONV + 2)
            head_scale(k4, 2, TT, gn[:, 1, :], 2)
            rotate(k4, 2, k_ready)
            dve.wait_ge(k_ready, 1)
            proj_out(2)
            head_scale(heads8, 8, 3 * TT, gn[:, 0, :], 3)
            proj_out(3)
            rotate(heads8, 8, q_ready)
            mixer_lo(U_CONV + 3)
            top_rounds(3, 3)
            proj_out(4)
            top_rounds(3, 4)
            mask_of(3)
            proj_out(5)
            mixer_lo(U_CONV + 4)
            top_rounds(2, 3)
            proj_out(6)
            neg_max(0)
            neg_max(1)
            top_rounds(2, 2)
            normalise(0)
            top_rounds(2, 3)
            proj_out(7)
            for n in range(len(ITEMS)):
                if n + 1 < len(ITEMS):
                    normalise(n + 1)
                if n + 2 < len(ITEMS):
                    neg_max(n + 2)
                for t, rounds in ROUNDS.items():
                    top_rounds(t, rounds.get(n, 0))
                    if n == max(rounds):
                        mask_of(t)
                for b in range(jobs_by(n - 1), jobs_by(n)):
                    proj_out(b)
                if n in PROJ_SPLITS:
                    mixer_lo(PROJ_SPLITS[n])
                if n in QUARTERS:
                    quarter_lo_of(*QUARTERS[n])
                if n in CONV_SPLITS:
                    for i in CONV_SPLITS[n]:
                        conv_lo(i)
                if n % 8 == 7:
                    t = ATT_TILES[n // 8]
                    dve.wait_ge(att_h_ready, n // 8 + 1)
                    dve.tensor_tensor(attended(xl, t), pv_bank(t), attended(xh, t).bitcast(F32),
                                      ALU.subtract).then_inc(bank_free[7], 1)
            for b in range(jobs_by(len(ITEMS) - 1), NPROJ + 2 * NOUT):
                proj_out(b)
                if b == NPROJ + NOUT:
                    mixer_lo(U_OUT + 3)
                if b == NPROJ + NOUT + 3:
                    mixer_lo(U_FFN2)
                if b >= NPROJ + NOUT + 4:
                    operand_lo(2, b - (NPROJ + NOUT + 4))
            ffn(1)

        @block.gpsimd
        def _(pool):
            chained = [0]

            def link(ins):
                chained[0] += 1
                ins.then_inc(pchain, 1)
                pool.wait_ge(pchain, chained[0])

            def root(out, in_):
                return pool.tensor_tensor(out, in_, half_pow[:, 0:in_.shape[1]], ALU.pow)

            def add_squares(stage, c):
                pool.wait_ge(sq_ready, C * stage + c + 1)
                if (C - 1) * stage + c - 1:
                    pool.wait_ge(sq_added, (C - 1) * stage + c - 1)
                pool.tensor_tensor(sqacc[:, :], sqacc[:, :], (sq, sq_odd)[c % 2][:, :], ALU.add)\
                    .then_inc(sq_added, 1)

            def norm_factors(stage):
                for c in range(1, C):
                    add_squares(stage, c)
                pool.wait_ge(var_ready, stage + 1)
                root(rstd[:, :], var[:, :]).then_inc(rstd_ready, 1)

            pool.memset(ones[:, :], 1.0).then_inc(ones_set, 1)
            pool.memset(half_pow[:, :], -0.5).then_inc(ones_set, 1)
            pool.memset(cstate[:, :, :, :], 0.0).then_inc(ones_set, 1)
            pool.wait_ge(ones_set, 3)
            norm_factors(0)
            norm_factors(1)
            pool.wait_ge(res_added, C)
            pool.memset(scores[4][:, SD:SD + PAD], -NEVER).then_inc(score_fill, 1)
            link(pool.memset(conv_u[:, 0:2], 0.0))
            link(pool.memset(masks[0], 0.0))
            pool.memset(masks[0][0:64, 64:128], OFF).then_inc(mask0_ready, 1)
            for at, n, ready in ((0, TT, ki_ss_ready), (TT, 2 * TT, k_ss_ready), (3 * TT, 8 * TT, q_ss_ready)):
                pool.wait_ge(ready, 1)
                root(head_rs[:, at:at + n], head_ss[:, at:at + n]).then_inc(head_rs_ready, 1)

            u_samples = conv_u[:, 2 + SEQ:].rearrange("p (b t) -> p b t", b=NB)
            samples = lambda ap: ap.rearrange("p (b t) -> p b t", b=NB)

            def conv(i):
                link(pool.tensor_copy(u_samples[:, :, 0:2], cpast[:, i, :, :]))
                pool.wait_ge(proj_evac, 3 * i + 2)
                pool.tensor_tensor(conv_u[:, 2:2 + SEQ], conv_v[:, 0:SEQ], rbc[:, 0:SEQ], ALU.mult)
                link(pool.tensor_tensor(u_samples[:, :, 2:], samples(conv_v[:, SEQ:TOK]),
                                        samples(rbc[:, SEQ:TOK]), ALU.mult))
                pool.tensor_copy(cstate[:, i, 0, :], conv_u[:, SEQ:SEQ + 2])
                pool.tensor_copy(cstate[:, i, 1:, :], u_samples[:, :, NT:])
                for j in range(3):
                    dst = conv_o[:, i, :] if j == 0 else conv_v[:, :]
                    pool.tensor_scalar(dst[:, 0:SEQ], conv_u[:, j:j + SEQ], conv_w(i, j), 1.0, ALU.mult,
                                       ALU.mult)
                    link(pool.tensor_scalar(samples(dst[:, SEQ:TOK]), u_samples[:, :, j:j + NT],
                                            conv_w(i, j), 1.0, ALU.mult, ALU.mult))
                    if j:
                        link(pool.tensor_tensor(conv_o[:, i, :], conv_o[:, i, :], conv_v[:, :], ALU.add))
                pool.wait_ge(proj_evac, 3 * i + 3)
                pool.tensor_tensor(conv_o[:, i, :], conv_o[:, i, :], conv_b[:, :], ALU.mult)\
                    .then_inc(conv_done, 1)

            for i in range(4):
                conv(i)
            norm_factors(2)


def rotation_tables():
    pos = np.concatenate([np.arange(SEQ), PAST + np.arange(NB * NT) % NT]).astype(np.float32)
    inv = np.float32(500000.0) ** (-np.arange(ROT, dtype=np.float32) * np.float32(2.0 / (2 * ROT)))
    ang = pos[:, None] * inv[None, :].astype(np.float32)
    lay = lambda a: a.astype(np.float32).reshape(TT, P, ROT).transpose(1, 0, 2).reshape(P, TT * ROT)
    return lay(np.cos(ang)), lay(np.sin(ang))


def tables():
    p = np.arange(P)
    cos, sin = rotation_tables()
    same_t = (p[:, None] % NT == np.arange(NT)[None, :]).astype(np.float32)
    spread = np.zeros((P, 240), np.float32)
    spread[:, 112:128] = same_t
    same_b = (p[:, None] // NT == np.arange(NB)[None, :]).astype(np.float32)
    other = np.where(p[:, None] // NT == p[None, :] // NT, 0.0, OFF).astype(np.float32)
    return np.concatenate([np.eye(P, dtype=np.float32), cos, sin, same_t, spread, same_b, other], axis=1)


def bf_tables():
    p = np.arange(P)
    expand = (p[:, None, None] // NT == np.arange(NB)[None, :, None]) & (
        p[:, None, None] % NT == p[None, None, :] % NT)
    return np.concatenate([expand, np.eye(P, dtype=bool)[:, None, :]], axis=1).astype(mybir.dt.np(BF16))


def lay_out(i):
    a = {k: np.asarray(v) for k, v in i.items()}
    x_all = np.concatenate([a["x_prompt"].reshape(SEQ, D), a["x_sample"].reshape(NB * NT, D)])

    def gate_up(g, u):
        both = np.stack([g[0], u[0]]).reshape(2, C, P, NF, P)
        return both.transpose(3, 2, 0, 1, 4).reshape(NF, P, 2 * C * P)

    def down(w):
        return w[0].reshape(NF // 2, 2, P, 2, 4, P).transpose(3, 0, 2, 1, 4, 5).reshape(DN, P, 8 * P)

    w_in = a["w_in"][0]
    gb, gc, xv = (w_in[:, 512 * n:512 * (n + 1)] for n in range(3))
    q = w_in[:, 1536:2048].reshape(D, 2, NG, HD).transpose(0, 2, 1, 3).reshape(D, 512)
    tok = np.concatenate([w_in[:, 2816:2888], w_in[:, 2304:2816], w_in[:, 2048:2304], q], axis=1)
    starts = np.cumsum((0,) + TOK_N)
    filled = lambda w: np.concatenate([w, np.zeros((P, 2048 - w.shape[1]), w.dtype)], axis=1)
    cols = lambda w: w.reshape(-1, P, w.shape[1]).transpose(1, 0, 2).reshape(P, -1)
    tiles = [w[:, P * n:P * (n + 1)] for n in range(4) for w in (gc, xv, gb)]
    w_out = a["w_out"][0]
    att = w_out[512:].reshape(2, NG, HD, D).transpose(1, 0, 2, 3).reshape(512, D)
    w_o = np.stack([w_out[:512], att]).reshape(2, 4, P, 2, 4, P).transpose(0, 3, 2, 1, 4, 5)
    norms = np.concatenate([a[n].reshape(C, P).T for n in ("ffn1_norm", "mix_norm", "ffn2_norm")], axis=1)
    conv_w = a["conv_w"][0].reshape(3, 4, P).transpose(2, 1, 0).reshape(P, 12)
    gains = np.stack([a["q_norm"][0], a["k_norm"][0], a["idx_k_norm"][0]])
    return {
        "xt": x_all.reshape(TOK, C, P).transpose(2, 1, 0),
        "gu1": gate_up(a["ffn1_w_gate"], a["ffn1_w_up"]), "dn1": down(a["ffn1_w_down"]),
        "gu2": gate_up(a["ffn2_w_gate"], a["ffn2_w_up"]), "dn2": down(a["ffn2_w_down"]),
        "wtok": np.stack([filled(cols(tok[h * 512:(h + 1) * 512, s:s + n]))
                          for s, n in zip(starts, TOK_N) for h in range(2)]),
        "wconv": np.stack([np.concatenate([cols(tiles[2 * n]), cols(tiles[2 * n + 1])], axis=1)
                           for n in range(6)]),
        "wout": w_o.reshape(4, P, 16 * P),
        "small": np.concatenate([norms, conv_w], axis=1),
        "gains": np.broadcast_to(gains[None], (P, 3, HD)),
        "kcache": a["cache_k"][0].transpose(2, 3, 0, 1).reshape(P, NB, PAST),
        "vcache": a["cache_v"][0].reshape(NB, 2, P, P).transpose(2, 0, 1, 3),
        "ikcache": a["cache_idx_k"][0].transpose(2, 0, 1),
        "conv_past": a["state_conv"][0].reshape(NB, 2, 4, P).transpose(3, 2, 0, 1),
        "tables": tables(), "bf_tables": bf_tables(),
    }


OUTS = {"y_out": (P, C, TOK), "k_out": (P, TT, P), "v_out": (P, TT, P), "ik_out": (P, TT, HD),
        "conv_out": (P, 4, NB + 1, 2)}


def build(nc, arrays):
    args = {n: nc.dram_tensor(n, v.shape, mybir.dt.from_np(v.dtype), kind="ExternalInput").ap()
            for n, v in arrays.items()}
    args |= {n: nc.dram_tensor(n, s, F32, kind="ExternalOutput").ap() for n, s in OUTS.items()}
    trunk(nc, **args)
    return nc


def kernel(**inputs):
    import concourse.bacc as bacc
    from concourse.bass_utils import run_bass_kernel_spmd

    arrays = {n: np.ascontiguousarray(v) for n, v in lay_out(inputs).items()}
    nc = build(bacc.Bacc("TRN2", target_bir_lowering=False, num_devices=1), arrays)
    r = run_bass_kernel_spmd(nc, [arrays], core_ids=[0]).results[0]
    y = r["y_out"].transpose(2, 1, 0).reshape(TOK, D)
    rows = lambda a: a.transpose(1, 0, 2).reshape(TOK, -1)
    k, v, ik = rows(r["k_out"]), rows(r["v_out"]), rows(r["ik_out"])
    state = r["conv_out"].transpose(2, 3, 1, 0).reshape(NB + 1, 2, 512)
    return (y[:SEQ].reshape(1, SEQ, D), y[SEQ:].reshape(NB, NT, D),
            k[:SEQ].reshape(1, 1, SEQ, 2, HD), v[:SEQ].reshape(1, 1, SEQ, 2, HD),
            ik[:SEQ].reshape(1, 1, SEQ, HD), state[:1].reshape(1, 1, 2, 512),
            k[SEQ:].reshape(1, NB, NT, 2, HD), v[SEQ:].reshape(1, NB, NT, 2, HD),
            ik[SEQ:].reshape(1, NB, NT, HD), state[1:].reshape(1, NB, 2, 512))
```
